# Optimizing a Trainium2 kernel written in Bass

```python
import jax, jax.numpy as jnp
from jax import lax
import numpy as np

D_MODEL = 1024
BATCH = 1
SEQ = 512
DEPTH = 1
DEC_BATCH = 8
DEC_SEQ = 1
PAST_LEN = 4096
PAGE_SIZE = 128

W_CONF = D_MODEL // 2
CONF_K = 31
POOL_WINDOWS = (2, 4, 8, 16)
N_POOL_GROUPS = 4
W_POOL = D_MODEL // 2
POOL_GW = W_POOL // N_POOL_GROUPS
POOL_OUT_GW = D_MODEL // N_POOL_GROUPS
POOL_BUF = 15
W_SC = D_MODEL // 2
SC_K = 3
N_BRANCH = 3
SPLIT_SIZES = (W_CONF, W_CONF, W_POOL, W_SC, W_SC, W_SC, D_MODEL, D_MODEL, D_MODEL)
D_IN = 2 * W_CONF + W_POOL + 3 * W_SC + N_BRANCH * D_MODEL
N_GROUPS = 4
EXP_PER_GROUP = 4
N_EXPERTS = N_GROUPS * EXP_PER_GROUP
TOP_K_INNER = 2
D_FF_EXPERT = D_MODEL // 2
EPS = 1e-6

kernel_name = "hybrid_conv_pool_shortconv_hmoe_step"

def _rmsnorm(x, g):
    xf = x.astype(jnp.float32)
    y = xf * lax.rsqrt(jnp.mean(xf * xf, axis=-1, keepdims=True) + EPS)
    return (y * g.astype(jnp.float32)).astype(x.dtype)

def _layernorm(x, g, b):
    xf = x.astype(jnp.float32)
    mu = jnp.mean(xf, axis=-1, keepdims=True)
    var = jnp.mean(jnp.square(xf - mu), axis=-1, keepdims=True)
    y = (xf - mu) * lax.rsqrt(var + EPS)
    return (y * g.astype(jnp.float32) + b.astype(jnp.float32)).astype(x.dtype)

def _causal_dwconv(u, buf, w):
    k = w.shape[0]
    full = jnp.concatenate([buf.astype(u.dtype), u], axis=1)
    y = lax.conv_general_dilated(full, w.astype(u.dtype)[:, None, :], window_strides=(1,),
                                 padding='VALID', dimension_numbers=('NWC', 'WIO', 'NWC'),
                                 feature_group_count=u.shape[-1])
    return y, full[:, full.shape[1] - (k - 1):]

def _multiscale_pool(u, buf, pos0, pool_w, pool_scale):
    t = u.shape[1]
    full = jnp.concatenate([buf.astype(u.dtype), u], axis=1)
    fullf = full.astype(jnp.float32)
    cs = jnp.concatenate([jnp.zeros_like(fullf[:, :1]), lax.cumsum(fullf, axis=1)], axis=1)
    pos = pos0 + jnp.arange(t)
    off = POOL_BUF + 1
    outs = []
    for gi, w in enumerate(POOL_WINDOWS):
        sl = slice(gi * POOL_GW, (gi + 1) * POOL_GW)
        win_sum = cs[:, off:off + t, sl] - cs[:, off - w:off - w + t, sl]
        count = jnp.minimum(pos + 1, w).astype(jnp.float32)
        pooled = (win_sum / count[None, :, None]).astype(u.dtype) - u[..., sl]
        outs.append(jnp.einsum('btc,co->bto', pooled, pool_w[gi]))
    y = jnp.concatenate(outs, axis=-1) * pool_scale
    return y, full[:, full.shape[1] - POOL_BUF:]

def _mixer(h, buf_a, buf_b, buf_c, pos0, w_in, conf_dw, conf_dw_b, conf_ln_g, conf_ln_b,
           conf_pw, pool_w, pool_scale, sc_dw, sc_out, w_o):
    z = jnp.einsum('btd,de->bte', h, w_in)
    idx = [int(i) for i in np.cumsum(SPLIT_SIZES)[:-1]]
    a_val, a_gate, u_b, s_x, s_b, s_c, z_ga, z_gb, z_gc = jnp.split(z, idx, axis=-1)
    u_a = a_val * jax.nn.sigmoid(a_gate)
    v_a, nb_a = _causal_dwconv(u_a, buf_a, conf_dw)
    v_a = v_a + conf_dw_b
    y_a = jnp.einsum('btc,cd->btd', jax.nn.silu(_layernorm(v_a, conf_ln_g, conf_ln_b)), conf_pw)
    y_b, nb_b = _multiscale_pool(u_b, buf_b, pos0, pool_w, pool_scale)
    v_c, nb_c = _causal_dwconv(s_c * s_x, buf_c, sc_dw)
    y_c = jnp.einsum('btc,cd->btd', s_b * v_c, sc_out)
    m = jax.nn.sigmoid(z_ga) * y_a + jax.nn.sigmoid(z_gb) * y_b + jax.nn.sigmoid(z_gc) * y_c
    return jnp.einsum('btd,de->bte', m, w_o), nb_a, nb_b, nb_c

def _moe(h, rg, rg_b, re, re_b, w1, w3, w2):
    b, t, d = h.shape
    hf = h.reshape(b * t, d)
    gp = jax.nn.softmax((hf @ rg + rg_b).astype(jnp.float32), axis=-1)
    gidx = jnp.argmax(gp, axis=-1)
    gval = jnp.take_along_axis(gp, gidx[:, None], axis=1)[:, 0]
    el = (hf @ re + re_b).astype(jnp.float32).reshape(-1, N_GROUPS, EXP_PER_GROUP)
    sel = jnp.take_along_axis(el, gidx[:, None, None], axis=1)[:, 0]
    tv, ti = lax.top_k(jax.nn.softmax(sel, axis=-1), TOP_K_INNER)
    tv = tv / jnp.sum(tv, axis=-1, keepdims=True)
    w_inner = jnp.sum(jax.nn.one_hot(ti, EXP_PER_GROUP, dtype=jnp.float32) * tv[..., None], axis=1)
    comb = (jax.nn.one_hot(gidx, N_GROUPS, dtype=jnp.float32)[:, :, None]
            * (gval[:, None, None] * w_inner[:, None, :])).reshape(-1, N_EXPERTS).astype(h.dtype)
    y = jnp.zeros_like(hf)
    for e in range(N_EXPERTS):
        act = jax.nn.silu(hf @ w1[e]) * (hf @ w3[e])
        y = y + (act @ w2[e]) * comb[:, e:e + 1]
    return y.reshape(b, t, d)

def _run_group(x, c, st_a, st_b, st_c, pos0, P):
    new_a, new_b, new_c = [], [], []
    sc = jax.nn.silu(c)
    for l in range(DEPTH):
        mod = sc @ P['w_ada'][l] + P['b_ada'][l]
        sh1, s1, g1, sh2, s2, g2 = jnp.split(mod[:, None, :], 6, axis=-1)
        h = _rmsnorm(x, P['norm1_g'][l]) * (1 + s1) + sh1
        m, na, nb, nc = _mixer(h, st_a[l], st_b[l], st_c[l], pos0, P['w_in'][l], P['conf_dw'][l],
                               P['conf_dw_b'][l], P['conf_ln_g'][l], P['conf_ln_b'][l],
                               P['conf_pw'][l], P['pool_w'][l], P['pool_scale'][l],
                               P['sc_dw'][l], P['sc_out'][l], P['w_o'][l])
        x = x + g1 * m
        h = _rmsnorm(x, P['norm2_g'][l]) * (1 + s2) + sh2
        x = x + g2 * _moe(h, P['router_g'][l], P['router_g_b'][l], P['router_e'][l],
                          P['router_e_b'][l], P['exp_w1'][l], P['exp_w3'][l], P['exp_w2'][l])
        new_a.append(na); new_b.append(nb); new_c.append(nc)
    y = _rmsnorm(x, P['final_g'])
    return y, jnp.stack(new_a, 0), jnp.stack(new_b, 0), jnp.stack(new_c, 0)

def setup_inputs(seed: int = 0) -> dict:
    key = jax.random.key(seed)
    ks = jax.random.split(key, 32)
    f = jnp.float32
    nrm = lambda k, s, sc: jax.random.normal(k, s, f) * sc
    D = D_MODEL
    return {
        'x_prompt': nrm(ks[0], (BATCH, SEQ, D), 1.0),
        'x_sample': nrm(ks[1], (DEC_BATCH, DEC_SEQ, D), 1.0),
        'state_conf': nrm(ks[2], (DEPTH, DEC_BATCH, CONF_K - 1, W_CONF), 1.0),
        'state_pool': nrm(ks[3], (DEPTH, DEC_BATCH, POOL_BUF, W_POOL), 1.0),
        'state_sconv': nrm(ks[4], (DEPTH, DEC_BATCH, SC_K - 1, W_SC), 1.0),
        'c_prompt': nrm(ks[5], (BATCH, D), 1.0),
        'c_sample': nrm(ks[6], (DEC_BATCH, D), 1.0),
        'w_ada': nrm(ks[7], (DEPTH, D, 6 * D), 0.5 * D ** -0.5),
        'b_ada': nrm(ks[8], (DEPTH, 6 * D), 0.01),
        'norm1_g': 1.0 + nrm(ks[9], (DEPTH, D), 0.02),
        'norm2_g': 1.0 + nrm(ks[10], (DEPTH, D), 0.02),
        'final_g': 1.0 + nrm(ks[11], (D,), 0.02),
        'w_in': nrm(ks[12], (DEPTH, D, D_IN), D ** -0.5),
        'conf_dw': nrm(ks[13], (DEPTH, CONF_K, W_CONF), CONF_K ** -0.5),
        'conf_dw_b': nrm(ks[14], (DEPTH, W_CONF), 0.01),
        'conf_ln_g': 1.0 + nrm(ks[15], (DEPTH, W_CONF), 0.02),
        'conf_ln_b': nrm(ks[16], (DEPTH, W_CONF), 0.02),
        'conf_pw': nrm(ks[17], (DEPTH, W_CONF, D), W_CONF ** -0.5),
        'pool_w': nrm(ks[18], (DEPTH, N_POOL_GROUPS, POOL_GW, POOL_OUT_GW), POOL_GW ** -0.5),
        'pool_scale': 1.0 + nrm(ks[19], (DEPTH, D), 0.1),
        'sc_dw': nrm(ks[20], (DEPTH, SC_K, W_SC), SC_K ** -0.5),
        'sc_out': nrm(ks[21], (DEPTH, W_SC, D), W_SC ** -0.5),
        'w_o': nrm(ks[22], (DEPTH, D, D), D ** -0.5),
        'router_g': nrm(ks[23], (DEPTH, D, N_GROUPS), D ** -0.5),
        'router_g_b': nrm(ks[24], (DEPTH, N_GROUPS), 0.01),
        'router_e': nrm(ks[25], (DEPTH, D, N_EXPERTS), D ** -0.5),
        'router_e_b': nrm(ks[26], (DEPTH, N_EXPERTS), 0.01),
        'exp_w1': nrm(ks[27], (DEPTH, N_EXPERTS, D, D_FF_EXPERT), D ** -0.5),
        'exp_w3': nrm(ks[28], (DEPTH, N_EXPERTS, D, D_FF_EXPERT), D ** -0.5),
        'exp_w2': nrm(ks[29], (DEPTH, N_EXPERTS, D_FF_EXPERT, D), D_FF_EXPERT ** -0.5),
    }

def reference(x_prompt, x_sample, state_conf, state_pool, state_sconv, c_prompt, c_sample,
              w_ada, b_ada, norm1_g, norm2_g, final_g, w_in, conf_dw, conf_dw_b, conf_ln_g,
              conf_ln_b, conf_pw, pool_w, pool_scale, sc_dw, sc_out, w_o, router_g, router_g_b,
              router_e, router_e_b, exp_w1, exp_w3, exp_w2):
    P = dict(w_ada=w_ada, b_ada=b_ada, norm1_g=norm1_g, norm2_g=norm2_g, final_g=final_g,
             w_in=w_in, conf_dw=conf_dw, conf_dw_b=conf_dw_b, conf_ln_g=conf_ln_g,
             conf_ln_b=conf_ln_b, conf_pw=conf_pw, pool_w=pool_w, pool_scale=pool_scale,
             sc_dw=sc_dw, sc_out=sc_out, w_o=w_o, router_g=router_g, router_g_b=router_g_b,
             router_e=router_e, router_e_b=router_e_b, exp_w1=exp_w1, exp_w3=exp_w3, exp_w2=exp_w2)
    dt = x_prompt.dtype
    z_a = jnp.zeros((DEPTH, BATCH, CONF_K - 1, W_CONF), dt)
    z_b = jnp.zeros((DEPTH, BATCH, POOL_BUF, W_POOL), dt)
    z_c = jnp.zeros((DEPTH, BATCH, SC_K - 1, W_SC), dt)
    y_prompt, conf_p, pool_p, sconv_p = _run_group(x_prompt, c_prompt, z_a, z_b, z_c, 0, P)
    y_sample, conf_s, pool_s, sconv_s = _run_group(x_sample, c_sample, state_conf, state_pool,
                                                    state_sconv, PAST_LEN, P)
    return (y_prompt, y_sample, conf_p, conf_s, pool_p, pool_s, sconv_p, sconv_s)


_drawn_inputs = setup_inputs


def setup_inputs(seed=0):
    import zlib

    import numpy as np

    out = dict(_drawn_inputs(seed))
    spreads = {}
    factors = {'b_ada': 3.357,
     'final_g': 8.084,
     'conf_dw_b': 8.0,
     'conf_ln_g': 31.755,
     'conf_ln_b': 30.673,
     'pool_scale': 3.274,
     'router_g_b': 54.232,
     'router_e_b': 64.0,
     'norm2_g': 8.0}
    for name, (base, spread) in spreads.items():
        noise = np.random.default_rng([zlib.crc32(name.encode()), seed]).standard_normal(out[name].shape)
        drawn = base * np.exp(spread * noise) if base else spread * noise
        out[name] = __import__('jax').numpy.asarray(drawn.astype(out[name].dtype))
    for name, factor in factors.items():
        out[name] = (out[name] * factor).astype(out[name].dtype)
    return out
```

```python
from contextlib import ExitStack

import numpy as np

import concourse.bass as bass
from concourse import mybir

ALU = mybir.AluOpType
ACT = mybir.ActivationFunctionType
AX = mybir.AxisListType
F32 = mybir.dt.float32
BF16 = mybir.dt.bfloat16
I32 = mybir.dt.int32

P = 128
D = 1024
KD = D // P
NP = 512
ND = 8
NT = NP + ND
HT = NT // 2
NTILE = NP // P + 1
W = D // 2
KW = W // P
CK = 31
SK = 3
WINDOWS = (2, 4, 8, 16)
PB = 15
DIN = 6 * W + 3 * D
NG = 4
EG = 4
NE = NG * EG
FF = D // 2
KF = FF // P
EPS = 1e-6
COLS = 512
G_ADA = 6 * D // COLS
G_IN = DIN // COLS
NBUF = 3
MAX_TILES = NE + 2 * NT // P
NR = NG + NE

R_TAPS, R_STAPS, R_CB, R_LG, R_LB, R_N1, R_PS = 0, 31, 34, 35, 36, 37, 39
N_PARAM = 41


def trunk_step(nc, x_prompt, x_sample, state_conf, state_pool, state_sconv, c_prompt, c_sample, w_ada,
               b_ada, norm1_g, norm2_g, final_g, w_in, conf_dw, conf_dw_b, conf_ln_g, conf_ln_b, conf_pw,
               pool_w, pool_scale, sc_dw, sc_out, w_o, router_g, router_g_b, router_e, router_e_b, exp_w1,
               exp_w3, exp_w2, y_prompt, y_sample, conf_p, conf_s, pool_p, pool_s, sconv_p, sconv_s):
    h2_dram = nc.dram_tensor("h2_rows", [NT, D], F32, kind="Internal").ap()
    slot_dram = nc.dram_tensor("slot_tokens", [(MAX_TILES + 1) * P, 1], I32, kind="Internal").ap()
    y_dram = nc.dram_tensor("expert_rows", [MAX_TILES * P, D], F32, kind="Internal").ap()

    ctx = ExitStack()
    with ctx:
        def sb(name, shape, dt=F32):
            return ctx.enter_context(nc.sbuf_tensor(name, shape, dt))

        def sem(name):
            return ctx.enter_context(nc.semaphore(name))

        wbuf = sb("wbuf", [P, NBUF, 4096])
        mod = sb("mod", [ND + 1, 6 * D])
        hT = sb("hT", [P, KD, NT])
        region_a = sb("region_a", [P, 3 * KD * NT])
        region_b = sb("region_b", [P, 12980])
        params = sb("params", [N_PARAM, W])
        pT = sb("pT", [P, KW, N_PARAM])
        confT = sb("confT", [P, KW, ND, CK - 1])
        poolT = sb("poolT", [P, KW, ND, PB])
        sconvT = sb("sconvT", [P, KW, ND, SK - 1])
        cT = sb("cT", [P, KD, ND + 1])
        scaleT = sb("scaleT", [P, KD, ND + 1])
        shiftT = sb("shiftT", [P, KD, ND + 1])
        ident = sb("ident", [P, P])
        onesK = sb("onesK", [P, P])
        pick = sb("pick", [ND + 1, P])
        before = sb("before", [P, P], BF16)
        ones16 = sb("ones16", [P, P], BF16)
        sums = sb("sums", [P, 4, 2 * NTILE])
        wrouter = sb("wrouter", [P, KD, NR])
        rbias = sb("rbias", [P, NR])
        small = sb("small", [P, 128])
        onehot_both = sb("onehot_both", [P, NTILE, NE], BF16)
        tok_id = sb("tok_id", [P, NTILE], I32)
        tile_no = sb("tile_no", [P, MAX_TILES], I32)
        slot_i = sb("slot_i", [P, 2, NTILE], I32)
        table = sb("table", [P, MAX_TILES + 2], I32)
        slot_idx = sb("slot_idx", [P, 1], I32)
        zslot = sb("zslot", [P, MAX_TILES + 1], I32)
        ps = ctx.enter_context(nc.psum_tensor("ps", [P, 8, 512], F32))

        def carve(region, at, *dims):
            n = int(np.prod(dims))
            v = region[:, at:at + n]
            if len(dims) == 2:
                return v.rearrange("p (a b) -> p a b", b=dims[1])
            if len(dims) == 3:
                return v.rearrange("p (a b c) -> p a b c", b=dims[1], c=dims[2])
            return v

        def weights(b, k):
            return wbuf[:, b, :].rearrange("p (k n) -> p k n", k=k)

        x_in = carve(region_a, 0, NTILE, D)
        conf_raw = carve(region_a, 5120, 2, W)
        pool_raw = carve(region_a, 6144, W)
        sconv_raw = carve(region_a, 6656, W)
        c_raw = carve(region_a, 7168, D)
        square_junk = carve(region_a, 8192, D)
        gates = carve(region_a, 0, 3 * KD, NT)
        x1 = carve(region_a, 0, NTILE, D)
        bvec = carve(region_a, 5120, 5, D)
        G1, SH2, SC2, G2, FG = range(5)
        sc2_dec = carve(region_a, 10240, D)
        n2b = carve(region_a, 11264, D)
        UA, UB, UC = CK - 1 + NT, PB + NT, SK - 1 + NT
        ua = carve(region_b, 0, KW, UA)
        va = carve(region_b, 2200, KW, NT)
        ub = carve(region_b, 4280, KW, UB)
        pooled = carve(region_b, 6420, KW, NT)
        uc = carve(region_b, 8500, KW, UC)
        sbr = carve(region_b, 10588, KW, NT)
        squares = carve(region_b, 0, KW, NT)
        h2 = carve(region_b, 0, 2, D)
        h2T = carve(region_b, 2048, KD, P)
        t_row = carve(region_b, 3072, D)
        sq_row = carve(region_b, 4096, D)
        xg = carve(region_b, 5120, D)
        xgT = carve(region_b, 6144, KD, P)
        silu_t = carve(region_b, 7168, FF)
        act_t = carve(region_b, 7680, FF)
        actT = carve(region_b, 8192, KF, P)
        y_t = carve(region_b, 8704, D)
        yg = carve(region_b, 9728, 2, D)
        tmp_a = sb("tmp_a", [P, UB])
        tmp_b = sb("tmp_b", [P, UB])
        sig = pooled[:, 2:4, :]
        rcount = sb("rcount", [P, 16])

        CONF_PW = weights(0, KW)
        SC_OUT = weights(1, KW)
        tail = wbuf[0:40, 2, 1024:1024 + 3 * W].rearrange("p (n c) -> p n c", n=3)
        rstdT = wbuf[:, 2, 2560:2560 + NT]
        POOL_W = wbuf[:, 2, 0:4 * 256].rearrange("p (g n) -> p g n", g=4)

        ld_c = sem("ld_c")
        ld_x = sem("ld_x")
        ld_rows = sem("ld_rows")
        ld_mod = sem("ld_mod")
        ld_router = sem("ld_router")
        ld_bcast = sem("ld_bcast")
        const_ready = sem("const_ready")
        sums_ready = sem("sums_ready")
        conv_step = sem("conv_step")
        pool_chain = sem("pool_chain")
        silu_c_ready = sem("silu_c_ready")
        turned = sem("turned")
        turned_out = sem("turned_out")
        w_buf = [sem(f"w_buf{b}") for b in range(NBUF)]
        ada_done = sem("ada_done")
        mod_ready = sem("mod_ready")
        modT_done = sem("modT_done")
        scaleT_ready = sem("scaleT_ready")
        ssq_ready = sem("ssq_ready")
        root_ready = sem("root_ready")
        ms_ready = sem("ms_ready")
        xn_ready = sem("xn_ready")
        xT_done = sem("xT_done")
        hT_dec = sem("hT_dec")
        z_done = sem("z_done")
        set_free = [sem(f"set_free{m}") for m in range(4)]
        z_act = sem("z_act")
        z_dve = sem("z_dve")
        pads_ready = sem("pads_ready")
        conv_ready = sem("conv_ready")
        sq_ready = sem("sq_ready")
        centred = sem("centred")
        branch_b = sem("branch_b")
        branch_c = sem("branch_c")
        normed = sem("normed")
        branch_a = sem("branch_a")
        mix_done = sem("mix_done")
        tail_ready = sem("tail_ready")
        merged = sem("merged")
        bc_done = sem("bc_done")
        bc_ready = sem("bc_ready")
        sc2_ready = sem("sc2_ready")
        wo_done = sem("wo_done")
        t_ready = sem("t_ready")
        x1_ready = sem("x1_ready")
        h2_scaled = sem("h2_scaled")
        h2_ready = sem("h2_ready")
        h2_stored = [sem(f"h2_stored{i}") for i in range(2)]
        h2T_done = sem("h2T_done")
        h2T_ready = sem("h2T_ready")
        logit_done = sem("logit_done")
        logits_ready = sem("logits_ready")
        diff_ready = sem("diff_ready")
        exp_ready = sem("exp_ready")
        onehot_ready = sem("onehot_ready")
        count_done = sem("count_done")
        slots_ready = sem("slots_ready")
        table_ready = sem("table_ready")
        slots_zeroed = sem("slots_zeroed")
        slots_stored = sem("slots_stored")
        slot_idx_ready = sem("slot_idx_ready")
        xg_ready = sem("xg_ready")
        gather_free = sem("gather_free")
        xgT_done = sem("xgT_done")
        xgT_act = sem("xgT_act")
        xgT_dve = sem("xgT_dve")
        e_w = [[sem(f"e_w{b}_{q}") for q in range(4)] for b in range(NBUF)]
        silu_ready = sem("silu_ready")
        act_ready = sem("act_ready")
        actT_done = sem("actT_done")
        actT_ready = sem("actT_ready")
        y_act = sem("y_act")
        y_dve = sem("y_dve")
        y_stored = sem("y_stored")
        y_zeroed = sem("y_zeroed")
        yg_ready = [sem(f"yg_ready{k}") for k in range(2)]
        yg_used = sem("yg_used")
        x2_ready = sem("x2_ready")
        out_ready = sem("out_ready")
        out_stored = sem("out_stored")
        dve_step = sem("dve_step")
        act_step = sem("act_step")
        w_used = [sem(f"w_used{b}") for b in range(NBUF)]

        route_at = [11776]

        def routing(*dims):
            route_at[0] += int(np.prod(dims))
            return carve(region_b, route_at[0] - int(np.prod(dims)), *dims)

        logits = routing(NTILE, NR)
        rank4 = routing(4)
        valid = routing(NTILE)
        gdiff, eq4, tmp4, gone, sel, one_a, one_b, exp_g = (routing(NTILE, 4) for _ in range(8))
        col1 = routing(NTILE, 6)
        work16 = routing(NTILE, NE)
        slotbase = routing(NTILE, NE)
        share = routing(2, NTILE)
        slot_f = routing(2, NTILE)
        count16, tiles16, scan_a, scan_b = (routing(NE) for _ in range(4))
        tile_f = routing(MAX_TILES)
        cmp = routing(MAX_TILES, NE)
        onehot = routing(2, NTILE, NE)
        exp_in = (gdiff, col1[:, :, 2])
        exp_out = (exp_g, col1[:, :, 5])

        def rows(i):
            return P if i < NP // P else ND

        def halves(m):
            return ps[:, 2 * m:2 * m + 2, 0:HT]

        def split(ap):
            return ap.rearrange("p (h t) -> p h t", h=2)

        row_loads = [
            (params[R_TAPS:R_TAPS + CK, :], conf_dw[0]),
            (params[R_STAPS:R_STAPS + SK, :], sc_dw[0]),
            (params[R_CB:R_CB + 1, :], conf_dw_b),
            (params[R_LG:R_LG + 1, :], conf_ln_g),
            (params[R_LB:R_LB + 1, :], conf_ln_b),
            (params[R_N1:R_N1 + 2, :], norm1_g.rearrange("a (h c) -> (a h) c", h=2)),
            (params[R_PS:R_PS + 2, :], pool_scale.rearrange("a (h c) -> (a h) c", h=2)),
            (conf_raw[0:120, 0, :], state_conf[0, 0:4].rearrange("s r c -> (s r) c")),
            (conf_raw[0:120, 1, :], state_conf[0, 4:8].rearrange("s r c -> (s r) c")),
            (pool_raw[0:120, :], state_pool[0].rearrange("s r c -> (s r) c")),
            (sconv_raw[0:16, :], state_sconv[0].rearrange("s r c -> (s r) c")),
        ]

        block = ctx.enter_context(nc.Block())

        @block.sync
        def _(sp):
            sp.dma_start(mod[:, :], b_ada[0].partition_broadcast(ND + 1)).then_inc(ld_mod, 16)
            ada_v = w_ada[0].rearrange("(k p) n -> p k n", p=P)
            in_v = w_in[0].rearrange("(k p) n -> p k n", p=P)
            for b in range(NBUF):
                sp.dma_start(weights(b, KD), ada_v[:, :, b * COLS:(b + 1) * COLS]).then_inc(w_buf[b], 16)
            with sp.Fori(1, G_ADA // NBUF) as i:
                for b in range(NBUF):
                    sp.wait_ge(ada_done, NBUF * i + (b + 1 - NBUF))
                    sp.dma_start(weights(b, KD), ada_v[:, :, bass.ds(i * (NBUF * COLS) + b * COLS, COLS)]).then_inc(w_buf[b], 16)
            for b in range(NBUF):
                sp.wait_ge(ada_done, G_ADA - NBUF + b + 1)
                sp.dma_start(weights(b, KD), in_v[:, :, b * COLS:(b + 1) * COLS]).then_inc(w_buf[b], 16)
            with sp.Fori(1, G_IN // NBUF) as i:
                for b in range(NBUF):
                    sp.wait_ge(z_done, 4 * NBUF * i + 4 * (b + 1 - NBUF))
                    sp.dma_start(weights(b, KD), in_v[:, :, bass.ds(i * (NBUF * COLS) + b * COLS, COLS)]).then_inc(w_buf[b], 16)
            sp.wait_ge(z_done, 4 * (G_IN - 2))
            sp.dma_start(CONF_PW, conf_pw[0].rearrange("(k p) n -> p k n", p=P)).then_inc(w_buf[0], 16)
            sp.wait_ge(z_done, 4 * (G_IN - 1))
            sp.dma_start(SC_OUT, sc_out[0].rearrange("(k p) n -> p k n", p=P)).then_inc(w_buf[1], 16)
            sp.wait_ge(z_done, 4 * G_IN)
            sp.dma_start(POOL_W, pool_w[0].rearrange("g p n -> p g n")).then_inc(w_buf[2], 16)
            sp.wait_ge(mix_done, 28)
            wo_v = w_o[0].rearrange("(k p) n -> p k n", p=P)
            for h in range(2):
                sp.dma_start(weights(h, KD), wo_v[:, :, h * COLS:(h + 1) * COLS]).then_inc(w_buf[h], 16)
            w2_q = [wbuf[:, 2, q * D:(q + 1) * D] for q in range(KF)]
            w13_q = [[weights(b, KD)[:, 2 * q:2 * q + 2, :] for q in range(4)] for b in range(2)]
            sp.wait_ge(out_stored, 16 * 9)
            for q in range(4):
                sp.dma_start(w2_q[q], exp_w2[0, 0, q * P:(q + 1) * P, :]).then_inc(e_w[2][q], 16)
            sp.wait_ge(wo_done, NTILE)
            for b, wx in ((0, exp_w1), (1, exp_w3)):
                for q in range(4):
                    sp.dma_start(w13_q[b][q], wx[0, 0, 2 * q * P:(2 * q + 2) * P, :].rearrange("(k p) n -> p k n", p=P)).then_inc(e_w[b][q], 16)
            sp.wait_ge(table_ready, 3)
            n_tiles = sp.value_load(table[0:1, 0:1], min_val=NE, max_val=MAX_TILES)
            with sp.Fori(1, n_tiles) as j:
                e = sp.value_load(table[0:1, bass.ds(j + 1, 1)], min_val=0, max_val=NE - 1)
                for b, wx in ((0, exp_w1), (1, exp_w3)):
                    for q in range(4):
                        sp.wait_ge(w_used[b], 4 * j + (q - 3))
                        sp.dma_start(w13_q[b][q], wx[0, bass.ds(e, 1), 2 * q * P:(2 * q + 2) * P, :].rearrange("a (k p) n -> p (a k) n", p=P)).then_inc(e_w[b][q], 16)
                for q in range(KF):
                    sp.wait_ge(w_used[2], KF * j + (q + 1 - KF))
                    sp.dma_start(w2_q[q], exp_w2[0, bass.ds(e, 1), q * P:(q + 1) * P, :].rearrange("a p n -> p (a n)")).then_inc(e_w[2][q], 16)

        @block.tensor
        def _(pe):
            pe.wait_ge(const_ready, 3)
            pe.wait_ge(silu_c_ready, 1)
            for k in range(KD):
                t = pe.transpose(ps[:, 0, 9 * k:9 * k + 9], c_raw[0:ND + 1, k * P:(k + 1) * P], ident[0:ND + 1, 0:ND + 1])
            t.then_inc(turned, 1)
            pe.wait_ge(ld_rows, 16 * len(row_loads))
            for c in range(KW):
                cs = slice(c * P, (c + 1) * P)
                pe.transpose(ps[:, 1, c * N_PARAM:(c + 1) * N_PARAM], params[:, cs], ident[0:N_PARAM, 0:N_PARAM])
                pe.transpose(ps[:, 1, 256 + 16 * c:272 + 16 * c], sconv_raw[0:16, cs], ident[0:16, 0:16])
                for g in range(2):
                    o = 240 * (c % 2) + 120 * g
                    pe.transpose(ps[:, 2 + c // 2, o:o + 120], conf_raw[0:120, g, cs], ident[0:120, 0:120])
                t = pe.transpose(ps[:, 4, 120 * c:120 * c + 120], pool_raw[0:120, cs], ident[0:120, 0:120])
            t.then_inc(turned, 1)

            def ada_group(b, i, first):
                pe.wait_ge(w_buf[b], 16 * i + 16)
                if not first:
                    pe.wait_ge(mod_ready, NBUF * i + (b + 1 - NBUF))
                for k in range(KD):
                    m = pe.matmul(ps[0:ND + 1, 5 + b, :], cT[:, k, :], weights(b, KD)[:, k, :], start=(k == 0), stop=(k == KD - 1))
                m.then_inc(ada_done, 1)

            pe.wait_ge(turned_out, 1)
            for b in range(NBUF):
                ada_group(b, 0, True)
            with pe.Fori(1, G_ADA // NBUF) as i:
                for b in range(NBUF):
                    ada_group(b, i, False)
            pe.wait_ge(mod_ready, G_ADA)
            for k in range(2 * KD):
                t = pe.transpose(ps[:, 0, 9 * k:9 * k + 9], mod[:, k * P:(k + 1) * P], ident[0:ND + 1, 0:ND + 1])
            t.then_inc(modT_done, 1)
            pe.wait_ge(xn_ready, NTILE)
            pe.wait_ge(turned_out, 4)
            for k in range(KD):
                t = pe.transpose(ps[:, 1, 8 * k:8 * k + 8], x_in[0:ND, 4, k * P:(k + 1) * P], ident[0:ND, 0:ND])
            t.then_inc(xT_done, 1)
            pe.wait_ge(hT_dec, 1)
            for k in range(KD):
                for i in range(NP // P):
                    t = pe.transpose(ps[:, k, i * P:(i + 1) * P], x_in[:, i, k * P:(k + 1) * P], ident[:, :])
                t.then_inc(xT_done, 1)

            for m in range(4):
                pe.wait_ge(set_free[m], 2)

            with pe.Fori(0, G_IN // NBUF) as i:
                for b in range(NBUF):
                    pe.wait_ge(w_buf[b], 16 * i + 16 * (G_ADA // NBUF + 1))
                    for m in range(4):
                        pe.wait_ge(set_free[m], NBUF * i + (b + 2))
                        for k in range(KD):
                            w = weights(b, KD)[:, k, m * P:(m + 1) * P]
                            for h in range(2):
                                mm = pe.matmul(ps[:, 2 * m + h, 0:HT], w, hT[:, k, h * HT:(h + 1) * HT], start=(k == 0), stop=(k == KD - 1))
                        mm.then_inc(z_done, 1)

            unit = [0]

            def next_set():
                s = unit[0] % 4
                pe.wait_ge(set_free[s], 2 + G_IN + unit[0] // 4)
                unit[0] += 1
                return s

            def product(s, lhs, rhs, n):
                for k in range(n):
                    for h in range(2):
                        mm = pe.matmul(ps[:, 2 * s + h, 0:HT], lhs(k), rhs(k)[:, h * HT:(h + 1) * HT], start=(k == 0), stop=(k == n - 1))
                mm.then_inc(mix_done, 1)

            pe.wait_ge(conv_ready, 1)
            product(next_set(), lambda k: onesK[:, :], lambda k: va[:, k, :], KW)
            s = next_set()
            for c in range(KW):
                pe.transpose(ps[0:38, 2 * s, c * P:(c + 1) * P], ua[:, c, UA - 38:UA], ident[:, :])
                t = pe.transpose(ps[0:23, 2 * s + 1, c * P:(c + 1) * P], ub[:, c, UB - 23:UB], ident[:, :])
            t.then_inc(mix_done, 1)
            s = next_set()
            pe.wait_ge(branch_c, KW)
            for c in range(KW):
                t = pe.transpose(ps[0:10, 2 * s, c * P:(c + 1) * P], uc[:, c, UC - 10:UC], ident[:, :])
            t.then_inc(mix_done, 1)
            pe.wait_ge(branch_b, len(WINDOWS))
            pe.wait_ge(w_buf[2], 16 * (2 * 4 + 1))
            for j in range(KD):
                g = j // 2
                product(next_set(), lambda k: POOL_W[:, g, (j % 2) * P:(j % 2 + 1) * P], lambda k: pooled[:, g, :], 1)
            pe.wait_ge(sq_ready, 1)
            product(next_set(), lambda k: onesK[:, :], lambda k: squares[:, k, :], KW)
            pe.wait_ge(w_buf[1], 16 * (2 * 4 + 1))
            for j in range(KD):
                product(next_set(), lambda k: SC_OUT[:, k, j * P:(j + 1) * P], lambda k: sbr[:, k, :], KW)
            pe.wait_ge(branch_a, 1)
            pe.wait_ge(w_buf[0], 16 * (2 * 4 + 1))
            for j in range(KD):
                product(next_set(), lambda k: CONF_PW[:, k, j * P:(j + 1) * P], lambda k: va[:, k, :], KW)

            for n in range(8):
                if n % 2 == 0:
                    pe.wait_ge(set_free[n // 2], 2 + G_IN + 7)
                col = (2 + n // 2) * D + (n % 2) * COLS
                pe.matmul(ps[:, n, :], pick[:, :], mod[:, col:col + COLS], start=True, stop=True).then_inc(bc_done, 1)

            pe.wait_ge(merged, 2 * KD)
            for h in range(2):
                pe.wait_ge(w_buf[h], 16 * (2 * 4 + 2))

            def w_o_tile(i):
                n = rows(i)
                pe.wait_ge(bc_ready, 8 if i else 4)
                if i >= 2:
                    pe.wait_ge(t_ready, i - 1)
                for h in range(2):
                    for k in range(KD):
                        mm = pe.matmul(ps[0:n, 2 * (i % 2) + h, :], hT[:, k, i * P:i * P + n], weights(h, KD)[:, k, :], start=(k == 0), stop=(k == KD - 1))
                mm.then_inc(wo_done, 1)

            def router_tile(i):
                n = rows(i)
                pe.wait_ge(h2_ready, i + 1)
                if i >= 1:
                    pe.wait_ge(h2T_ready, i)
                for k in range(KD):
                    t = pe.transpose(ps[:, 4 + k // 4, (k % 4) * P:(k % 4) * P + n], h2[0:n, i % 2, k * P:(k + 1) * P], ident[0:n, 0:n])
                t.then_inc(h2T_done, 1)
                pe.wait_ge(h2T_ready, i + 1)
                if i >= 1:
                    pe.wait_ge(logits_ready, i)
                for k in range(KD):
                    mm = pe.matmul(ps[0:n, 6, 0:NR], h2T[:, k, 0:n], wrouter[:, k, :], start=(k == 0), stop=(k == KD - 1))
                mm.then_inc(logit_done, 1)

            pe.wait_ge(ld_router, 64)
            for i in range(NTILE + 1):
                if i < NTILE:
                    w_o_tile(i)
                if i >= 1:
                    router_tile(i - 1)

            pe.wait_ge(onehot_ready, 1)
            oh = onehot_both
            for i in range(NTILE):
                for j in range(i + 1):
                    pe.matmul(ps[:, 7, i * NE:(i + 1) * NE], (before if j == i else ones16)[:, :], oh[:, j, :], start=(j == 0), stop=(j == i))
            for j in range(NTILE):
                mm = pe.matmul(ps[:, 7, NTILE * NE:(NTILE + 1) * NE], ones16[:, :], oh[:, j, :], start=(j == 0), stop=(j == NTILE - 1))
            mm.then_inc(count_done, 1)

            def up(b, j, evacuated, first):
                for q in range(4):
                    pe.wait_ge(e_w[b][q], 16 * j + 16)
                    for k in (2 * q, 2 * q + 1):
                        if k == 0 and not first:
                            pe.wait_ge(evacuated, j)
                        mm = pe.matmul(ps[:, b, :], xgT[:, k, :], weights(b, KD)[:, k, :], start=(k == 0), stop=(k == KD - 1))
                    mm.then_inc(w_used[b], 1)

            def turn_rows(j):
                pe.wait_ge(xg_ready, 16 * j + 16)
                for k in range(KD):
                    t = pe.transpose(ps[:, 2 + k // 4, (k % 4) * P:(k % 4 + 1) * P], xg[:, k * P:(k + 1) * P], ident[:, :])
                t.then_inc(xgT_done, 1)

            def turn_product(j):
                pe.wait_ge(act_ready, j + 1)
                for k in range(KF):
                    t = pe.transpose(ps[:, 6, k * P:(k + 1) * P], act_t[:, k * P:(k + 1) * P], ident[:, :])
                t.then_inc(actT_done, 1)

            def down(jn, jm, first):
                pe.wait_ge(actT_ready, jn)
                if not first:
                    pe.wait_ge(y_act, jm)
                    pe.wait_ge(y_dve, jm)
                for q in range(KF):
                    pe.wait_ge(e_w[2][q], 16 * jn)
                    for h in range(2):
                        mm = pe.matmul(ps[:, 4 + h, :], actT[:, q, :], wbuf[:, 2, q * D + h * COLS:q * D + (h + 1) * COLS], start=(q == 0), stop=(q == KF - 1))
                    mm.then_inc(w_used[2], 1)

            pe.wait_ge(table_ready, 3)
            n_tiles = pe.value_load(table[0:1, 0:1], min_val=NE, max_val=MAX_TILES)
            last = pe.value_load(table[0:1, MAX_TILES + 1:MAX_TILES + 2], min_val=NE - 1, max_val=MAX_TILES - 1)
            turn_rows(0)
            for j in range(2):
                first = j == 0
                pe.wait_ge(xgT_act, j + 1)
                pe.wait_ge(xgT_dve, j + 1)
                up(0, j, silu_ready, first)
                up(1, j, act_ready, first)
                turn_rows(j + 1)
                if not first:
                    down(j, j - 1, True)
                turn_product(j)
            with pe.Fori(2, n_tiles) as j:
                pe.wait_ge(xgT_act, j + 1)
                pe.wait_ge(xgT_dve, j + 1)
                up(0, j, silu_ready, False)
                up(1, j, act_ready, False)
                turn_rows(j + 1)
                down(j, j - 1, False)
                turn_product(j)
            down(n_tiles, last, False)

        @block.scalar
        def _(act):
            steps = [0]

            def link(ins):
                steps[0] += 1
                ins.then_inc(act_step, 1)
                act.wait_ge(act_step, steps[0])

            act.dma_start(c_raw[0:ND, :], c_sample).then_inc(ld_c, 16)
            act.dma_start(c_raw[ND:ND + 1, :], c_prompt).then_inc(ld_c, 16)
            for i in range(NP // P):
                act.dma_start(x_in[:, i, :], x_prompt[0, i * P:(i + 1) * P, :]).then_inc(ld_x, 16)
            act.dma_start(x_in[0:ND, 4, :], x_sample.rearrange("b t d -> (b t) d")).then_inc(ld_x, 16)
            for dst, src in row_loads:
                act.dma_start(dst, src).then_inc(ld_rows, 16)
            act.dma_start(wrouter[:, :, 0:NG], router_g[0].rearrange("(k p) n -> p k n", p=P)).then_inc(ld_router, 16)
            act.dma_start(wrouter[:, :, NG:NR], router_e[0].rearrange("(k p) n -> p k n", p=P)).then_inc(ld_router, 16)
            act.dma_start(rbias[:, 0:NG], router_g_b[0].partition_broadcast(P)).then_inc(ld_router, 16)
            act.dma_start(rbias[:, NG:NR], router_e_b[0].partition_broadcast(P)).then_inc(ld_router, 16)
            act.dma_start(conf_s[0, :, 0:CK - 2, :], state_conf[0, :, 1:CK - 1, :]).then_inc(out_stored, 16)
            act.dma_start(pool_s[0, :, 0:PB - 1, :], state_pool[0, :, 1:PB, :]).then_inc(out_stored, 16)
            act.dma_start(sconv_s[0, :, 0:SK - 2, :], state_sconv[0, :, 1:SK - 1, :]).then_inc(out_stored, 16)

            act.wait_ge(ld_c, 32)
            act.activation(c_raw[0:ND + 1, :], c_raw[0:ND + 1, :], ACT.Silu).then_inc(silu_c_ready, 1)
            act.wait_ge(ld_x, 16 * NTILE)
            act.wait_ge(sums_ready, 1)
            for i in range(NTILE):
                n = rows(i)
                if i:
                    act.wait_ge(ssq_ready, i)
                act.activation(square_junk[0:n, :], x_in[0:n, i, :], ACT.Square, accum_out=sums[0:n, 0, i:i + 1]).then_inc(ssq_ready, 1)
            act.wait_ge(ms_ready, 1)
            act.activation(sums[:, 2, 0:NTILE], sums[:, 1, 0:NTILE], ACT.Sqrt).then_inc(root_ready, 1)
            act.wait_ge(scaleT_ready, 2)
            for k in range(0, KD, 2):
                act.wait_ge(xT_done, k + 2)
                act.activation(hT[:, k, 0:NP], ps[:, k, :], ACT.Identity, bias=shiftT[:, k, ND:ND + 1], scale=scaleT[:, k, ND:ND + 1]).then_inc(set_free[k // 2], 1)

            act.wait_ge(pads_ready, 1)
            for g in range(G_IN):
                if g == 5:
                    continue
                for m in range(4):
                    act.wait_ge(z_done, 4 * g + m + 1)
                    if g == 0:
                        act.activation(split(ua[:, m, CK - 1:UA]), halves(m), ACT.Copy).then_inc(set_free[m], 1)
                    elif g == 1:
                        if m >= 2:
                            act.wait_ge(z_dve, m - 1)
                        act.activation(split(sig[:, m % 2, :]), halves(m), ACT.Sigmoid).then_inc(set_free[m], 1)
                    elif g == 2:
                        act.activation(split(ub[:, m, PB:UB]), halves(m), ACT.Copy).then_inc(set_free[m], 1)
                    elif g == 3:
                        act.activation(split(uc[:, m, SK - 1:UC]), halves(m), ACT.Copy).then_inc(set_free[m], 1)
                    elif g == 4:
                        act.activation(split(sbr[:, m, :]), halves(m), ACT.Copy).then_inc(set_free[m], 1)
                    else:
                        act.activation(split(gates[:, 4 * (g - 6) + m, :]), halves(m), ACT.Sigmoid).then_inc(set_free[m], 1)

            act.wait_ge(z_done, 4 * G_IN)
            act.wait_ge(mix_done, 2)
            act.activation(tail[0:38, 0, :], ps[0:38, 2, :], ACT.Copy).then_inc(tail_ready, 1)
            act.activation(tail[0:23, 1, :], ps[0:23, 3, :], ACT.Copy).then_inc(set_free[1], 1)
            act.wait_ge(mix_done, 3)
            act.activation(tail[0:10, 2, :], ps[0:10, 4, :], ACT.Copy).then_inc(set_free[2], 1)
            act.wait_ge(tail_ready, 1)
            act.wait_ge(set_free[1], 2 + G_IN + 1)
            act.wait_ge(set_free[2], 2 + G_IN + 1)
            for n, (own, last, new_p, new_s) in enumerate(((CK - 1, CK - 2, conf_p, conf_s), (PB, PB - 1, pool_p, pool_s), (SK - 1, SK - 2, sconv_p, sconv_s))):
                act.dma_start(new_p[0, 0], tail[0:own, n, :]).then_inc(out_stored, 16)
                act.dma_start(new_s[0, :, last, :], tail[own:own + ND, n, :]).then_inc(out_stored, 16)
            act.wait_ge(centred, KW - 1)
            act.wait_ge(set_free[0], 2 + G_IN + 1)
            for c in range(KW):
                s = act.activation(squares[:, c, :], va[:, c, :], ACT.Square)
            s.then_inc(sq_ready, 1)
            act.wait_ge(ms_ready, 2)
            act.activation(tmp_b[:, 0:NT], tmp_a[:, 0:NT], ACT.Sqrt).then_inc(root_ready, 1)
            act.wait_ge(normed, KW)
            for c in range(KW):
                s = act.activation(va[:, c, :], va[:, c, :], ACT.Silu, bias=pT[:, c, R_LB:R_LB + 1], scale=pT[:, c, R_LG:R_LG + 1])
            s.then_inc(branch_a, 1)

            act.wait_ge(merged, 2 * KD)
            act.dma_start(n2b, norm2_g[0].partition_broadcast(P)).then_inc(ld_bcast, 16)
            act.dma_start(bvec[:, FG, :], final_g.partition_broadcast(P)).then_inc(ld_bcast, 16)
            for i in range(NP // P):
                act.dma_start(x1[:, i, :], x_prompt[0, i * P:(i + 1) * P, :]).then_inc(ld_x, 16)
            act.dma_start(x1[0:ND, 4, :], x_sample.rearrange("b t d -> (b t) d")).then_inc(ld_x, 16)
            for n in range(8):
                act.wait_ge(bc_done, n + 1)
                act.activation(bvec[:, n // 2, (n % 2) * COLS:(n % 2 + 1) * COLS], ps[:, n, :], ACT.Copy).then_inc(bc_ready, 1)
            for i in range(NTILE):
                n = rows(i)
                act.wait_ge(x1_ready, i + 1)
                act.activation(sq_row[0:n, :], x1[0:n, i, :], ACT.Square, accum_out=sums[0:n, 0, i:i + 1]).then_inc(ssq_ready, 1)
                act.wait_ge(ms_ready, 3 + i)
                act.activation(sums[0:n, 2, i:i + 1], sums[0:n, 1, i:i + 1], ACT.Sqrt).then_inc(root_ready, 1)
                act.wait_ge(h2_ready, i + 1)
                act.dma_start(h2_dram[i * P:i * P + n, :], h2[0:n, i % 2, :]).then_inc(h2_stored[i % 2], 16)
                act.wait_ge(h2T_done, i + 1)
                if i >= 1:
                    act.wait_ge(logit_done, i)
                act.activation(h2T[:, :, 0:n].rearrange("p (b k) t -> p b k t", b=2),
                               ps[:, 4:6, :].rearrange("p b (k t) -> p b k t", k=4)[:, :, :, 0:n], ACT.Copy).then_inc(h2T_ready, 1)
            for n in range(2):
                act.wait_ge(diff_ready, n + 1)
                act.activation(exp_out[n], exp_in[n], ACT.Exp).then_inc(exp_ready, 1)

            def silu_tile(j, first):
                act.wait_ge(w_used[0], 4 * j + 4)
                if not first:
                    act.wait_ge(act_ready, j)
                act.activation(silu_t, ps[:, 0, :], ACT.Silu).then_inc(silu_ready, 1)

            def turned_rows_out(j):
                act.wait_ge(xgT_done, j + 1)
                act.activation(xgT[:, 0:4, :], ps[:, 2, :].rearrange("p (k t) -> p k t", k=4), ACT.Copy).then_inc(xgT_act, 1)

            def y_out(jn, jm, first):
                act.wait_ge(w_used[2], KF * jn)
                if not first:
                    act.wait_ge(y_stored, 16 * jm)
                act.activation(y_t[:, 0:COLS], ps[:, 4, :], ACT.Copy).then_inc(y_act, 1)
                act.wait_ge(y_act, jn)
                act.wait_ge(y_dve, jn)
                act.dma_start(y_dram[bass.ds(jm * P, P), :], y_t).then_inc(y_stored, 16)

            def turned_product_out(j):
                act.wait_ge(actT_done, j + 1)
                act.activation(actT, ps[:, 6, :].rearrange("p (k t) -> p k t", k=KF), ACT.Copy).then_inc(actT_ready, 1)

            act.wait_ge(y_zeroed, 16 * (MAX_TILES - NE))
            act.wait_ge(table_ready, 3)
            n_tiles = act.value_load(table[0:1, 0:1], min_val=NE, max_val=MAX_TILES)
            last = act.value_load(table[0:1, MAX_TILES + 1:MAX_TILES + 2], min_val=NE - 1, max_val=MAX_TILES - 1)
            turned_rows_out(0)
            for j in range(2):
                silu_tile(j, j == 0)
                turned_rows_out(j + 1)
                if j:
                    y_out(j, j - 1, True)
                turned_product_out(j)
            with act.Fori(2, n_tiles) as j:
                silu_tile(j, False)
                turned_rows_out(j + 1)
                y_out(j, j - 1, False)
                turned_product_out(j)
            y_out(n_tiles, last, False)
            for i in range(NTILE):
                n = rows(i)
                act.wait_ge(x2_ready, i + 1)
                act.activation(sq_row[0:n, :], x1[0:n, i, :], ACT.Square, accum_out=sums[0:n, 0, NTILE + i:NTILE + i + 1]).then_inc(ssq_ready, 1)
                act.wait_ge(ms_ready, 3 + NTILE + i)
                act.activation(sums[0:n, 2, NTILE + i:NTILE + i + 1], sums[0:n, 1, NTILE + i:NTILE + i + 1], ACT.Sqrt).then_inc(root_ready, 1)
                act.wait_ge(out_ready, i + 1)
                dst = y_prompt[0, i * P:(i + 1) * P, :] if i < NP // P else y_sample.rearrange("b t d -> (b t) d")
                act.dma_start(dst, x1[0:n, i, :]).then_inc(out_stored, 16)
            act.wait_ge(out_stored, 16 * (3 + 6 + NTILE))

        @block.gpsimd
        def _(pool):
            pool.memset(ident[:, :], 0.0).then_inc(pool_chain, 1)
            pool.memset(before[:, :], 1.0).then_inc(pool_chain, 1)
            pool.memset(onesK[:, :], 1.0 / W).then_inc(pool_chain, 1)
            pool.memset(ones16[:, :], 1.0).then_inc(pool_chain, 1)
            pool.memset(pick[:, :], 1.0).then_inc(pool_chain, 1)
            pool.iota(tok_id[:, :], [[P, NTILE]], base=0, channel_multiplier=1).then_inc(pool_chain, 1)
            pool.iota(tile_no[:, :], [[1, MAX_TILES]], base=0, channel_multiplier=0).then_inc(pool_chain, 1)
            pool.memset(zslot[:, :], 0).then_inc(pool_chain, 1)
            pool.wait_ge(pool_chain, 8)
            pool.affine_select(out=ident[:, :], in_=ident[:, :], compare_op=ALU.not_equal, fill=1.0, base=0,
                               pattern=[[-1, P]], channel_multiplier=1).then_inc(const_ready, 1)
            pool.affine_select(out=before[:, :], in_=before[:, :], compare_op=ALU.is_gt, fill=0.0, base=0,
                               pattern=[[1, P]], channel_multiplier=-1).then_inc(const_ready, 1)
            pool.memset(pick[0:ND, :], 0.0).then_inc(const_ready, 1)
            pool.memset(region_b[:, 0:D], 0.0).then_inc(pool_chain, 1)
            pool.wait_ge(pool_chain, 9)
            for t in range(NE, MAX_TILES):
                pool.dma_start(y_dram[t * P:(t + 1) * P, :], region_b[:, 0:D]).then_inc(y_zeroed, 16)
            pool.dma_start(slot_dram.rearrange("(p t) a -> p (t a)", p=P), zslot[:, :]).then_inc(slots_zeroed, 16)

            for i in range(NTILE):
                n = rows(i)
                pool.wait_ge(t_ready, i + 1)
                pool.tensor_tensor(x1[0:n, i, :], x1[0:n, i, :], t_row[0:n, :], ALU.add).then_inc(x1_ready, 1)
                shift = bvec[0:n, SH2, :] if i < NP // P else mod[0:ND, 3 * D:4 * D]
                pool.wait_ge(h2_scaled, i + 1)
                pool.tensor_tensor(h2[0:n, i % 2, :], h2[0:n, i % 2, :], shift, ALU.add).then_inc(h2_ready, 1)

            pool.wait_ge(slots_ready, 1)
            pool.wait_ge(slots_zeroed, 16)
            for k in range(2):
                for i in range(NTILE):
                    n = rows(i)
                    pool.indirect_dma_start(slot_dram, bass.IndirectOffsetOnAxis(ap=slot_i[0:n, k, i:i + 1], axis=0),
                                            tok_id[0:n, i:i + 1], None).then_inc(slots_stored, 16)
            pool.wait_ge(slots_stored, 16 * 2 * NTILE)
            def gather(j, first):
                if not first:
                    pool.wait_ge(xg_ready, 16 * j)
                pool.dma_start(slot_idx[:, :], slot_dram[bass.ds(j * P, P), :]).then_inc(slot_idx_ready, 16)
                pool.wait_ge(slot_idx_ready, 16 * j + 16)
                if not first:
                    pool.wait_ge(xgT_done, j)
                for p in range(2):
                    pool.wait_ge(h2_stored[p], 16 * ((NTILE + 1 - p) // 2))
                pool.sem_inc(gather_free, 1)
                pool.indirect_dma_start(xg, None, h2_dram, bass.IndirectOffsetOnAxis(ap=slot_idx[:, :], axis=0)).then_inc(xg_ready, 16)

            pool.wait_ge(table_ready, 3)
            n_tiles = pool.value_load(table[0:1, 0:1], min_val=NE, max_val=MAX_TILES)
            gather(0, True)
            with pool.Fori(1, n_tiles + 1) as j:
                gather(j, False)
            pool.wait_ge(y_stored, 16 * n_tiles)
            pool.sem_inc(gather_free, 1)
            for i in range(NTILE):
                n = rows(i)
                if i:
                    pool.wait_ge(yg_used, i)
                for k in range(2):
                    pool.indirect_dma_start(yg[0:n, k, :], None, y_dram, bass.IndirectOffsetOnAxis(ap=slot_i[0:n, k, i:i + 1], axis=0)).then_inc(yg_ready[k], 16)

        @block.vector
        def _(dve):
            steps = [0]

            def link(ins, signal=None, value=0):
                if signal is None:
                    steps[0] += 1
                ins.then_inc(dve_step if signal is None else signal, 1)
                dve.wait_ge(dve_step if signal is None else signal, steps[0] if signal is None else value)

            def rsqrt(ms, root, out, tmp, n_root):
                dve.wait_ge(root_ready, n_root)
                link(dve.reciprocal(out, root))
                link(dve.tensor_tensor(tmp, out, out, ALU.mult))
                link(dve.tensor_tensor(tmp, tmp, ms, ALU.mult))
                link(dve.tensor_scalar(tmp, tmp, -0.5, 1.5, ALU.mult, ALU.add))
                link(dve.tensor_tensor(out, out, tmp, ALU.mult))

            dve.memset(sums[:, :, :], 1.0).then_inc(sums_ready, 1)
            for t in range(16):
                dve.memset(rcount[:, t:t + 1], 1.0 / (t + 1))

            dve.wait_ge(turned, 1)
            dve.tensor_copy(cT[:, :, :], ps[:, 0, 0:9 * KD].rearrange("p (k s) -> p k s", s=9)).then_inc(turned_out, 1)
            dve.wait_ge(turned, 2)
            dve.tensor_copy(pT[:, :, :], ps[:, 1, 0:KW * N_PARAM].rearrange("p (c r) -> p c r", c=KW))
            dve.tensor_copy(sconvT[:, :, :, :], ps[:, 1, 256:320].rearrange("p (c s r) -> p c s r", c=KW, s=ND)).then_inc(turned_out, 1)
            for c in range(2):
                dve.tensor_copy(confT[:, 2 * c:2 * c + 2, :, :].rearrange("p c s r -> p (c s r)"), ps[:, 2 + c, 0:480])
            dve.tensor_copy(poolT[:, :, :, :], ps[:, 4, 0:480].rearrange("p (c s r) -> p c s r", c=KW, s=ND)).then_inc(turned_out, 2)

            dve.wait_ge(ld_mod, 16)

            def mod_group(b, i):
                dve.wait_ge(ada_done, NBUF * i + b + 1)
                cols = mod[:, bass.ds(i * (NBUF * COLS) + b * COLS, COLS)]
                dve.tensor_tensor(cols, ps[0:ND + 1, 5 + b, :], cols, ALU.add).then_inc(mod_ready, 1)

            with dve.Fori(0, G_ADA // NBUF) as i:
                for b in range(NBUF):
                    mod_group(b, i)

            dve.wait_ge(modT_done, 1)
            dve.tensor_copy(shiftT[:, :, :], ps[:, 0, 0:72].rearrange("p (k s) -> p k s", s=9))
            link(dve.tensor_scalar(scaleT[:, :, :], ps[:, 0, 72:144].rearrange("p (k s) -> p k s", s=9), 1.0, None, ALU.add))
            for h in range(2):
                s = dve.tensor_tensor(scaleT[:, 4 * h:4 * h + 4, :], scaleT[:, 4 * h:4 * h + 4, :],
                                      pT[:, :, R_N1 + h:R_N1 + h + 1].broadcast_to([P, KW, ND + 1]), ALU.mult)
                s.then_inc(scaleT_ready, 1)

            dve.wait_ge(ssq_ready, NTILE)
            dve.tensor_scalar(sums[:, 1, 0:NTILE], sums[:, 0, 0:NTILE], 1.0 / D, EPS, ALU.mult, ALU.add).then_inc(ms_ready, 1)
            dve.wait_ge(ms_ready, 1)
            rsqrt(sums[:, 1, 0:NTILE], sums[:, 2, 0:NTILE], sums[:, 3, 0:NTILE], sums[:, 2, 0:NTILE], 1)
            for i in range(NTILE):
                n = rows(i)
                dve.tensor_scalar(x_in[0:n, i, :], x_in[0:n, i, :], sums[0:n, 3, i:i + 1], None, ALU.mult).then_inc(xn_ready, 1)
            dve.wait_ge(xT_done, 1)
            dve.wait_ge(scaleT_ready, 2)
            link(dve.tensor_tensor(small[:, 0:64].rearrange("p (k s) -> p k s", k=KD), ps[:, 1, 0:64].rearrange("p (k s) -> p k s", k=KD), scaleT[:, :, 0:ND], ALU.mult))
            dve.tensor_tensor(hT[:, :, NP:NT], small[:, 0:64].rearrange("p (k s) -> p k s", k=KD), shiftT[:, :, 0:ND], ALU.add).then_inc(hT_dec, 1)
            for k in range(1, KD, 2):
                dve.wait_ge(xT_done, k + 2)
                dve.tensor_scalar(hT[:, k, 0:NP], ps[:, k, :], scaleT[:, k, ND:ND + 1], shiftT[:, k, ND:ND + 1], ALU.mult, ALU.add).then_inc(set_free[k // 2], 1)

            dve.wait_ge(y_zeroed, 16 * (MAX_TILES - NE))
            dve.memset(ua[:, :, 0:CK - 1], 0.0)
            dve.memset(ub[:, :, 0:PB], 0.0)
            dve.memset(uc[:, :, 0:SK - 1], 0.0).then_inc(pads_ready, 1)

            for m in range(4):
                dve.wait_ge(set_free[m], 2 + 2)
                dve.tensor_tensor(ua[:, m, CK - 1:UA], ua[:, m, CK - 1:UA], sig[:, m % 2, :], ALU.mult).then_inc(z_dve, 1)
            dve.wait_ge(z_dve, 4)

            def taps(t):
                for c in range(KW):
                    w = pT[:, c, R_TAPS + t:R_TAPS + t + 1]
                    if t:
                        dve.wait_ge(conv_step, KW * (t - 1) + c + 1)
                        dve.scalar_tensor_tensor(va[:, c, 0:NP], ua[:, c, t:t + NP], w, va[:, c, 0:NP], ALU.mult, ALU.add).then_inc(conv_step, 1)
                    else:
                        dve.tensor_scalar(va[:, c, 0:NP], ua[:, c, 0:NP], w, pT[:, c, R_CB:R_CB + 1], ALU.mult, ALU.add).then_inc(conv_step, 1)

            for t in range(CK):
                taps(t)
            prod = confT[:, :, :, :]
            for c in range(KW):
                s = dve.tensor_tensor(prod[:, c, :, :], confT[:, c, :, :], pT[:, c:c + 1, 0:CK - 1].broadcast_to([P, ND, CK - 1]), ALU.mult)
            link(s)
            va_d, ua_d = va[:, :, NP:NT], ua[:, :, CK - 1 + NP:UA]
            dec = small[:, 64:96].rearrange("p (c s) -> p c s", c=KW)
            link(dve.tensor_reduce(va_d, prod, AX.X, ALU.add))
            link(dve.tensor_tensor(dec, ua_d, pT[:, :, CK - 1:CK].broadcast_to([P, KW, ND]), ALU.mult))
            link(dve.tensor_tensor(va_d, va_d, dec, ALU.add))
            dve.tensor_tensor(va_d, va_d, pT[:, :, R_CB:R_CB + 1].broadcast_to([P, KW, ND]), ALU.add).then_inc(conv_ready, 1)

            for g, w in enumerate(WINDOWS):
                dve.wait_ge(set_free[g], 2 + 3)
                src, n = ub[:, g, 0:PB + NP], 1
                for turn, dst in enumerate((tmp_a, tmp_b, tmp_a, tmp_b)[:g + 1]):
                    lo = 2 * n - 1
                    link(dve.tensor_tensor(dst[:, lo:PB + NP], src[:, lo:PB + NP], src[:, lo - n:PB + NP - n], ALU.add))
                    src, n = dst, 2 * n
                tok, tot, out = ub[:, g, PB:PB + NP], src[:, PB:PB + NP], pooled[:, g, 0:NP]
                link(dve.scalar_tensor_tensor(out, tot, 1.0 / w, tok, ALU.mult, ALU.subtract))
                link(dve.tensor_tensor(small[:, 0:w - 1], tot[:, 0:w - 1], rcount[:, 0:w - 1], ALU.mult))
                link(dve.tensor_tensor(out[:, 0:w - 1], small[:, 0:w - 1], tok[:, 0:w - 1], ALU.subtract))
                tok, out, tot = ub[:, g, PB + NP:UB], pooled[:, g, NP:NT], small[:, 32:40]
                link(dve.tensor_reduce(tot, poolT[:, g, :, PB - (w - 1):PB], AX.X, ALU.add))
                link(dve.tensor_tensor(tot, tot, tok, ALU.add))
                link(dve.scalar_tensor_tensor(out, tot, 1.0 / w, tok, ALU.mult, ALU.subtract), branch_b, g + 1)

            for m in range(4):
                dve.wait_ge(z_done, 4 * 5 + m + 1)
                dve.wait_ge(set_free[m], 2 + 5)
                dve.tensor_tensor(split(uc[:, m, SK - 1:UC]), halves(m), split(uc[:, m, SK - 1:UC]), ALU.mult).then_inc(set_free[m], 1)
            for m in range(4):
                dve.wait_ge(set_free[m], 2 + 6)
                tap = [pT[:, m, R_STAPS + t:R_STAPS + t + 1] for t in range(SK)]
                acc = tmp_a[:, 0:NP]
                link(dve.tensor_scalar(acc, uc[:, m, 0:NP], tap[0], None, ALU.mult))
                link(dve.scalar_tensor_tensor(acc, uc[:, m, 1:1 + NP], tap[1], acc, ALU.mult, ALU.add))
                link(dve.scalar_tensor_tensor(acc, uc[:, m, 2:2 + NP], tap[2], acc, ALU.mult, ALU.add))
                link(dve.tensor_tensor(sbr[:, m, 0:NP], sbr[:, m, 0:NP], acc, ALU.mult))
                acc = tmp_a[:, 0:ND]
                link(dve.tensor_scalar(acc, sconvT[:, m, :, 0:1].rearrange("p s r -> p (s r)"), tap[0], None, ALU.mult))
                link(dve.scalar_tensor_tensor(acc, sconvT[:, m, :, 1:2].rearrange("p s r -> p (s r)"), tap[1], acc, ALU.mult, ALU.add))
                link(dve.scalar_tensor_tensor(acc, uc[:, m, SK - 1 + NP:UC], tap[2], acc, ALU.mult, ALU.add))
                link(dve.tensor_tensor(sbr[:, m, NP:NT], sbr[:, m, NP:NT], acc, ALU.mult), branch_c, m + 1)

            dve.wait_ge(mix_done, 1)
            dve.wait_ge(conv_ready, 1)
            for c in range(KW):
                s = dve.tensor_tensor(split(va[:, c, :]), split(va[:, c, :]), halves(0), ALU.subtract)
                s.then_inc(centred if c < KW - 1 else set_free[0], 1)

            def unit(n):
                dve.wait_ge(mix_done, n + 1)
                return n % 4

            def free_at(n):
                return 2 + G_IN + n // 4 + 1

            for j in range(KD):
                s = unit(3 + j)
                dve.scalar_tensor_tensor(split(hT[:, j, :]), halves(s), pT[:, j % 4, R_PS + j // 4:R_PS + j // 4 + 1], split(gates[:, KD + j, :]), ALU.mult, ALU.mult).then_inc(set_free[s], 1)
            s = unit(11)
            link(dve.tensor_scalar(split(tmp_b[:, 0:NT]), halves(s), EPS, None, ALU.add), set_free[s], free_at(11))
            dve.tensor_copy(tmp_a[:, 0:NT], tmp_b[:, 0:NT]).then_inc(ms_ready, 1)
            dve.wait_ge(ms_ready, 2)
            rsqrt(tmp_a[:, 0:NT], tmp_b[:, 0:NT], rstdT, tmp_b[:, 0:NT], 2)
            for c in range(KW):
                dve.tensor_tensor(va[:, c, :], va[:, c, :], rstdT, ALU.mult).then_inc(normed, 1)
            for base, first in ((12, 2 * KD), (20, 0)):
                for j in range(KD):
                    s = unit(base + j)
                    tmp = (tmp_a, tmp_b)[j % 2][:, 0:NT]
                    link(dve.tensor_tensor(split(tmp), halves(s), split(gates[:, first + j, :]), ALU.mult), set_free[s], free_at(base + j))
                    dve.tensor_tensor(hT[:, j, :], hT[:, j, :], tmp, ALU.add).then_inc(merged, 1)

            dve.wait_ge(merged, 2 * KD)
            for r in range(4):
                dve.memset(rank4[:, r:r + 1], 4.0 - r)
            dve.memset(valid[:, 0:NTILE - 1], 1.0)
            link(dve.memset(valid[:, NTILE - 1:NTILE], 0.0))
            dve.memset(valid[0:ND, NTILE - 1:NTILE], 1.0)
            link(dve.memset(logits[:, :, :], 0.0))
            dve.wait_ge(ld_bcast, 32)
            dve.wait_ge(bc_ready, 8)
            dve.wait_ge(merged, 2 * KD)
            link(dve.scalar_tensor_tensor(bvec[:, SC2, :], bvec[:, SC2, :], 1.0, n2b, ALU.add, ALU.mult))
            link(dve.scalar_tensor_tensor(sc2_dec[0:ND, :], mod[0:ND, 4 * D:5 * D], 1.0, n2b[0:ND, :], ALU.add, ALU.mult))
            dve.wait_ge(ld_x, 2 * 16 * NTILE)
            dve.wait_ge(ld_router, 64)

            def norm_rows(i, col, n_ssq, n_root):
                n = rows(i)
                dve.wait_ge(ssq_ready, n_ssq)
                link(dve.tensor_scalar(sums[0:n, 1, col:col + 1], sums[0:n, 0, col:col + 1], 1.0 / D, EPS, ALU.mult, ALU.add), ms_ready, n_root)
                rsqrt(sums[0:n, 1, col:col + 1], sums[0:n, 2, col:col + 1], sums[0:n, 3, col:col + 1], sums[0:n, 2, col:col + 1], n_root)
                return sums[0:n, 3, col:col + 1]

            def logit_tile(i):
                n = rows(i)
                dve.wait_ge(logit_done, i + 1)
                dve.tensor_tensor(logits[0:n, i, :], ps[0:n, 6, 0:NR], rbias[0:n, :], ALU.add).then_inc(logits_ready, 1)

            for i in range(NTILE):
                n = rows(i)
                prompt = i < NP // P
                dve.wait_ge(wo_done, i + 1)
                if i:
                    dve.wait_ge(x1_ready, i)
                g1 = bvec[0:n, G1, :] if prompt else mod[0:ND, 2 * D:3 * D]
                dve.tensor_tensor(split(t_row[0:n, :]), ps[0:n, 2 * (i % 2):2 * (i % 2) + 2, :], split(g1), ALU.mult).then_inc(t_ready, 1)
                r = norm_rows(i, i, NTILE + i + 1, 3 + i)
                if i >= 2:
                    dve.wait_ge(h2T_done, i - 1)
                    dve.wait_ge(h2_stored[i % 2], 16 * (i // 2))
                sc2 = bvec[0:n, SC2, :] if prompt else sc2_dec[0:ND, :]
                dve.scalar_tensor_tensor(h2[0:n, i % 2, :], x1[0:n, i, :], r, sc2, ALU.mult, ALU.mult).then_inc(h2_scaled, 1)
                if i:
                    logit_tile(i - 1)
            logit_tile(NTILE - 1)
            dve.wait_ge(logits_ready, NTILE)

            T5 = [P, NTILE, 4]

            def first_of(eq, rank_tmp, out):
                link(dve.tensor_tensor(rank_tmp, eq, rank4[:, None, :].broadcast_to(T5), ALU.mult))
                link(dve.tensor_reduce(col1[:, :, 0], rank_tmp, AX.X, ALU.max))
                link(dve.tensor_tensor(out, rank_tmp, col1[:, :, 0:1].broadcast_to(T5), ALU.is_equal))

            glog, elog = logits[:, :, 0:NG], logits[:, :, NG:NR]
            link(dve.tensor_reduce(col1[:, :, 0], glog, AX.X, ALU.max))
            link(dve.tensor_tensor(gdiff, glog, col1[:, :, 0:1].broadcast_to(T5), ALU.subtract), diff_ready, 1)
            link(dve.tensor_scalar(eq4, gdiff, 0.0, None, ALU.is_equal))
            first_of(eq4, tmp4, gone)
            link(dve.tensor_tensor(gone, gone, valid[:, :, None].broadcast_to(T5), ALU.mult))
            e44 = elog.rearrange("p t (g j) -> p t g j", g=NG)
            w44 = work16.rearrange("p t (g j) -> p t g j", g=NG)
            link(dve.tensor_tensor(w44, e44, gone[:, :, :, None].broadcast_to([P, NTILE, NG, EG]), ALU.mult))
            link(dve.tensor_reduce(sel, work16.rearrange("p t (g j) -> p t j g", g=NG), AX.X, ALU.add))
            link(dve.tensor_reduce(col1[:, :, 1], sel, AX.X, ALU.max))
            link(dve.tensor_tensor(sel, sel, col1[:, :, 1:2].broadcast_to(T5), ALU.subtract))
            link(dve.tensor_scalar(eq4, sel, 0.0, None, ALU.is_equal))
            first_of(eq4, tmp4, one_a)
            link(dve.scalar_tensor_tensor(sel, one_a, -1.0e30, sel, ALU.mult, ALU.add))
            link(dve.tensor_reduce(col1[:, :, 2], sel, AX.X, ALU.max), diff_ready, 2)
            link(dve.tensor_tensor(eq4, sel, col1[:, :, 2:3].broadcast_to(T5), ALU.is_equal))
            first_of(eq4, tmp4, one_b)
            for one, oh in ((one_a, onehot[:, 0]), (one_b, onehot[:, 1])):
                link(dve.tensor_tensor(oh.rearrange("p t (g j) -> p t g j", g=NG), gone[:, :, :, None].broadcast_to([P, NTILE, NG, EG]),
                                       one[:, :, None, :].broadcast_to([P, NTILE, NG, EG]), ALU.mult))
            dve.tensor_tensor(onehot_both[:, :, :], onehot[:, 0], onehot[:, 1], ALU.add).then_inc(onehot_ready, 1)
            dve.wait_ge(exp_ready, 2)
            link(dve.tensor_reduce(col1[:, :, 3], exp_out[0], AX.X, ALU.add))
            link(dve.tensor_scalar(col1[:, :, 4], col1[:, :, 5], 1.0, None, ALU.add))
            link(dve.tensor_tensor(col1[:, :, 4], col1[:, :, 4], col1[:, :, 3], ALU.mult))
            link(dve.reciprocal(share[:, 0, :], col1[:, :, 4]))
            link(dve.tensor_tensor(share[:, 1, :], share[:, 0, :], col1[:, :, 5], ALU.mult))

            dve.wait_ge(count_done, 1)
            link(dve.tensor_copy(count16, ps[:, 7, NTILE * NE:(NTILE + 1) * NE]))
            link(dve.tensor_scalar(tiles16, count16, float(P), 1.0, ALU.is_gt, ALU.add))
            for full in range(2, (NT + P - 1) // P):
                link(dve.scalar_tensor_tensor(tiles16, count16, float(full * P), tiles16, ALU.is_gt, ALU.add))
            src, dst = scan_a, scan_b
            link(dve.tensor_copy(src, tiles16))
            for s in (1, 2, 4, 8):
                dve.tensor_copy(dst[:, 0:s], src[:, 0:s])
                link(dve.tensor_tensor(dst[:, s:NE], src[:, s:NE], src[:, 0:NE - s], ALU.add))
                src, dst = dst, src
            ends = src
            link(dve.tensor_tensor(dst, ends, tiles16, ALU.subtract))
            link(dve.tensor_scalar(dst, dst, float(P), None, ALU.mult))
            link(dve.tensor_tensor(slotbase, ps[:, 7, 0:NTILE * NE].rearrange("p (t e) -> p t e", e=NE),
                                   dst[:, None, :].broadcast_to([P, NTILE, NE]), ALU.add))
            for k in range(2):
                link(dve.tensor_tensor(work16, onehot[:, k], slotbase, ALU.mult))
                link(dve.tensor_reduce(slot_f[:, k, :], work16, AX.X, ALU.add))
            dve.tensor_copy(slot_i[:, :, :], slot_f).then_inc(slots_ready, 1)
            link(dve.tensor_copy(tile_f, tile_no[:, :]))
            link(dve.tensor_tensor(cmp, ends[:, None, :].broadcast_to([P, MAX_TILES, NE]), tile_f[:, :, None].broadcast_to([P, MAX_TILES, NE]), ALU.is_le))
            link(dve.tensor_reduce(tile_f, cmp, AX.X, ALU.add))
            dve.tensor_copy(table[:, 1:MAX_TILES + 1], tile_f).then_inc(table_ready, 1)
            dve.tensor_scalar(table[:, MAX_TILES + 1:MAX_TILES + 2], ends[:, NE - 1:NE], -1.0, None, ALU.add).then_inc(table_ready, 1)
            dve.tensor_copy(table[:, 0:1], ends[:, NE - 1:NE]).then_inc(table_ready, 1)

            def product_tile(j, first):
                dve.wait_ge(w_used[1], 4 * j + 4)
                dve.wait_ge(silu_ready, j + 1)
                if not first:
                    dve.wait_ge(actT_done, j)
                dve.tensor_tensor(act_t, ps[:, 1, :], silu_t, ALU.mult).then_inc(act_ready, 1)

            def turned_rows_out(j):
                dve.wait_ge(xgT_done, j + 1)
                dve.tensor_copy(xgT[:, 4:8, :], ps[:, 3, :].rearrange("p (k t) -> p k t", k=4)).then_inc(xgT_dve, 1)

            def y_out(jn, jm, first):
                dve.wait_ge(w_used[2], KF * jn)
                if not first:
                    dve.wait_ge(y_stored, 16 * jm)
                dve.tensor_copy(y_t[:, COLS:D], ps[:, 5, :]).then_inc(y_dve, 1)

            dve.wait_ge(table_ready, 3)
            n_tiles = dve.value_load(table[0:1, 0:1], min_val=NE, max_val=MAX_TILES)
            last = dve.value_load(table[0:1, MAX_TILES + 1:MAX_TILES + 2], min_val=NE - 1, max_val=MAX_TILES - 1)
            turned_rows_out(0)
            for j in range(2):
                product_tile(j, j == 0)
                turned_rows_out(j + 1)
                if j:
                    y_out(j, j - 1, True)
            with dve.Fori(2, n_tiles) as j:
                product_tile(j, False)
                turned_rows_out(j + 1)
                y_out(j, j - 1, False)
            y_out(n_tiles, last, False)

            for i in range(NTILE):
                n = rows(i)
                prompt = i < NP // P
                for k in range(2):
                    dve.wait_ge(yg_ready[k], 16 * (i + 1))
                link(dve.tensor_scalar(t_row[0:n, :], yg[0:n, 0, :], share[0:n, 0, i:i + 1], None, ALU.mult))
                link(dve.scalar_tensor_tensor(t_row[0:n, :], yg[0:n, 1, :], share[0:n, 1, i:i + 1], t_row[0:n, :], ALU.mult, ALU.add), yg_used, i + 1)
                g2 = bvec[0:n, G2, :] if prompt else mod[0:ND, 5 * D:6 * D]
                link(dve.tensor_tensor(t_row[0:n, :], t_row[0:n, :], g2, ALU.mult))
                link(dve.tensor_tensor(x1[0:n, i, :], x1[0:n, i, :], t_row[0:n, :], ALU.add), x2_ready, i + 1)
                r = norm_rows(i, NTILE + i, 2 * NTILE + i + 1, 3 + NTILE + i)
                dve.scalar_tensor_tensor(x1[0:n, i, :], x1[0:n, i, :], r, bvec[0:n, FG, :], ALU.mult, ALU.mult).then_inc(out_ready, 1)


_INS = ['x_prompt', 'x_sample', 'state_conf', 'state_pool', 'state_sconv', 'c_prompt', 'c_sample', 'w_ada', 'b_ada',
        'norm1_g', 'norm2_g', 'final_g', 'w_in', 'conf_dw', 'conf_dw_b', 'conf_ln_g', 'conf_ln_b', 'conf_pw',
        'pool_w', 'pool_scale', 'sc_dw', 'sc_out', 'w_o', 'router_g', 'router_g_b', 'router_e', 'router_e_b',
        'exp_w1', 'exp_w3', 'exp_w2']
_OUTS = [(1, NP, D), (ND, 1, D), (1, 1, CK - 1, W), (1, ND, CK - 1, W), (1, 1, PB, W), (1, ND, PB, W),
         (1, 1, SK - 1, W), (1, ND, SK - 1, W)]


def kernel(**inputs):
    import concourse.bacc as bacc
    from concourse.bass_utils import run_bass_kernel_spmd

    nc = bacc.Bacc("TRN2", target_bir_lowering=False, num_devices=1)
    arrays, args = {}, []
    for name in _INS:
        a = np.ascontiguousarray(inputs[name])
        arrays[f"in_{name}_dram"] = a
        args.append(nc.dram_tensor(f"in_{name}_dram", a.shape, mybir.dt.from_np(a.dtype), kind="ExternalInput").ap())
    for i, shape in enumerate(_OUTS):
        args.append(nc.dram_tensor(f"out_{i}_dram", shape, F32, kind="ExternalOutput").ap())
    trunk_step(nc, *args)
    r = run_bass_kernel_spmd(nc, [arrays], core_ids=[0])
    return tuple(r.results[0][f"out_{i}_dram"] for i in range(len(_OUTS)))
```

```python
from contextlib import ExitStack

import numpy as np

import concourse.bass as bass
from concourse import mybir

ALU = mybir.AluOpType
ACT = mybir.ActivationFunctionType
AX = mybir.AxisListType
F32 = mybir.dt.float32
F32R = mybir.dt.float32r
BF16 = mybir.dt.bfloat16
I32 = mybir.dt.int32

P = 128
D = 1024
KD = D // P
NP = 512
ND = 8
NT = NP + ND
HT = NT // 2
NTILE = NP // P + 1
W = D // 2
KW = W // P
CK = 31
SK = 3
WINDOWS = (2, 4, 8, 16)
PB = 15
DIN = 6 * W + 3 * D
NG = 4
EG = 4
NE = NG * EG
FF = D // 2
KF = FF // P
EPS = 1e-6
COLS = 512
G_ADA = 6 * D // COLS
G_IN = DIN // COLS
RAW = 6
SPLIT = 4
QUARTER = 1024
TURN = 12
N_IN = 4 * G_ADA
N_MIX = N_IN + 4 * G_IN
N_WO = N_MIX + 9
N_EXP = N_WO + 8
MAX_TILES = NE + 2 * NT // P
NR = NG + NE
Q_PARAMS = 11
Q_NORM = 13
Q_SCALE = 20
Q_TURN = Q_SCALE + 2
AHEAD = 4

R_TAPS, R_STAPS, R_CB, R_LG, R_LB, R_N1, R_PS = 0, 31, 34, 35, 36, 37, 39
N_PARAM = 41

def trunk_step(nc, x_prompt, x_sample, state_conf, state_pool, state_sconv, c_prompt, c_sample, w_ada,
               b_ada, norm1_g, norm2_g, final_g, w_in, conf_dw, conf_dw_b, conf_ln_g, conf_ln_b, conf_pw,
               pool_w, pool_scale, sc_dw, sc_out, w_o, router_g, router_g_b, router_e, router_e_b, exp_w1,
               exp_w3, exp_w2, y_prompt, y_sample, conf_p, conf_s, pool_p, pool_s, sconv_p, sconv_s):
    mod_dram = nc.dram_tensor("mod_rows", [ND + 1, 4 * D], F32, kind="Internal").ap()
    h2_dram = nc.dram_tensor("h2_rows", [NT, D], F32, kind="Internal").ap()
    slot_dram = nc.dram_tensor("slot_tokens", [MAX_TILES * P, 1], I32, kind="Internal").ap()
    y_dram = nc.dram_tensor("expert_rows", [MAX_TILES * P, D], F32, kind="Internal").ap()

    ctx = ExitStack()
    with ctx:
        def sb(name, shape, dt=F32):
            return ctx.enter_context(nc.sbuf_tensor(name, shape, dt))

        def sem(name):
            return ctx.enter_context(nc.semaphore(name))

        raw = sb("raw", [P, RAW, QUARTER])
        w_hi = sb("w_hi", [P, SPLIT, QUARTER], F32R)
        w_lo = sb("w_lo", [P, SPLIT, QUARTER], F32R)
        hT_hi = sb("hT_hi", [P, KD, NT], F32R)
        hT_lo = sb("hT_lo", [P, KD, NT], F32R)
        region_a = sb("region_a", [P, 3 * KD * NT])
        region_b = sb("region_b", [P, 13500])
        pT = sb("pT", [P, KW, N_PARAM])
        confT = sb("confT", [P, KW, ND, CK - 1])
        poolT = sb("poolT", [P, KW, ND, PB])
        sconvT = sb("sconvT", [P, KW, ND, SK - 1])
        cT_hi = sb("cT_hi", [P, KD, 16], F32R)
        cT_lo = sb("cT_lo", [P, KD, 16], F32R)
        scaleT = sb("scaleT", [P, KD, ND + 1])
        shiftT = sb("shiftT", [P, KD, ND + 1])
        ident = sb("ident", [P, P])
        onesK = sb("onesK", [P, P])
        before = sb("before", [P, P], BF16)
        ones16 = sb("ones16", [P, P], BF16)
        sums = sb("sums", [P, 4, 2 * NTILE])
        wrouter = sb("wrouter", [P, KD, NR])
        rbias = sb("rbias", [P, NR])
        small = sb("small", [P, 128])
        onehot_both = sb("onehot_both", [P, NTILE, NE], BF16)
        tok_id = sb("tok_id", [P, NTILE], I32)
        tile_no = sb("tile_no", [P, MAX_TILES], I32)
        slot_i = sb("slot_i", [P, 2, NTILE], I32)
        table = sb("table", [P, MAX_TILES + 3], I32)
        slot_idx = sb("slot_idx", [P, 1], I32)
        zslot = sb("zslot", [P, MAX_TILES], I32)
        ps = ctx.enter_context(nc.psum_tensor("ps", [P, 8, 512], F32))

        def carve(region, at, *dims):
            n = int(np.prod(dims))
            v = region[:, at:at + n]
            if len(dims) == 2:
                return v.rearrange("p (a b) -> p a b", b=dims[1])
            if len(dims) == 3:
                return v.rearrange("p (a b c) -> p a b c", b=dims[1], c=dims[2])
            return v

        def slot(ring, s, k):
            return ring[:, s, :].rearrange("p (k n) -> p k n", k=k)

        def split_slot(n):
            return (n - (N_WO - N_MIX) * (n >= N_WO)) % SPLIT

        def splits(n):
            return n + 1 - (N_WO - N_MIX) * (n >= N_WO)

        x_in = carve(region_a, 0, NTILE, D)
        conf_raw = carve(region_a, 5120, 2, W)
        pool_raw = carve(region_a, 6144, W)
        sconv_raw = carve(region_a, 6656, W)
        c_raw = carve(region_a, 7168, D)
        square_junk = carve(region_a, 8192, D)
        params = carve(region_a, 9216, W)[0:N_PARAM]
        zeros = square_junk
        gates = carve(region_a, 0, 3 * KD, NT)
        x1 = carve(region_a, 0, NTILE, D)
        bvec = carve(region_a, 5120, 5, D)
        G1, SH2, SC2, G2, FG = range(5)
        sc2_dec = carve(region_a, 10240, D)
        n2b = carve(region_a, 11264, D)
        mod = region_b[0:ND + 1, 0:6 * D]
        UA, UB, UC = CK - 1 + NT, PB + NT, SK - 1 + NT
        ua = carve(region_b, 0, KW, UA)
        va = carve(region_b, 2200, KW, NT)
        ub = carve(region_b, 4280, KW, UB)
        pooled = carve(region_b, 6420, KW, NT)
        uc = carve(region_b, 8500, KW, UC)
        sbr = carve(region_b, 10588, KW, NT)
        squares = carve(region_b, 0, KW, NT)
        rstdT = carve(region_b, 4280, NT)
        tail = carve(region_b, 8500, 3, W)[0:40]
        h2 = carve(region_b, 0, 2, D)
        h2T = carve(region_b, 2048, KD, P)
        t_row = carve(region_b, 3072, D)
        sq_row = carve(region_b, 4096, D)
        xg = carve(region_b, 5120, D)
        silu_t = carve(region_b, 7168, FF)
        act_t = carve(region_b, 7680, FF)
        y_t = carve(region_b, 8192, D)
        g1_dec = carve(region_b, 9216, D)
        sh2_dec = carve(region_b, 10240, D)
        g2_dec = carve(region_b, 11264, D)
        yg = [carve(region_b, at, 2, D) for at in (9216, 0, 5120, 7168)]
        xgT_hi, xgT_lo = (t[:, :, 0:P] for t in (hT_hi, hT_lo))
        actT_hi, actT_lo = (t[:, 0:KF, P:2 * P] for t in (hT_hi, hT_lo))
        tmp_a = sb("tmp_a", [P, UB])
        tmp_b = sb("tmp_b", [P, UB])
        sig = pooled[:, 2:4, :]
        rcount = sb("rcount", [P, 16])

        ld_c = sem("ld_c")
        ld_x = sem("ld_x")
        ld_rows = sem("ld_rows")
        ld_mod = sem("ld_mod")
        ld_router = sem("ld_router")
        ld_bcast = sem("ld_bcast")
        const_ready = sem("const_ready")
        sums_ready = sem("sums_ready")
        conv_step = sem("conv_step")
        pool_chain = sem("pool_chain")
        silu_c_ready = sem("silu_c_ready")
        turned = sem("turned")
        turned_out = sem("turned_out")
        raw_ready = [sem(f"raw_ready{s}") for s in range(RAW)]
        hi_done = sem("hi_done")
        lo_done = sem("lo_done")
        quarter_used = sem("quarter_used")
        cT_split = sem("cT_split")
        mod_stored = sem("mod_stored")
        hT_raw = sem("hT_raw")
        hT_hi_done = sem("hT_hi_done")
        hT_lo_done = sem("hT_lo_done")
        ld_dec = sem("ld_dec")
        m_hi_done = sem("m_hi_done")
        m_lo_done = sem("m_lo_done")
        xgT_hi_done = sem("xgT_hi_done")
        xgT_lo_done = sem("xgT_lo_done")
        actT_hi_done = sem("actT_hi_done")
        actT_lo_done = sem("actT_lo_done")
        ada_done = sem("ada_done")
        mod_ready = sem("mod_ready")
        modT_done = sem("modT_done")
        scaleT_ready = sem("scaleT_ready")
        ssq_ready = sem("ssq_ready")
        root_ready = sem("root_ready")
        ms_ready = sem("ms_ready")
        xn_ready = sem("xn_ready")
        xT_done = sem("xT_done")
        z_done = sem("z_done")
        set_free = [sem(f"set_free{m}") for m in range(4)]
        z_dve = sem("z_dve")
        pads_ready = sem("pads_ready")
        conv_ready = sem("conv_ready")
        sq_ready = sem("sq_ready")
        centred = sem("centred")
        branch_b = sem("branch_b")
        branch_c = sem("branch_c")
        normed = sem("normed")
        branch_a = sem("branch_a")
        mix_done = sem("mix_done")
        tail_ready = sem("tail_ready")
        merged = sem("merged")
        wo_done = sem("wo_done")
        t_ready = sem("t_ready")
        x1_ready = sem("x1_ready")
        h2_ready = sem("h2_ready")
        h2_stored = [sem(f"h2_stored{i}") for i in range(2)]
        h2T_done = sem("h2T_done")
        h2T_ready = sem("h2T_ready")
        logit_done = sem("logit_done")
        logits_ready = sem("logits_ready")
        diff_ready = sem("diff_ready")
        exp_ready = sem("exp_ready")
        onehot_ready = sem("onehot_ready")
        count_done = sem("count_done")
        slots_ready = sem("slots_ready")
        table_ready = sem("table_ready")
        slots_zeroed = sem("slots_zeroed")
        slots_stored = sem("slots_stored")
        slot_idx_ready = sem("slot_idx_ready")
        xg_ready = sem("xg_ready")
        gather_free = sem("gather_free")
        xgT_done = sem("xgT_done")
        silu_ready = sem("silu_ready")
        act_ready = sem("act_ready")
        actT_done = sem("actT_done")
        y_act = sem("y_act")
        y_dve = sem("y_dve")
        y_stored = sem("y_stored")
        y_zeroed = sem("y_zeroed")
        yg_ready = [[sem(f"yg_ready{b}_{k}") for k in range(2)] for b in range(4)]
        yg_scaled = sem("yg_scaled")
        moe_ready = sem("moe_ready")
        share_ready = sem("share_ready")
        x2_ready = sem("x2_ready")
        out_ready = sem("out_ready")
        out_stored = sem("out_stored")
        dve_step = sem("dve_step")
        act_step = sem("act_step")

        route_at = [12288]

        def routing(*dims):
            route_at[0] += int(np.prod(dims))
            return carve(region_b, route_at[0] - int(np.prod(dims)), *dims)

        logits = routing(NTILE, NR)
        rank4 = routing(4)
        valid = routing(NTILE)
        gdiff, eq4, tmp4, gone, sel, one_a, one_b, exp_g = (routing(NTILE, 4) for _ in range(8))
        col1 = routing(NTILE, 6)
        work16 = routing(NTILE, NE)
        slotbase = routing(NTILE, NE)
        share = routing(2, NTILE)
        slot_f = routing(2, NTILE)
        count16, tiles16, scan_a, scan_b = (routing(NE) for _ in range(4))
        tile_f = routing(MAX_TILES)
        cmp = routing(MAX_TILES, NE)
        onehot = routing(2, NTILE, NE)
        exp_in = (gdiff, col1[:, :, 2])
        exp_out = (exp_g, col1[:, :, 5])

        def rows(i):
            return P if i < NP // P else ND

        def halves(m):
            return ps[:, 2 * m:2 * m + 2, 0:HT]

        def split(ap):
            return ap.rearrange("p (h t) -> p h t", h=2)

        def z_complete(g, m):
            return (z_done, 3 * g + m + 1) if m < 3 else (quarter_used, N_IN + 4 * g + 4)

        row_loads = [
            (params[R_TAPS:R_TAPS + CK, :], conf_dw[0]),
            (params[R_STAPS:R_STAPS + SK, :], sc_dw[0]),
            (params[R_CB:R_CB + 1, :], conf_dw_b),
            (params[R_LG:R_LG + 1, :], conf_ln_g),
            (params[R_LB:R_LB + 1, :], conf_ln_b),
            (params[R_N1:R_N1 + 2, :], norm1_g.rearrange("a (h c) -> (a h) c", h=2)),
            (params[R_PS:R_PS + 2, :], pool_scale.rearrange("a (h c) -> (a h) c", h=2)),
            (conf_raw[0:120, 0, :], state_conf[0, 0:4].rearrange("s r c -> (s r) c")),
            (conf_raw[0:120, 1, :], state_conf[0, 4:8].rearrange("s r c -> (s r) c")),
            (pool_raw[0:120, :], state_pool[0].rearrange("s r c -> (s r) c")),
            (sconv_raw[0:16, :], state_sconv[0].rearrange("s r c -> (s r) c")),
        ]

        block = ctx.enter_context(nc.Block())

        @block.sync
        def _(sp):
            ada_v = w_ada[0].rearrange("(k p) n -> p k n", p=P)
            in_v = w_in[0].rearrange("(k p) n -> p k n", p=P)
            wo_v = w_o[0].rearrange("(k p) n -> p k n", p=P)

            sp.dma_start(c_raw[0:ND, :], c_sample).then_inc(ld_c, 16)
            sp.dma_start(c_raw[ND:ND + 1, :], c_prompt).then_inc(ld_c, 16)

            def load(n, k, src):
                sp.dma_start(slot(raw, n % RAW, k), src).then_inc(raw_ready[n % RAW], 16)

            def column_group(view, first_n, i):
                for q in range(TURN):
                    sp.wait_ge(hi_done, TURN * i + (first_n + q - RAW + 1))
                    sp.wait_ge(lo_done, TURN * i + (first_n + q - RAW + 1))
                    g, k = q // 4, 2 * (q % 4)
                    load(first_n + q, 2, view[:, k:k + 2, bass.ds(i * (3 * COLS) + g * COLS, COLS)])

            for n in range(TURN):
                if n == RAW:
                    sp.dma_start(mod, b_ada[0].partition_broadcast(ND + 1)).then_inc(ld_mod, 16)
                    for dst, src in row_loads:
                        sp.dma_start(dst, src).then_inc(ld_rows, 16)
                    for i in range(NP // P):
                        sp.dma_start(x_in[:, i, :], x_prompt[0, i * P:(i + 1) * P, :]).then_inc(ld_x, 16)
                    sp.dma_start(x_in[0:ND, 4, :], x_sample.rearrange("b t d -> (b t) d")).then_inc(ld_x, 16)
                if n >= RAW:
                    sp.wait_ge(hi_done, n - RAW + 1)
                    sp.wait_ge(lo_done, n - RAW + 1)
                k = 2 * (n % 4)
                load(n, 2, ada_v[:, k:k + 2, n // 4 * COLS:(n // 4 + 1) * COLS])
            with sp.Fori(1, G_ADA // 3) as i:
                column_group(ada_v, 0, i)
            with sp.Fori(0, G_IN // 3) as i:
                column_group(in_v, N_IN, i)

            def free(n):
                if N_MIX <= n - RAW < N_WO:
                    sp.wait_ge(mix_done, 11 if n - RAW == N_MIX else 12 + 2 * (n - RAW - N_MIX))
                else:
                    sp.wait_ge(hi_done, splits(n - RAW))
                    sp.wait_ge(lo_done, splits(n - RAW))

            free(N_MIX)
            load(N_MIX, 4, pool_w[0].rearrange("g p n -> p g n"))
            for b, w in enumerate((sc_out, conf_pw)):
                for q in range(4):
                    n = N_MIX + 1 + 4 * b + q
                    free(n)
                    load(n, KW, w[0].rearrange("(k p) n -> p k n", p=P)[:, :, q * 256:(q + 1) * 256])
            for h in range(2):
                for q in range(4):
                    n = N_WO + 4 * h + q
                    free(n)
                    load(n, 2, wo_v[:, 2 * q:2 * q + 2, h * COLS:(h + 1) * COLS])

            def up_weights(c, wx, e, j):
                for q in range(4):
                    if j is not None:
                        sp.wait_ge(hi_done, TURN * j + splits(N_EXP + c + q - RAW))
                        sp.wait_ge(lo_done, TURN * j + splits(N_EXP + c + q - RAW))
                    else:
                        free(N_EXP + c + q)
                    load(N_EXP + c + q, 2, wx[0, bass.ds(e, 1), 2 * q * P:(2 * q + 2) * P, :].rearrange("a (k p) n -> p (a k) n", p=P))

            def down_weights(c, e, j):
                for q in range(KF):
                    sp.wait_ge(hi_done, TURN * j + splits(N_EXP + c + q - RAW))
                    sp.wait_ge(lo_done, TURN * j + splits(N_EXP + c + q - RAW))
                    load(N_EXP + c + q, 1, exp_w2[0, bass.ds(e, 1), q * P:(q + 1) * P, :].rearrange("a p n -> p a n"))

            def expert_of(at):
                return sp.value_load(table[0:1, at], min_val=0, max_val=NE - 1)

            up_weights(0, exp_w1, 0, None)
            up_weights(4, exp_w3, 0, None)
            sp.wait_ge(table_ready, 4)
            last = sp.value_load(table[0:1, MAX_TILES + 1:MAX_TILES + 2], min_val=NE - 1, max_val=MAX_TILES - 1)
            up_weights(8, exp_w1, expert_of(slice(2, 3)), None)
            with sp.Fori(1, last) as j:
                up_weights(0, exp_w3, expert_of(bass.ds(j + 1, 1)), j)
                down_weights(4, expert_of(bass.ds(j, 1)), j)
                up_weights(8, exp_w1, expert_of(bass.ds(j + 2, 1)), j)
            up_weights(0, exp_w3, expert_of(bass.ds(last + 1, 1)), last)
            down_weights(4, expert_of(bass.ds(last, 1)), last)
            down_weights(8, expert_of(bass.ds(last + 1, 1)), last)

        @block.tensor
        def _(pe):
            def three(out, pairs, moving, start, stop):
                pe.matmul(out, pairs[0], moving[0], start=start, stop=False)
                pe.matmul(out, pairs[0], moving[1], start=False, stop=False)
                return pe.matmul(out, pairs[1], moving[0], start=False, stop=stop)

            def split_weights(n, k):
                return slot(w_hi, split_slot(n), k), slot(w_lo, split_slot(n), k)

            pe.wait_ge(const_ready, 2)
            pe.wait_ge(silu_c_ready, 1)
            for k in range(KD):
                t = pe.transpose(ps[:, 0, 9 * k:9 * k + 9], c_raw[0:ND + 1, k * P:(k + 1) * P], ident[0:ND + 1, 0:ND + 1])
            t.then_inc(turned, 1)

            pe.wait_ge(cT_split, 2)
            for n in range(N_IN):
                g, q = n // 4, n % 4
                pe.wait_ge(lo_done, n + 1)
                if q == 0 and g >= 3:
                    pe.wait_ge(mod_ready, g - 2)
                hi, lo = split_weights(n, 2)
                for k in range(2):
                    x = (cT_hi[:, 2 * q + k, :], cT_lo[:, 2 * q + k, :])
                    m = three(ps[0:16, 5 + g % 3, :], x, (hi[:, k, :], lo[:, k, :]), q == 0 and k == 0, q == 3 and k == 1)
                m.then_inc(quarter_used, 1)
                if n == Q_PARAMS:
                    pe.wait_ge(ld_rows, 16 * len(row_loads))
                    for c in range(KW):
                        cs = slice(c * P, (c + 1) * P)
                        pe.transpose(ps[:, 1, c * N_PARAM:(c + 1) * N_PARAM], params[:, cs], ident[0:N_PARAM, 0:N_PARAM])
                        pe.transpose(ps[:, 1, 256 + 16 * c:272 + 16 * c], sconv_raw[0:16, cs], ident[0:16, 0:16])
                        for h in range(2):
                            o = 240 * (c % 2) + 120 * h
                            pe.transpose(ps[:, 2 + c // 2, o:o + 120], conf_raw[0:120, h, cs], ident[0:120, 0:120])
                        t = pe.transpose(ps[:, 4, 120 * c:120 * c + 120], pool_raw[0:120, cs], ident[0:120, 0:120])
                    t.then_inc(turned, 1)
                elif n == Q_SCALE:
                    pe.wait_ge(mod_ready, 4)
                    pe.wait_ge(turned_out, 4)
                    for k in range(2 * KD):
                        t = pe.transpose(ps[:, 0, 9 * k:9 * k + 9], mod[:, k * P:(k + 1) * P], ident[0:ND + 1, 0:ND + 1])
                    t.then_inc(modT_done, 1)
                elif n == Q_SCALE + 1:
                    pe.wait_ge(xn_ready, NTILE)
                    for k in range(KD):
                        t = pe.transpose(ps[:, 1, 8 * k:8 * k + 8], x_in[0:ND, 4, k * P:(k + 1) * P], ident[0:ND, 0:ND])
                    t.then_inc(xT_done, 1)
                elif Q_TURN <= n < Q_TURN + KD:
                    k = n - Q_TURN
                    if k >= 3:
                        pe.wait_ge(hT_raw, max(1, k - 3))
                    for i in range(NP // P):
                        t = pe.transpose(ps[:, (2 + k) % 5, i * P:(i + 1) * P], x_in[:, i, k * P:(k + 1) * P], ident[:, :])
                    t.then_inc(xT_done, 1)

            pe.wait_ge(hT_lo_done, KD + 1)
            with pe.Fori(0, G_IN // 3) as i:
                for n in range(TURN):
                    g, q = n // 4, n % 4
                    pe.wait_ge(lo_done, TURN * i + splits(N_IN + n))
                    hi, lo = split_weights(N_IN + n, 2)
                    for m in range(4):
                        ms = slice(m * P, (m + 1) * P)
                        if q == 0:
                            pe.wait_ge(set_free[m], 3 * i + g)
                            if m >= 2 and g == 0:
                                pe.wait_ge(mod_ready, G_ADA + m - 3)
                        for k in range(2):
                            kk = 2 * q + k
                            first, final = kk == 0, kk == KD - 1
                            for w, x, start, stop in ((hi, hT_hi, first, False), (hi, hT_lo, False, False), (lo, hT_hi, False, final)):
                                for h in range(2):
                                    mm = pe.matmul(ps[:, 2 * m + h, 0:HT], w[:, k, ms], x[:, kk, h * HT:(h + 1) * HT], start=start, stop=stop)
                        if q == 3 and m < 3:
                            mm.then_inc(z_done, 1)
                    mm.then_inc(quarter_used, 1)

            unit = [0]

            def next_set():
                s = unit[0] % 4
                pe.wait_ge(set_free[s], G_IN + unit[0] // 4)
                unit[0] += 1
                return s

            def product(s, lhs, rhs, n):
                for k in range(n):
                    for h in range(2):
                        mm = pe.matmul(ps[:, 2 * s + h, 0:HT], lhs(k), rhs(k)[:, h * HT:(h + 1) * HT], start=(k == 0), stop=(k == n - 1))
                return mm.then_inc(mix_done, 1)

            def raw_weights(n, k):
                pe.wait_ge(raw_ready[n % RAW], 16 * (n // RAW + 1))
                return slot(raw, n % RAW, k)

            pe.wait_ge(conv_ready, 1)
            product(next_set(), lambda k: onesK[:, :], lambda k: va[:, k, :], KW)
            s = next_set()
            for c in range(KW):
                pe.transpose(ps[0:38, 2 * s, c * P:(c + 1) * P], ua[:, c, UA - 38:UA], ident[:, :])
                t = pe.transpose(ps[0:23, 2 * s + 1, c * P:(c + 1) * P], ub[:, c, UB - 23:UB], ident[:, :])
            t.then_inc(mix_done, 1)
            s = next_set()
            pe.wait_ge(branch_c, KW)
            for c in range(KW):
                t = pe.transpose(ps[0:10, 2 * s, c * P:(c + 1) * P], uc[:, c, UC - 10:UC], ident[:, :])
            t.then_inc(mix_done, 1)
            pe.wait_ge(branch_b, len(WINDOWS))
            w = raw_weights(N_MIX, 4)
            for j in range(KD):
                g = j // 2
                product(next_set(), lambda k: w[:, g, (j % 2) * P:(j % 2 + 1) * P], lambda k: pooled[:, g, :], 1)
            pe.wait_ge(sq_ready, 1)
            product(next_set(), lambda k: onesK[:, :], lambda k: squares[:, k, :], KW)
            for j in range(KD):
                if j % 2 == 0:
                    w = raw_weights(N_MIX + 1 + j // 2, KW)
                product(next_set(), lambda k: w[:, k, (j % 2) * P:(j % 2 + 1) * P], lambda k: sbr[:, k, :], KW)
            pe.wait_ge(branch_a, 1)
            for j in range(KD):
                if j % 2 == 0:
                    w = raw_weights(N_MIX + 5 + j // 2, KW)
                product(next_set(), lambda k: w[:, k, (j % 2) * P:(j % 2 + 1) * P], lambda k: va[:, k, :], KW)

            def w_o_part(out, i, kk, w, k):
                n = rows(i)
                hi, lo = w
                x = (hT_hi[:, kk, i * P:i * P + n], hT_lo[:, kk, i * P:i * P + n])
                return three(out, x, (hi[:, k, :], lo[:, k, :]), kk == 0, kk == KD - 1)

            for q in range(4):
                pe.wait_ge(lo_done, splits(N_WO + q))
                for k in range(2):
                    pe.wait_ge(m_lo_done, 2 * q + k + 1)
                    if q == k == 0:
                        for m in range(4):
                            pe.wait_ge(set_free[m], G_IN + 7)
                    for i in range(NTILE):
                        mm = w_o_part(ps[0:rows(i), i, :], i, 2 * q + k, split_weights(N_WO + q, 2), k)
                mm.then_inc(quarter_used, 1)

            def w_o_tile(i):
                if i >= 2:
                    pe.wait_ge(t_ready, i - 1)
                for q in range(4):
                    pe.wait_ge(lo_done, splits(N_WO + 4 + q))
                    for k in range(2):
                        mm = w_o_part(ps[0:rows(i), 5 + i % 2, :], i, 2 * q + k, split_weights(N_WO + 4 + q, 2), k)
                    if i == NTILE - 1:
                        mm.then_inc(quarter_used, 1)
                if i < NTILE - 1:
                    mm.then_inc(wo_done, 1)

            def router_tile(i):
                n = rows(i)
                pe.wait_ge(h2_ready, i + 1)
                if i >= 1:
                    pe.wait_ge(h2T_ready, i)
                for k in range(KD):
                    t = pe.transpose(ps[:, (i, 7)[k // 4], (k % 4) * P:(k % 4) * P + n], h2[0:n, i % 2, k * P:(k + 1) * P], ident[0:n, 0:n])
                t.then_inc(h2T_done, 1)
                pe.wait_ge(h2T_ready, i + 1)
                for k in range(KD):
                    mm = pe.matmul(ps[0:n, i, 0:NR], h2T[:, k, 0:n], wrouter[:, k, :], start=(k == 0), stop=(k == KD - 1))
                mm.then_inc(logit_done, 1)

            pe.wait_ge(ld_router, 64)
            for i in range(NTILE + 1):
                if i < NTILE:
                    w_o_tile(i)
                if i >= 1:
                    router_tile(i - 1)

            pe.wait_ge(onehot_ready, 1)
            oh = onehot_both
            for i in range(NTILE):
                for j in range(i + 1):
                    pe.matmul(ps[:, 7, i * NE:(i + 1) * NE], (before if j == i else ones16)[:, :], oh[:, j, :], start=(j == 0), stop=(j == i))
            for j in range(NTILE):
                mm = pe.matmul(ps[:, 7, NTILE * NE:(NTILE + 1) * NE], ones16[:, :], oh[:, j, :], start=(j == 0), stop=(j == NTILE - 1))
            mm.then_inc(count_done, 1)

            def turn_rows(j):
                pe.wait_ge(xg_ready, 16 * j + 16)
                for k in range(KD):
                    t = pe.transpose(ps[:, 2 + k // 4, (k % 4) * P:(k % 4 + 1) * P], xg[:, k * P:(k + 1) * P], ident[:, :])
                t.then_inc(xgT_done, 1)

            def up(c, j, bank):
                for q in range(4):
                    n = N_EXP + c + q
                    pe.wait_ge(lo_done, TURN * j + splits(n))
                    hi, lo = split_weights(n, 2)
                    for k in range(2):
                        kk = 2 * q + k
                        mm = three(ps[:, bank, :], (xgT_hi[:, kk, :], xgT_lo[:, kk, :]), (hi[:, k, :], lo[:, k, :]), kk == 0, kk == KD - 1)
                    mm.then_inc(quarter_used, 1)

            def down(c, j):
                for q in range(KF):
                    n = N_EXP + c + q
                    pe.wait_ge(lo_done, TURN * j + splits(n))
                    x = (actT_hi[:, q, :], actT_lo[:, q, :])
                    for h in range(2):
                        hs = slice(h * COLS, (h + 1) * COLS)
                        mm = three(ps[:, 4 + h, :], x, (w_hi[:, split_slot(n), hs], w_lo[:, split_slot(n), hs]), q == 0, q == KF - 1)
                    mm.then_inc(quarter_used, 1)

            def turn_product(j):
                pe.wait_ge(act_ready, j + 1)
                for k in range(KF):
                    t = pe.transpose(ps[:, 6, k * P:(k + 1) * P], act_t[:, k * P:(k + 1) * P], ident[:, :])
                t.then_inc(actT_done, 1)

            pe.wait_ge(table_ready, 4)
            last = pe.value_load(table[0:1, MAX_TILES + 1:MAX_TILES + 2], min_val=NE - 1, max_val=MAX_TILES - 1)
            before_last = pe.value_load(table[0:1, MAX_TILES + 2:MAX_TILES + 3], min_val=NE - 2, max_val=MAX_TILES - 2)
            turn_rows(0)
            pe.wait_ge(xgT_lo_done, 1)
            up(0, 0, 0)
            up(4, 0, 1)
            turn_rows(1)
            turn_product(0)
            pe.wait_ge(xgT_lo_done, 2)
            pe.wait_ge(silu_ready, 1)
            up(8, 0, 0)

            def w3_of(j):
                pe.wait_ge(act_ready, j)
                up(0, j, 1)

            def w2_of(c, turn, jn, y_before):
                pe.wait_ge(actT_lo_done, jn)
                pe.wait_ge(y_act, y_before)
                pe.wait_ge(y_dve, y_before)
                down(c, turn)

            with pe.Fori(1, last) as j:
                w3_of(j)
                turn_rows(j + 1)
                w2_of(4, j, j, j - 1)
                turn_product(j)
                pe.wait_ge(xgT_lo_done, j + 2)
                pe.wait_ge(silu_ready, j + 1)
                up(8, j, 0)
            w3_of(last)
            w2_of(4, last, last, before_last)
            turn_product(last)
            w2_of(8, last, last + 1, last)

        @block.scalar
        def _(act):
            steps = [0]

            def link(ins):
                steps[0] += 1
                ins.then_inc(act_step, 1)
                act.wait_ge(act_step, steps[0])

            def hi(n, turn=None):
                def at(value, step):
                    return value if turn is None else turn * step + value
                act.wait_ge(raw_ready[n % RAW], at(16 * (n // RAW + 1), 16 * (TURN // RAW)))
                if splits(n) > SPLIT or turn is not None:
                    act.wait_ge(quarter_used, at(splits(n) - SPLIT, TURN))
                act.activation(w_hi[:, split_slot(n), :], raw[:, n % RAW, :], ACT.Copy).then_inc(hi_done, 1)

            act.wait_ge(ld_c, 32)
            act.activation(c_raw[0:ND + 1, :], c_raw[0:ND + 1, :], ACT.Silu).then_inc(silu_c_ready, 1)
            act.wait_ge(turned_out, 1)
            act.activation(cT_hi[:, :, :], small[:, 0:16 * KD].rearrange("p (k s) -> p k s", k=KD), ACT.Copy).then_inc(cT_split, 1)
            for n in range(N_IN):
                hi(n)
                if Q_NORM <= n < Q_NORM + NTILE:
                    i = n - Q_NORM
                    if i == 0:
                        act.wait_ge(ld_x, 16 * NTILE)
                        act.wait_ge(sums_ready, 1)
                    else:
                        act.wait_ge(ssq_ready, i)
                    act.activation(square_junk[0:rows(i), :], x_in[0:rows(i), i, :], ACT.Square, accum_out=sums[0:rows(i), 0, i:i + 1]).then_inc(ssq_ready, 1)
                elif n == Q_NORM + NTILE + 2:
                    act.wait_ge(ms_ready, 1)
                    act.activation(sums[:, 2, 0:NTILE], sums[:, 1, 0:NTILE], ACT.Sqrt).then_inc(root_ready, 1)
                elif Q_TURN + AHEAD + 2 <= n <= Q_TURN + AHEAD + KD + 2:
                    k = n - (Q_TURN + AHEAD + 2)
                    act.wait_ge(hT_raw, k + 1)
                    if k == 0:
                        act.activation(hT_hi[:, :, NP:NT], small[:, 0:64].rearrange("p (k s) -> p k s", k=KD), ACT.Copy).then_inc(hT_hi_done, 1)
                    else:
                        act.activation(hT_hi[:, k - 1, 0:NP], (tmp_a, tmp_b)[(k - 1) % 2][:, 0:NP], ACT.Copy).then_inc(hT_hi_done, 1)
            for q in range(7):
                hi(N_IN + q)
                if q == 4:
                    act.wait_ge(mod_ready, G_ADA)
                    act.dma_start(mod_dram, mod[:, 2 * D:6 * D]).then_inc(mod_stored, 16)
            act.dma_start(wrouter[:, :, 0:NG], router_g[0].rearrange("(k p) n -> p k n", p=P)).then_inc(ld_router, 16)
            act.dma_start(wrouter[:, :, NG:NR], router_e[0].rearrange("(k p) n -> p k n", p=P)).then_inc(ld_router, 16)
            act.dma_start(rbias[:, 0:NG], router_g_b[0].partition_broadcast(P)).then_inc(ld_router, 16)
            act.dma_start(rbias[:, NG:NR], router_e_b[0].partition_broadcast(P)).then_inc(ld_router, 16)
            act.dma_start(conf_s[0, :, 0:CK - 2, :], state_conf[0, :, 1:CK - 1, :]).then_inc(out_stored, 16)
            act.dma_start(pool_s[0, :, 0:PB - 1, :], state_pool[0, :, 1:PB, :]).then_inc(out_stored, 16)
            act.dma_start(sconv_s[0, :, 0:SK - 2, :], state_sconv[0, :, 1:SK - 1, :]).then_inc(out_stored, 16)


            act.wait_ge(pads_ready, 1)
            for g in range(G_IN):
                if g == 9:
                    act.wait_ge(y_zeroed, 16 * (MAX_TILES - NE))
                for m in range(4):
                    if g == 5:
                        break
                    act.wait_ge(*z_complete(g, m))
                    if g == 0:
                        act.activation(split(ua[:, m, CK - 1:UA]), halves(m), ACT.Copy).then_inc(set_free[m], 1)
                    elif g == 1:
                        if m >= 2:
                            act.wait_ge(z_dve, m - 1)
                        act.activation(split(sig[:, m % 2, :]), halves(m), ACT.Sigmoid).then_inc(set_free[m], 1)
                    elif g == 2:
                        act.activation(split(ub[:, m, PB:UB]), halves(m), ACT.Copy).then_inc(set_free[m], 1)
                    elif g == 3:
                        act.activation(split(uc[:, m, SK - 1:UC]), halves(m), ACT.Copy).then_inc(set_free[m], 1)
                    elif g == 4:
                        act.activation(split(sbr[:, m, :]), halves(m), ACT.Copy).then_inc(set_free[m], 1)
                    else:
                        act.activation(split(gates[:, 4 * (g - 6) + m, :]), halves(m), ACT.Sigmoid).then_inc(set_free[m], 1)
                for q in range(4 * g + 7, min(4 * g + 11, 4 * G_IN)):
                    hi(N_IN + q)

            act.wait_ge(mix_done, 3)
            act.activation(tail[0:38, 0, :], ps[0:38, 2, :], ACT.Copy).then_inc(tail_ready, 1)
            act.activation(tail[0:23, 1, :], ps[0:23, 3, :], ACT.Copy).then_inc(set_free[1], 1)
            act.activation(tail[0:10, 2, :], ps[0:10, 4, :], ACT.Copy).then_inc(set_free[2], 1)
            act.wait_ge(tail_ready, 1)
            act.wait_ge(set_free[1], G_IN + 1)
            act.wait_ge(set_free[2], G_IN + 1)
            for n, (own, last, new_p, new_s) in enumerate(((CK - 1, CK - 2, conf_p, conf_s), (PB, PB - 1, pool_p, pool_s), (SK - 1, SK - 2, sconv_p, sconv_s))):
                act.dma_start(new_p[0, 0], tail[0:own, n, :]).then_inc(out_stored, 16)
                act.dma_start(new_s[0, :, last, :], tail[own:own + ND, n, :]).then_inc(out_stored, 16)
            act.wait_ge(centred, KW - 1)
            act.wait_ge(set_free[0], G_IN + 1)
            for c in range(KW):
                s = act.activation(squares[:, c, :], va[:, c, :], ACT.Square)
            s.then_inc(sq_ready, 1)
            act.wait_ge(ms_ready, 2)
            act.activation(tmp_b[:, 0:NT], tmp_a[:, 0:NT], ACT.Sqrt).then_inc(root_ready, 1)
            act.wait_ge(normed, KW)
            for c in range(KW):
                s = act.activation(va[:, c, :], va[:, c, :], ACT.Silu, bias=pT[:, c, R_LB:R_LB + 1], scale=pT[:, c, R_LG:R_LG + 1])
            s.then_inc(branch_a, 1)

            for q in range(2):
                hi(N_WO + q)
            for j in range(KD):
                act.wait_ge(merged, KD + j + 1)
                act.activation(hT_hi[:, j, :], gates[:, KD + j, :], ACT.Copy).then_inc(m_hi_done, 1)
                if j in (3, 5):
                    hi(N_WO + 2 + j // 5)
            act.wait_ge(m_lo_done, KD)
            act.wait_ge(mod_stored, 16)
            for n, dst in enumerate((G1, SH2, SC2, G2)):
                act.dma_start(bvec[:, dst, :], mod_dram[ND, n * D:(n + 1) * D].partition_broadcast(P)).then_inc(ld_bcast, 16)
            act.dma_start(n2b, norm2_g[0].partition_broadcast(P)).then_inc(ld_bcast, 16)
            act.dma_start(bvec[:, FG, :], final_g.partition_broadcast(P)).then_inc(ld_bcast, 16)
            act.wait_ge(out_stored, 16 * 9)
            for n, dst in enumerate((g1_dec, sh2_dec, sc2_dec, g2_dec)):
                act.dma_start(dst[0:ND, :], mod_dram[0:ND, n * D:(n + 1) * D]).then_inc(ld_dec, 16)
            for i in range(NP // P):
                act.dma_start(x1[:, i, :], x_prompt[0, i * P:(i + 1) * P, :]).then_inc(ld_x, 16)
            act.dma_start(x1[0:ND, 4, :], x_sample.rearrange("b t d -> (b t) d")).then_inc(ld_x, 16)
            for q in range(4, 8):
                hi(N_WO + q)
            for i in range(NTILE):
                n = rows(i)
                act.wait_ge(x1_ready, i + 1)
                act.activation(sq_row[0:n, :], x1[0:n, i, :], ACT.Square, accum_out=sums[0:n, 0, i:i + 1]).then_inc(ssq_ready, 1)
                act.wait_ge(ms_ready, 3 + i)
                act.activation(sums[0:n, 2, i:i + 1], sums[0:n, 1, i:i + 1], ACT.Sqrt).then_inc(root_ready, 1)
                act.wait_ge(h2_ready, i + 1)
                act.dma_start(h2_dram[i * P:i * P + n, :], h2[0:n, i % 2, :]).then_inc(h2_stored[i % 2], 16)
                act.wait_ge(h2T_done, i + 1)
                if i >= 1:
                    act.wait_ge(logit_done, i)
                for half, bank in ((0, i), (1, 7)):
                    out = act.activation(h2T[:, 4 * half:4 * half + 4, 0:n],
                                         ps[:, bank, :].rearrange("p (k t) -> p k t", k=4)[:, :, 0:n], ACT.Copy)
                out.then_inc(h2T_ready, 1)
            for n in range(2):
                act.wait_ge(diff_ready, n + 1)
                act.activation(exp_out[n], exp_in[n], ACT.Exp).then_inc(exp_ready, 1)

            def silu_tile(j):
                act.wait_ge(quarter_used, TURN * j + splits(N_EXP - 1))
                act.wait_ge(act_ready, j)
                act.activation(silu_t, ps[:, 0, :], ACT.Silu).then_inc(silu_ready, 1)

            def turned_rows_out(j):
                act.wait_ge(xgT_done, j + 1)
                act.activation(xgT_hi, ps[:, 2:4, :].rearrange("p b (k t) -> p (b k) t", k=4), ACT.Copy).then_inc(xgT_hi_done, 1)

            def y_out(jm, used):
                act.wait_ge(quarter_used, used)
                act.wait_ge(y_stored, jm * 16)
                act.activation(y_t[:, 0:COLS], ps[:, 4, :], ACT.Copy).then_inc(y_act, 1)

            def y_store(jn, jm):
                act.wait_ge(y_act, jn)
                act.wait_ge(y_dve, jn)
                act.dma_start(y_dram[bass.ds(jm * P, P), :], y_t).then_inc(y_stored, 16)

            def turned_product_out(j):
                act.wait_ge(actT_done, j + 1)
                act.activation(actT_hi, ps[:, 6, :].rearrange("p (k t) -> p k t", k=KF), ACT.Copy).then_inc(actT_hi_done, 1)

            def his(first, end, j=None):
                for c in range(first, end):
                    hi(N_EXP + c, j)

            his(0, 4)
            act.wait_ge(table_ready, 4)
            last = act.value_load(table[0:1, MAX_TILES + 1:MAX_TILES + 2], min_val=NE - 1, max_val=MAX_TILES - 1)
            before_last = act.value_load(table[0:1, MAX_TILES + 2:MAX_TILES + 3], min_val=NE - 2, max_val=MAX_TILES - 2)
            turned_rows_out(0)
            his(4, 8)
            act.wait_ge(quarter_used, splits(N_EXP + 3))
            act.activation(silu_t, ps[:, 0, :], ACT.Silu).then_inc(silu_ready, 1)
            his(8, 11)
            turned_rows_out(1)
            turned_product_out(0)
            his(11, 15)
            with act.Fori(1, last) as j:
                his(3, 4, j)
                silu_tile(j)
                his(4, 8, j)
                turned_rows_out(j + 1)
                his(8, 11, j)
                y_out(j - 1, TURN * j + splits(N_EXP + 7))
                turned_product_out(j)
                his(11, 12, j)
                y_store(j, j - 1)
                his(12, 15, j)
            his(3, 4, last)
            silu_tile(last)
            his(4, 11, last)
            y_out(before_last, TURN * last + splits(N_EXP + 7))
            y_store(last, before_last)
            turned_product_out(last)
            his(11, 12, last)
            y_out(last, TURN * last + splits(N_EXP + 11))
            y_store(last + 1, last)
            act.wait_ge(share_ready, 1)

            def scale_first(i):
                n = rows(i)
                act.wait_ge(yg_ready[i % 4][0], 16 * (i // 4 + 1))
                act.activation(yg[i % 4][0:n, 0, :], yg[i % 4][0:n, 0, :], ACT.Copy, scale=share[0:n, 0, i:i + 1]).then_inc(yg_scaled, 1)

            scale_first(0)
            for i in range(NTILE):
                n = rows(i)
                if i + 1 < NTILE:
                    scale_first(i + 1)
                act.wait_ge(x2_ready, i + 1)
                act.activation(sq_row[0:n, :], x1[0:n, i, :], ACT.Square, accum_out=sums[0:n, 0, NTILE + i:NTILE + i + 1]).then_inc(ssq_ready, 1)
                act.wait_ge(ms_ready, 3 + NTILE + i)
                act.activation(sums[0:n, 2, NTILE + i:NTILE + i + 1], sums[0:n, 1, NTILE + i:NTILE + i + 1], ACT.Sqrt).then_inc(root_ready, 1)
                act.wait_ge(out_ready, i + 1)
                dst = y_prompt[0, i * P:(i + 1) * P, :] if i < NP // P else y_sample.rearrange("b t d -> (b t) d")
                act.dma_start(dst, x1[0:n, i, :]).then_inc(out_stored, 16)
            act.wait_ge(out_stored, 16 * (3 + 6 + NTILE))

        @block.gpsimd
        def _(pool):
            pool.memset(ident[:, :], 0.0).then_inc(pool_chain, 1)
            pool.memset(before[:, :], 1.0).then_inc(pool_chain, 1)
            pool.memset(onesK[:, :], 1.0 / W).then_inc(pool_chain, 1)
            pool.memset(ones16[:, :], 1.0).then_inc(pool_chain, 1)
            pool.iota(tok_id[:, :], [[P, NTILE]], base=0, channel_multiplier=1).then_inc(pool_chain, 1)
            pool.iota(tile_no[:, :], [[1, MAX_TILES]], base=0, channel_multiplier=0).then_inc(pool_chain, 1)
            pool.memset(zslot[:, :], 0).then_inc(pool_chain, 1)
            pool.wait_ge(pool_chain, 7)
            pool.affine_select(out=ident[:, :], in_=ident[:, :], compare_op=ALU.not_equal, fill=1.0, base=0,
                               pattern=[[-1, P]], channel_multiplier=1).then_inc(const_ready, 1)
            pool.affine_select(out=before[:, :], in_=before[:, :], compare_op=ALU.is_gt, fill=0.0, base=0,
                               pattern=[[1, P]], channel_multiplier=-1).then_inc(const_ready, 1)
            pool.wait_ge(set_free[0], 1)
            pool.memset(zeros, 0.0).then_inc(pool_chain, 1)
            pool.wait_ge(pool_chain, 8)
            for t in range(NE, MAX_TILES):
                pool.dma_start(y_dram[t * P:(t + 1) * P, :], zeros).then_inc(y_zeroed, 16)
            pool.dma_start(slot_dram.rearrange("(p t) a -> p (t a)", p=P), zslot[:, :]).then_inc(slots_zeroed, 16)

            pool.wait_ge(slots_ready, 1)
            pool.wait_ge(slots_zeroed, 16)
            for k in range(2):
                for i in range(NTILE):
                    n = rows(i)
                    pool.indirect_dma_start(slot_dram, bass.IndirectOffsetOnAxis(ap=slot_i[0:n, k, i:i + 1], axis=0),
                                            tok_id[0:n, i:i + 1], None).then_inc(slots_stored, 16)
            pool.wait_ge(slots_stored, 16 * 2 * NTILE)
            def gather(j, first):
                if not first:
                    pool.wait_ge(xg_ready, 16 * j)
                pool.dma_start(slot_idx[:, :], slot_dram[bass.ds(j * P, P), :]).then_inc(slot_idx_ready, 16)
                pool.wait_ge(slot_idx_ready, 16 * j + 16)
                if not first:
                    pool.wait_ge(xgT_done, j)
                for p in range(2):
                    pool.wait_ge(h2_stored[p], 16 * ((NTILE + 1 - p) // 2))
                pool.sem_inc(gather_free, 1)
                pool.indirect_dma_start(xg, None, h2_dram, bass.IndirectOffsetOnAxis(ap=slot_idx[:, :], axis=0)).then_inc(xg_ready, 16)

            pool.wait_ge(table_ready, 4)
            n_tiles = pool.value_load(table[0:1, 0:1], min_val=NE, max_val=MAX_TILES)
            gather(0, True)
            with pool.Fori(1, n_tiles) as j:
                gather(j, False)
            pool.wait_ge(y_stored, 16 * n_tiles)
            pool.sem_inc(gather_free, 1)
            for i in range(NTILE):
                n = rows(i)
                if i >= 4:
                    pool.wait_ge(x2_ready, 1)
                for k in range(2):
                    pool.indirect_dma_start(yg[i % 4][0:n, k, :], None, y_dram, bass.IndirectOffsetOnAxis(ap=slot_i[0:n, k, i:i + 1], axis=0)).then_inc(yg_ready[i % 4][k], 16)
                if i >= 3:
                    for t in ((0,) if i == 3 else range(1, NTILE)):
                        pool.wait_ge(moe_ready, t + 1)
                        pool.tensor_tensor(x1[0:rows(t), t, :], x1[0:rows(t), t, :], yg[t % 4][0:rows(t), 1, :], ALU.add).then_inc(x2_ready, 1)

        @block.vector
        def _(dve):
            steps = [0]

            def link(ins, signal=None, value=0):
                if signal is None:
                    steps[0] += 1
                ins.then_inc(dve_step if signal is None else signal, 1)
                dve.wait_ge(dve_step if signal is None else signal, steps[0] if signal is None else value)

            def rsqrt(ms, root, out, tmp, n_root):
                dve.wait_ge(root_ready, n_root)
                link(dve.reciprocal(out, root))
                link(dve.tensor_tensor(tmp, out, out, ALU.mult))
                link(dve.tensor_tensor(tmp, tmp, ms, ALU.mult))
                link(dve.tensor_scalar(tmp, tmp, -0.5, 1.5, ALU.mult, ALU.add))
                link(dve.tensor_tensor(out, out, tmp, ALU.mult))

            dve.memset(sums[:, :, :], 1.0).then_inc(sums_ready, 1)
            for t in range(16):
                dve.memset(rcount[:, t:t + 1], 1.0 / (t + 1))

            def rest(out, whole, first):
                return dve.tensor_tensor(out, whole, first.bitcast(F32), ALU.subtract)

            def lo(n, turn=None):
                count = splits(n) if turn is None else turn * TURN + splits(n)
                dve.wait_ge(hi_done, count)
                rest(w_lo[:, split_slot(n), :], raw[:, n % RAW, :], w_hi[:, split_slot(n), :]).then_inc(lo_done, 1)

            c_pad = small[:, 0:16 * KD].rearrange("p (k s) -> p k s", k=KD)
            link(dve.memset(small[:, :], 0.0))
            dve.wait_ge(turned, 1)
            link(dve.tensor_copy(c_pad[:, :, 0:ND + 1], ps[:, 0, 0:9 * KD].rearrange("p (k s) -> p k s", s=9)), turned_out, 1)
            dve.wait_ge(cT_split, 1)
            rest(cT_lo[:, :, :], c_pad, cT_hi[:, :, :]).then_inc(cT_split, 1)

            def mod_group(g):
                dve.wait_ge(quarter_used, 4 * g + 4)
                cols = mod[:, g * COLS:(g + 1) * COLS]
                dve.tensor_tensor(cols, ps[0:ND + 1, 5 + g % 3, :], cols, ALU.add).then_inc(mod_ready, 1)

            def params_out():
                dve.wait_ge(turned, 2)
                dve.tensor_copy(pT[:, :, :], ps[:, 1, 0:KW * N_PARAM].rearrange("p (c r) -> p c r", c=KW))
                dve.tensor_copy(sconvT[:, :, :, :], ps[:, 1, 256:320].rearrange("p (c s r) -> p c s r", c=KW, s=ND)).then_inc(turned_out, 1)
                for c in range(2):
                    dve.tensor_copy(confT[:, 2 * c:2 * c + 2, :, :].rearrange("p c s r -> p (c s r)"), ps[:, 2 + c, 0:480])
                dve.tensor_copy(poolT[:, :, :, :], ps[:, 4, 0:480].rearrange("p (c s r) -> p c s r", c=KW, s=ND)).then_inc(turned_out, 2)

            def mean_squares():
                dve.wait_ge(ssq_ready, NTILE)
                dve.tensor_scalar(sums[:, 1, 0:NTILE], sums[:, 0, 0:NTILE], 1.0 / D, EPS, ALU.mult, ALU.add).then_inc(ms_ready, 1)

            def norm_root():
                rsqrt(sums[:, 1, 0:NTILE], sums[:, 2, 0:NTILE], sums[:, 3, 0:NTILE], sums[:, 2, 0:NTILE], 1)

            def scale_out():
                dve.wait_ge(modT_done, 1)
                dve.tensor_copy(shiftT[:, :, :], ps[:, 0, 0:72].rearrange("p (k s) -> p k s", s=9))
                link(dve.tensor_scalar(scaleT[:, :, :], ps[:, 0, 72:144].rearrange("p (k s) -> p k s", s=9), 1.0, None, ALU.add))
                for h in range(2):
                    s = dve.tensor_tensor(scaleT[:, 4 * h:4 * h + 4, :], scaleT[:, 4 * h:4 * h + 4, :],
                                          pT[:, :, R_N1 + h:R_N1 + h + 1].broadcast_to([P, KW, ND + 1]), ALU.mult)
                    s.then_inc(scaleT_ready, 1)

            dec = small[:, 0:64].rearrange("p (k s) -> p k s", k=KD)

            def sampled_input():
                dve.wait_ge(xT_done, 1)
                dve.wait_ge(scaleT_ready, 2)
                link(dve.tensor_tensor(dec, ps[:, 1, 0:64].rearrange("p (k s) -> p k s", k=KD), scaleT[:, :, 0:ND], ALU.mult))
                dve.tensor_tensor(dec, dec, shiftT[:, :, 0:ND], ALU.add).then_inc(hT_raw, 1)

            def sampled_rest():
                dve.wait_ge(hT_hi_done, 1)
                rest(hT_lo[:, :, NP:NT], dec, hT_hi[:, :, NP:NT]).then_inc(hT_lo_done, 1)

            def prompt_chunk(k):
                dve.wait_ge(xT_done, k + 2)
                if k >= 2:
                    dve.wait_ge(hT_hi_done, k)
                    dve.wait_ge(hT_lo_done, k)
                dve.tensor_scalar((tmp_a, tmp_b)[k % 2][:, 0:NP], ps[:, (2 + k) % 5, :], scaleT[:, k, ND:ND + 1], shiftT[:, k, ND:ND + 1], ALU.mult, ALU.add).then_inc(hT_raw, 1)

            def prompt_rest(k):
                dve.wait_ge(hT_hi_done, k + 2)
                rest(hT_lo[:, k, 0:NP], (tmp_a, tmp_b)[k % 2][:, 0:NP], hT_hi[:, k, 0:NP]).then_inc(hT_lo_done, 1)

            for n in range(N_IN + 4):
                lo(n)
                if n == 7:
                    dve.wait_ge(ld_mod, 16)
                if n % 4 == 3 and n > 4:
                    mod_group(n // 4 - 1)
                i = n - (Q_NORM + NTILE)
                k = n - (Q_TURN + AHEAD + 1)
                if n == Q_PARAMS + AHEAD:
                    params_out()
                elif i == 0:
                    mean_squares()
                elif i == 2:
                    norm_root()
                elif 3 <= i < 6:
                    for t in range(2 * i - 6, min(2 * i - 4, NTILE)):
                        dve.tensor_scalar(x_in[0:rows(t), t, :], x_in[0:rows(t), t, :], sums[0:rows(t), 3, t:t + 1], None, ALU.mult).then_inc(xn_ready, 1)
                elif n == Q_SCALE + AHEAD:
                    scale_out()
                elif k == -1:
                    sampled_input()
                elif 0 <= k <= KD + 1:
                    if k == 1:
                        sampled_rest()
                    elif k > 1:
                        prompt_rest(k - 2)
                    if k < KD:
                        prompt_chunk(k)

            dve.wait_ge(mod_stored, 16)
            dve.memset(ua[:, :, 0:CK - 1], 0.0)
            dve.memset(ub[:, :, 0:PB], 0.0)
            dve.memset(uc[:, :, 0:SK - 1], 0.0).then_inc(pads_ready, 1)
            for q in range(4, 7):
                lo(N_IN + q)

            def glu():
                for m in range(4):
                    dve.wait_ge(set_free[m], 2)
                    dve.tensor_tensor(ua[:, m, CK - 1:UA], ua[:, m, CK - 1:UA], sig[:, m % 2, :], ALU.mult).then_inc(z_dve, 1)

            def taps(t):
                for c in range(KW):
                    w = pT[:, c, R_TAPS + t:R_TAPS + t + 1]
                    if t:
                        dve.wait_ge(conv_step, KW * (t - 1) + c + 1)
                        dve.scalar_tensor_tensor(va[:, c, 0:NP], ua[:, c, t:t + NP], w, va[:, c, 0:NP], ALU.mult, ALU.add).then_inc(conv_step, 1)
                    else:
                        dve.wait_ge(z_dve, c + 1)
                        dve.tensor_scalar(va[:, c, 0:NP], ua[:, c, 0:NP], w, pT[:, c, R_CB:R_CB + 1], ALU.mult, ALU.add).then_inc(conv_step, 1)

            def conv_sampled():
                prod = confT[:, :, :, :]
                for c in range(KW):
                    s = dve.tensor_tensor(prod[:, c, :, :], confT[:, c, :, :], pT[:, c:c + 1, 0:CK - 1].broadcast_to([P, ND, CK - 1]), ALU.mult)
                link(s)
                va_d, ua_d = va[:, :, NP:NT], ua[:, :, CK - 1 + NP:UA]
                dec = small[:, 64:96].rearrange("p (c s) -> p c s", c=KW)
                link(dve.tensor_reduce(va_d, prod, AX.X, ALU.add))
                link(dve.tensor_tensor(dec, ua_d, pT[:, :, CK - 1:CK].broadcast_to([P, KW, ND]), ALU.mult))
                link(dve.tensor_tensor(va_d, va_d, dec, ALU.add))
                dve.tensor_tensor(va_d, va_d, pT[:, :, R_CB:R_CB + 1].broadcast_to([P, KW, ND]), ALU.add).then_inc(conv_ready, 1)

            def pooling(g):
                w = WINDOWS[g]
                dve.wait_ge(set_free[g], 3)
                src, n = ub[:, g, 0:PB + NP], 1
                for dst in (tmp_a, tmp_b, tmp_a, tmp_b)[:g + 1]:
                    at = 2 * n - 1
                    link(dve.tensor_tensor(dst[:, at:PB + NP], src[:, at:PB + NP], src[:, at - n:PB + NP - n], ALU.add))
                    src, n = dst, 2 * n
                tok, tot, out = ub[:, g, PB:PB + NP], src[:, PB:PB + NP], pooled[:, g, 0:NP]
                link(dve.scalar_tensor_tensor(out, tot, 1.0 / w, tok, ALU.mult, ALU.subtract))
                link(dve.tensor_tensor(small[:, 0:w - 1], tot[:, 0:w - 1], rcount[:, 0:w - 1], ALU.mult))
                link(dve.tensor_tensor(out[:, 0:w - 1], small[:, 0:w - 1], tok[:, 0:w - 1], ALU.subtract))
                tok, out, tot = ub[:, g, PB + NP:UB], pooled[:, g, NP:NT], small[:, 32:40]
                link(dve.tensor_reduce(tot, poolT[:, g, :, PB - (w - 1):PB], AX.X, ALU.add))
                link(dve.tensor_tensor(tot, tot, tok, ALU.add))
                link(dve.scalar_tensor_tensor(out, tot, 1.0 / w, tok, ALU.mult, ALU.subtract), branch_b, g + 1)

            def times_s_c():
                for m in range(4):
                    dve.wait_ge(*z_complete(5, m))
                    dve.wait_ge(set_free[m], 5)
                    dve.tensor_tensor(split(uc[:, m, SK - 1:UC]), halves(m), split(uc[:, m, SK - 1:UC]), ALU.mult).then_inc(set_free[m], 1)

            def short_conv(m):
                dve.wait_ge(set_free[m], 6)
                tap = [pT[:, m, R_STAPS + t:R_STAPS + t + 1] for t in range(SK)]
                acc = tmp_a[:, 0:NP]
                link(dve.tensor_scalar(acc, uc[:, m, 0:NP], tap[0], None, ALU.mult))
                link(dve.scalar_tensor_tensor(acc, uc[:, m, 1:1 + NP], tap[1], acc, ALU.mult, ALU.add))
                link(dve.scalar_tensor_tensor(acc, uc[:, m, 2:2 + NP], tap[2], acc, ALU.mult, ALU.add))
                link(dve.tensor_tensor(sbr[:, m, 0:NP], sbr[:, m, 0:NP], acc, ALU.mult))
                acc = tmp_a[:, 0:ND]
                link(dve.tensor_scalar(acc, sconvT[:, m, :, 0:1].rearrange("p s r -> p (s r)"), tap[0], None, ALU.mult))
                link(dve.scalar_tensor_tensor(acc, sconvT[:, m, :, 1:2].rearrange("p s r -> p (s r)"), tap[1], acc, ALU.mult, ALU.add))
                link(dve.scalar_tensor_tensor(acc, uc[:, m, SK - 1 + NP:UC], tap[2], acc, ALU.mult, ALU.add))
                link(dve.tensor_tensor(sbr[:, m, NP:NT], sbr[:, m, NP:NT], acc, ALU.mult), branch_c, m + 1)

            for q in range(7, 4 * G_IN):
                if q == 11:
                    glu()
                if q == 27:
                    times_s_c()
                lo(N_IN + q)
                if 11 <= q < 11 + CK:
                    taps(q - 11)
                elif q == 11 + CK:
                    conv_sampled()
                elif 11 + CK < q <= 11 + CK + len(WINDOWS):
                    pooling(q - 12 - CK)
                if q >= 44:
                    short_conv(q - 44)
            dve.wait_ge(mix_done, 1)
            dve.wait_ge(conv_ready, 1)
            for c in range(KW):
                s = dve.tensor_tensor(split(va[:, c, :]), split(va[:, c, :]), halves(0), ALU.subtract)
                s.then_inc(centred if c < KW - 1 else set_free[0], 1)

            def unit(n):
                dve.wait_ge(mix_done, n + 1)
                return n % 4

            def free_at(n):
                return G_IN + n // 4 + 1

            for j in range(KD):
                s = unit(3 + j)
                dve.scalar_tensor_tensor(split(gates[:, KD + j, :]), halves(s), pT[:, j % 4, R_PS + j // 4:R_PS + j // 4 + 1], split(gates[:, KD + j, :]), ALU.mult, ALU.mult).then_inc(set_free[s], 1)
            s = unit(11)
            link(dve.tensor_scalar(split(tmp_b[:, 0:NT]), halves(s), EPS, None, ALU.add), set_free[s], free_at(11))
            dve.tensor_copy(tmp_a[:, 0:NT], tmp_b[:, 0:NT]).then_inc(ms_ready, 1)
            dve.wait_ge(ms_ready, 2)
            rsqrt(tmp_a[:, 0:NT], tmp_b[:, 0:NT], rstdT, tmp_b[:, 0:NT], 2)
            for c in range(KW):
                dve.tensor_tensor(va[:, c, :], va[:, c, :], rstdT, ALU.mult).then_inc(normed, 1)
            def merged_rest(j):
                dve.wait_ge(m_hi_done, j + 1)
                rest(hT_lo[:, j, :], gates[:, KD + j, :], hT_hi[:, j, :]).then_inc(m_lo_done, 1)

            for base, first in ((12, 2 * KD), (20, 0)):
                if base == 20:
                    lo(N_WO)
                    lo(N_WO + 1)
                for j in range(KD):
                    s = unit(base + j)
                    tmp = (tmp_a, tmp_b)[j % 2][:, 0:NT]
                    link(dve.tensor_tensor(split(tmp), halves(s), split(gates[:, first + j, :]), ALU.mult), set_free[s], free_at(base + j))
                    dve.tensor_tensor(gates[:, KD + j, :], gates[:, KD + j, :], tmp, ALU.add).then_inc(merged, 1)
                    if base == 20 and j:
                        merged_rest(j - 1)
                        if j in (4, 6):
                            lo(N_WO + j // 2)
            merged_rest(KD - 1)

            dve.wait_ge(merged, 2 * KD)
            for r in range(4):
                dve.memset(rank4[:, r:r + 1], 4.0 - r)
            dve.memset(valid[:, 0:NTILE - 1], 1.0)
            link(dve.memset(valid[:, NTILE - 1:NTILE], 0.0))
            dve.memset(valid[0:ND, NTILE - 1:NTILE], 1.0)
            link(dve.memset(logits[:, :, :], 0.0))
            for q in range(4, 8):
                lo(N_WO + q)
            dve.wait_ge(ld_bcast, 16 * 6)
            dve.wait_ge(ld_dec, 16 * 4)
            link(dve.scalar_tensor_tensor(bvec[:, SC2, :], bvec[:, SC2, :], 1.0, n2b, ALU.add, ALU.mult))
            link(dve.scalar_tensor_tensor(sc2_dec[0:ND, :], sc2_dec[0:ND, :], 1.0, n2b[0:ND, :], ALU.add, ALU.mult))
            dve.wait_ge(ld_x, 2 * 16 * NTILE)
            dve.wait_ge(ld_router, 64)

            def norm_rows(i, col, n_ssq, n_root):
                n = rows(i)
                dve.wait_ge(ssq_ready, n_ssq)
                link(dve.tensor_scalar(sums[0:n, 1, col:col + 1], sums[0:n, 0, col:col + 1], 1.0 / D, EPS, ALU.mult, ALU.add), ms_ready, n_root)
                rsqrt(sums[0:n, 1, col:col + 1], sums[0:n, 2, col:col + 1], sums[0:n, 3, col:col + 1], sums[0:n, 2, col:col + 1], n_root)
                return sums[0:n, 3, col:col + 1]

            def logit_tile(i):
                n = rows(i)
                dve.wait_ge(logit_done, i + 1)
                dve.tensor_tensor(logits[0:n, i, :], ps[0:n, i, 0:NR], rbias[0:n, :], ALU.add).then_inc(logits_ready, 1)

            for i in range(NTILE):
                n = rows(i)
                prompt = i < NP // P
                if i < NTILE - 1:
                    dve.wait_ge(wo_done, i + 1)
                else:
                    dve.wait_ge(quarter_used, splits(N_WO + 7))
                g1 = bvec[0:n, G1, :] if prompt else g1_dec[0:ND, :]
                dve.tensor_tensor(t_row[0:n, 0:COLS], ps[0:n, i, :], g1[:, 0:COLS], ALU.mult)
                link(dve.tensor_tensor(t_row[0:n, COLS:D], ps[0:n, 5 + i % 2, :], g1[:, COLS:D], ALU.mult), t_ready, i + 1)
                link(dve.tensor_tensor(x1[0:n, i, :], x1[0:n, i, :], t_row[0:n, :], ALU.add), x1_ready, i + 1)
                r = norm_rows(i, i, NTILE + i + 1, 3 + i)
                if i >= 2:
                    dve.wait_ge(h2T_done, i - 1)
                    dve.wait_ge(h2_stored[i % 2], 16 * (i // 2))
                sc2 = bvec[0:n, SC2, :] if prompt else sc2_dec[0:ND, :]
                link(dve.scalar_tensor_tensor(h2[0:n, i % 2, :], x1[0:n, i, :], r, sc2, ALU.mult, ALU.mult))
                shift = bvec[0:n, SH2, :] if prompt else sh2_dec[0:ND, :]
                dve.tensor_tensor(h2[0:n, i % 2, :], h2[0:n, i % 2, :], shift, ALU.add).then_inc(h2_ready, 1)
                if i:
                    logit_tile(i - 1)
            logit_tile(NTILE - 1)
            dve.wait_ge(logits_ready, NTILE)

            T5 = [P, NTILE, 4]

            def first_of(eq, rank_tmp, out):
                link(dve.tensor_tensor(rank_tmp, eq, rank4[:, None, :].broadcast_to(T5), ALU.mult))
                link(dve.tensor_reduce(col1[:, :, 0], rank_tmp, AX.X, ALU.max))
                link(dve.tensor_tensor(out, rank_tmp, col1[:, :, 0:1].broadcast_to(T5), ALU.is_equal))

            glog, elog = logits[:, :, 0:NG], logits[:, :, NG:NR]
            link(dve.tensor_reduce(col1[:, :, 0], glog, AX.X, ALU.max))
            link(dve.tensor_tensor(gdiff, glog, col1[:, :, 0:1].broadcast_to(T5), ALU.subtract), diff_ready, 1)
            link(dve.tensor_scalar(eq4, gdiff, 0.0, None, ALU.is_equal))
            first_of(eq4, tmp4, gone)
            link(dve.tensor_tensor(gone, gone, valid[:, :, None].broadcast_to(T5), ALU.mult))
            e44 = elog.rearrange("p t (g j) -> p t g j", g=NG)
            w44 = work16.rearrange("p t (g j) -> p t g j", g=NG)
            link(dve.tensor_tensor(w44, e44, gone[:, :, :, None].broadcast_to([P, NTILE, NG, EG]), ALU.mult))
            link(dve.tensor_reduce(sel, work16.rearrange("p t (g j) -> p t j g", g=NG), AX.X, ALU.add))
            link(dve.tensor_reduce(col1[:, :, 1], sel, AX.X, ALU.max))
            link(dve.tensor_tensor(sel, sel, col1[:, :, 1:2].broadcast_to(T5), ALU.subtract))
            link(dve.tensor_scalar(eq4, sel, 0.0, None, ALU.is_equal))
            first_of(eq4, tmp4, one_a)
            link(dve.scalar_tensor_tensor(sel, one_a, -1.0e30, sel, ALU.mult, ALU.add))
            link(dve.tensor_reduce(col1[:, :, 2], sel, AX.X, ALU.max), diff_ready, 2)
            link(dve.tensor_tensor(eq4, sel, col1[:, :, 2:3].broadcast_to(T5), ALU.is_equal))
            first_of(eq4, tmp4, one_b)
            for one, oh in ((one_a, onehot[:, 0]), (one_b, onehot[:, 1])):
                link(dve.tensor_tensor(oh.rearrange("p t (g j) -> p t g j", g=NG), gone[:, :, :, None].broadcast_to([P, NTILE, NG, EG]),
                                       one[:, :, None, :].broadcast_to([P, NTILE, NG, EG]), ALU.mult))
            dve.tensor_tensor(onehot_both[:, :, :], onehot[:, 0], onehot[:, 1], ALU.add).then_inc(onehot_ready, 1)
            dve.wait_ge(exp_ready, 2)
            link(dve.tensor_reduce(col1[:, :, 3], exp_out[0], AX.X, ALU.add))
            link(dve.tensor_scalar(col1[:, :, 4], col1[:, :, 5], 1.0, None, ALU.add))
            link(dve.tensor_tensor(col1[:, :, 4], col1[:, :, 4], col1[:, :, 3], ALU.mult))
            link(dve.reciprocal(share[:, 0, :], col1[:, :, 4]))
            link(dve.tensor_tensor(share[:, 1, :], share[:, 0, :], col1[:, :, 5], ALU.mult), share_ready, 1)

            dve.wait_ge(count_done, 1)
            link(dve.tensor_copy(count16, ps[:, 7, NTILE * NE:(NTILE + 1) * NE]))
            link(dve.tensor_scalar(tiles16, count16, float(P), 1.0, ALU.is_gt, ALU.add))
            for full in range(2, (NT + P - 1) // P):
                link(dve.scalar_tensor_tensor(tiles16, count16, float(full * P), tiles16, ALU.is_gt, ALU.add))
            src, dst = scan_a, scan_b
            link(dve.tensor_copy(src, tiles16))
            for s in (1, 2, 4, 8):
                dve.tensor_copy(dst[:, 0:s], src[:, 0:s])
                link(dve.tensor_tensor(dst[:, s:NE], src[:, s:NE], src[:, 0:NE - s], ALU.add))
                src, dst = dst, src
            ends = src
            link(dve.tensor_tensor(dst, ends, tiles16, ALU.subtract))
            link(dve.tensor_scalar(dst, dst, float(P), None, ALU.mult))
            link(dve.tensor_tensor(slotbase, ps[:, 7, 0:NTILE * NE].rearrange("p (t e) -> p t e", e=NE),
                                   dst[:, None, :].broadcast_to([P, NTILE, NE]), ALU.add))
            for k in range(2):
                link(dve.tensor_tensor(work16, onehot[:, k], slotbase, ALU.mult))
                link(dve.tensor_reduce(slot_f[:, k, :], work16, AX.X, ALU.add))
            dve.tensor_copy(slot_i[:, :, :], slot_f).then_inc(slots_ready, 1)
            link(dve.tensor_copy(tile_f, tile_no[:, :]))
            link(dve.tensor_tensor(cmp, ends[:, None, :].broadcast_to([P, MAX_TILES, NE]), tile_f[:, :, None].broadcast_to([P, MAX_TILES, NE]), ALU.is_le))
            link(dve.tensor_reduce(tile_f, cmp, AX.X, ALU.add))
            dve.tensor_copy(table[:, 1:MAX_TILES + 1], tile_f).then_inc(table_ready, 1)
            dve.tensor_scalar(table[:, MAX_TILES + 1:MAX_TILES + 2], ends[:, NE - 1:NE], -1.0, None, ALU.add).then_inc(table_ready, 1)
            dve.tensor_scalar(table[:, MAX_TILES + 2:MAX_TILES + 3], ends[:, NE - 1:NE], -2.0, None, ALU.add).then_inc(table_ready, 1)
            dve.tensor_copy(table[:, 0:1], ends[:, NE - 1:NE]).then_inc(table_ready, 1)

            def product_tile(j, used):
                dve.wait_ge(quarter_used, used)
                dve.wait_ge(silu_ready, j + 1)
                dve.wait_ge(actT_done, j)
                dve.tensor_tensor(act_t, ps[:, 1, :], silu_t, ALU.mult).then_inc(act_ready, 1)

            def turned_rows_rest(j):
                dve.wait_ge(xgT_hi_done, j + 1)
                rest(xgT_lo, ps[:, 2:4, :].rearrange("p b (k t) -> p (b k) t", k=4), xgT_hi).then_inc(xgT_lo_done, 1)

            def turned_product_rest(j):
                dve.wait_ge(actT_hi_done, j + 1)
                rest(actT_lo, ps[:, 6, :].rearrange("p (k t) -> p k t", k=KF), actT_hi).then_inc(actT_lo_done, 1)

            def y_out(jm, used):
                dve.wait_ge(quarter_used, used)
                dve.wait_ge(y_stored, jm * 16)
                dve.tensor_copy(y_t[:, COLS:D], ps[:, 5, :]).then_inc(y_dve, 1)

            def los(first, end, j=None):
                for c in range(first, end):
                    lo(N_EXP + c, j)

            los(0, 4)
            dve.wait_ge(table_ready, 4)
            last = dve.value_load(table[0:1, MAX_TILES + 1:MAX_TILES + 2], min_val=NE - 1, max_val=MAX_TILES - 1)
            before_last = dve.value_load(table[0:1, MAX_TILES + 2:MAX_TILES + 3], min_val=NE - 2, max_val=MAX_TILES - 2)
            turned_rows_rest(0)
            los(4, 11)
            dve.wait_ge(quarter_used, splits(N_EXP + 7))
            dve.wait_ge(silu_ready, 1)
            dve.tensor_tensor(act_t, ps[:, 1, :], silu_t, ALU.mult).then_inc(act_ready, 1)
            turned_rows_rest(1)
            turned_product_rest(0)
            los(11, 15)
            with dve.Fori(1, last) as j:
                los(3, 7, j)
                product_tile(j, TURN * j + splits(N_EXP + 3))
                los(7, 8, j)
                turned_rows_rest(j + 1)
                los(8, 11, j)
                y_out(j - 1, TURN * j + splits(N_EXP + 7))
                turned_product_rest(j)
                los(11, 15, j)
            los(3, 7, last)
            product_tile(last, TURN * last + splits(N_EXP + 3))
            los(7, 11, last)
            y_out(before_last, TURN * last + splits(N_EXP + 7))
            turned_product_rest(last)
            los(11, 12, last)
            y_out(last, TURN * last + splits(N_EXP + 11))

            for i in range(NTILE + 1):
                if i < NTILE:
                    n = rows(i)
                    y = yg[i % 4]
                    dve.wait_ge(yg_scaled, i + 1)
                    dve.wait_ge(yg_ready[i % 4][1], 16 * (i // 4 + 1))
                    link(dve.scalar_tensor_tensor(y[0:n, 1, :], y[0:n, 1, :], share[0:n, 1, i:i + 1], y[0:n, 0, :], ALU.mult, ALU.add))
                    g2 = bvec[0:n, G2, :] if i < NP // P else g2_dec[0:ND, :]
                    dve.tensor_tensor(y[0:n, 1, :], y[0:n, 1, :], g2, ALU.mult).then_inc(moe_ready, 1)
                if i:
                    t = i - 1
                    r = norm_rows(t, NTILE + t, 2 * NTILE + t + 1, 3 + NTILE + t)
                    dve.scalar_tensor_tensor(x1[0:rows(t), t, :], x1[0:rows(t), t, :], r, bvec[0:rows(t), FG, :], ALU.mult, ALU.mult).then_inc(out_ready, 1)


_INS = ['x_prompt', 'x_sample', 'state_conf', 'state_pool', 'state_sconv', 'c_prompt', 'c_sample', 'w_ada', 'b_ada',
        'norm1_g', 'norm2_g', 'final_g', 'w_in', 'conf_dw', 'conf_dw_b', 'conf_ln_g', 'conf_ln_b', 'conf_pw',
        'pool_w', 'pool_scale', 'sc_dw', 'sc_out', 'w_o', 'router_g', 'router_g_b', 'router_e', 'router_e_b',
        'exp_w1', 'exp_w3', 'exp_w2']
_OUTS = [(1, NP, D), (ND, 1, D), (1, 1, CK - 1, W), (1, ND, CK - 1, W), (1, 1, PB, W), (1, ND, PB, W),
         (1, 1, SK - 1, W), (1, ND, SK - 1, W)]


def kernel(**inputs):
    import concourse.bacc as bacc
    from concourse.bass_utils import run_bass_kernel_spmd

    nc = bacc.Bacc("TRN2", target_bir_lowering=False, num_devices=1)
    arrays, args = {}, []
    for name in _INS:
        a = np.ascontiguousarray(inputs[name])
        arrays[f"in_{name}_dram"] = a
        args.append(nc.dram_tensor(f"in_{name}_dram", a.shape, mybir.dt.from_np(a.dtype), kind="ExternalInput").ap())
    for i, shape in enumerate(_OUTS):
        args.append(nc.dram_tensor(f"out_{i}_dram", shape, F32, kind="ExternalOutput").ap())
    trunk_step(nc, *args)
    r = run_bass_kernel_spmd(nc, [arrays], core_ids=[0])
    return tuple(r.results[0][f"out_{i}_dram"] for i in range(len(_OUTS)))
```

```python
from contextlib import ExitStack

import numpy as np

import concourse.bass as bass
from concourse import mybir

ALU = mybir.AluOpType
ACT = mybir.ActivationFunctionType
AX = mybir.AxisListType
F32 = mybir.dt.float32
F32R = mybir.dt.float32r
BF16 = mybir.dt.bfloat16
I32 = mybir.dt.int32

P = 128
D = 1024
KD = D // P
NP = 512
ND = 8
NT = NP + ND
HT = NT // 2
NTILE = NP // P + 1
W = D // 2
KW = W // P
CK = 31
SK = 3
WINDOWS = (2, 4, 8, 16)
PB = 15
DIN = 6 * W + 3 * D
NG = 4
EG = 4
NE = NG * EG
FF = D // 2
KF = FF // P
EPS = 1e-6
COLS = 512
G_ADA = 6 * D // COLS
G_IN = DIN // COLS
RAW = 6
SPLIT = 4
QUARTER = 1024
TURN = 12
N_IN = 4 * G_ADA
N_MIX = N_IN + 4 * G_IN
N_WO = N_MIX + 9
N_EXP = N_WO + 8
MAX_TILES = NE + 2 * NT // P
LISTED = MAX_TILES + 1
CHOICES = 2 * NTILE
NR = NG + NE

MERGE_ORDER = (4, 5, 6, 7, 0, 1, 2, 3)
Q_PARAMS = 11
Q_NORM = 9
Q_ROOT = Q_NORM + 9
Q_SCALE = 20
Q_TURN = Q_SCALE + 2
AHEAD = 4

R_TAPS, R_STAPS, R_CB, R_LG, R_LB, R_N1, R_PS = 0, 31, 34, 35, 36, 37, 39
N_PARAM = 41


def trunk_step(nc, x_prompt, x_sample, state_conf, state_pool, state_sconv, c_prompt, c_sample, w_ada,
               b_ada, norm1_g, norm2_g, final_g, w_in, conf_dw, conf_dw_b, conf_ln_g, conf_ln_b, conf_pw,
               pool_w, pool_scale, sc_dw, sc_out, w_o, router_g, router_g_b, router_e, router_e_b, exp_w1,
               exp_w3, exp_w2, y_prompt, y_sample, conf_p, conf_s, pool_p, pool_s, sconv_p, sconv_s):
    mod_dram = nc.dram_tensor("mod_rows", [ND + 1, 4 * D], F32, kind="Internal").ap()
    h2_dram = nc.dram_tensor("h2_rows", [NT, D], F32, kind="Internal").ap()
    y_dram = nc.dram_tensor("expert_rows", [MAX_TILES * P, D], F32, kind="Internal").ap()

    ctx = ExitStack()
    with ctx:
        def sb(name, shape, dt=F32):
            return ctx.enter_context(nc.sbuf_tensor(name, shape, dt))

        def sem(name):
            return ctx.enter_context(nc.semaphore(name))

        raw = sb("raw", [P, RAW, QUARTER])
        w_hi = sb("w_hi", [P, SPLIT, QUARTER], F32R)
        w_lo = sb("w_lo", [P, SPLIT, QUARTER], F32R)
        hT_hi = sb("hT_hi", [P, KD, NT], F32R)
        hT_lo = sb("hT_lo", [P, KD, NT], F32R)
        region_a = sb("region_a", [P, 3 * KD * NT])
        region_b = sb("region_b", [P, 13500])
        pT = sb("pT", [P, KW, N_PARAM])
        confT = sb("confT", [P, KW, ND, CK - 1])
        poolT = sb("poolT", [P, KW, ND, PB])
        sconvT = sb("sconvT", [P, KW, ND, SK - 1])
        cT_hi = sb("cT_hi", [P, KD, 16], F32R)
        cT_lo = sb("cT_lo", [P, KD, 16], F32R)
        scaleT = sb("scaleT", [P, KD, ND + 1])
        shiftT = sb("shiftT", [P, KD, ND + 1])
        ident = sb("ident", [P, P])
        ones_w = sb("ones_w", [P, P])
        before = sb("before", [P, P], BF16)
        ones16 = sb("ones16", [P, P], BF16)
        sums = sb("sums", [P, 4, 2 * NTILE])
        wrouter = sb("wrouter", [P, KD, NR])
        rbias = sb("rbias", [P, NR])
        small = sb("small", [P, 128])
        onehot_both = sb("onehot_both", [P, NTILE, NE], BF16)
        tok_id = sb("tok_id", [P, 1], I32)
        tile_no = sb("tile_no", [P, LISTED + 1], I32)
        slot_i = sb("slot_i", [P, 2, NTILE], I32)
        table = sb("table", [P, 3], I32)
        kept_mark = sb("kept_mark", [1, TURN], I32)
        tile_expert = sb("tile_expert", [P, MAX_TILES], I32)
        fresh_flags = sb("fresh_flags", [P, 2, MAX_TILES], I32)
        slot_idx = sb("slot_idx", [P, 1], I32)
        slot_tokens = sb("slot_tokens", [P, LISTED], I32)
        slot_no = sb("slot_no", [P, P], I32)
        tok_parts = sb("tok_parts", [P, NTILE, 2], BF16)
        ps = ctx.enter_context(nc.psum_tensor("ps", [P, 8, 512], F32))

        def carve(region, at, *dims):
            n = int(np.prod(dims))
            v = region[:, at:at + n]
            if len(dims) == 2:
                return v.rearrange("p (a b) -> p a b", b=dims[1])
            if len(dims) == 3:
                return v.rearrange("p (a b c) -> p a b c", b=dims[1], c=dims[2])
            return v

        def slot(ring, s, k):
            return ring[:, s, :].rearrange("p (k n) -> p k n", k=k)

        def raw_place(n, turn=None):
            if n < N_EXP:
                count, step = n // RAW + 1, TURN // RAW
                place = raw[:, n % RAW, :]
                ready = raw_ready[n % RAW]
            else:
                c = n - N_EXP
                if c % TURN < RAW:
                    s = (N_EXP + c % TURN) % RAW
                    place, ready = raw[:, s, :], raw_ready[s]
                    count = (N_EXP - s + RAW - 1) // RAW + c // TURN + 1
                else:
                    place, ready = more_raw[c % TURN - RAW], more_ready[c % TURN - RAW]
                    count = c // TURN + 1
                step = 1
            return place, ready, 16 * count if turn is None else turn * (16 * step) + 16 * count

        def split_slot(n):
            return (n - (n > N_MIX)) % SPLIT

        def splits(n):
            return n + 1 - (n > N_MIX)

        x_in = carve(region_a, 0, NTILE, D)
        conf_raw = carve(region_a, 5120, 2, W)
        pool_raw = carve(region_a, 6144, W)
        sconv_raw = carve(region_a, 6656, W)
        c_raw = carve(region_a, 7168, D)
        square_junk = carve(region_a, 8192, D)
        params = carve(region_a, 9216, W)[0:N_PARAM]
        zeros = square_junk
        gates = carve(region_a, 0, 3 * KD, NT)
        x1 = carve(region_a, 0, NTILE, D)
        bvec = carve(region_a, 5120, 5, D)
        G2, FG, G1, SH2, SC2 = range(5)
        sc2_dec = carve(region_a, 10240, D)
        n2b = carve(region_a, 11264, D)
        more_raw = [region_a[:, at:at + QUARTER] for at in range(7168, 12288, QUARTER)]
        mod = region_b[0:ND + 1, 0:6 * D]
        UA, UB, UC = CK - 1 + NT, PB + NT, SK - 1 + NT
        ua = carve(region_b, 0, KW, UA)
        va = carve(region_b, 2200, KW, NT)
        ub = carve(region_b, 4280, KW, UB)
        pooled = carve(region_b, 6420, KW, NT)
        uc = carve(region_b, 8500, KW, UC)
        sbr = carve(region_b, 10588, KW, NT)
        squares = carve(region_b, 0, KW, NT)
        rstdT = carve(region_b, 4280, NT)
        tail = carve(region_b, 8500, 3, W)[0:40]
        h2 = [carve(region_b, at, D) for at in (0, 1024, 6144)]
        h2T = carve(region_b, 2048, KD, P)
        t_row = carve(region_b, 3072, D)
        sq_row = carve(region_b, 4096, D)
        xg = carve(region_b, 5120, D)
        silu_t = carve(region_b, 7168, FF)
        act_t = carve(region_b, 7680, FF)
        y_t = carve(region_b, 8192, D)
        g1_dec = carve(region_b, 9216, D)
        sh2_dec = carve(region_b, 10240, D)
        g2_dec = carve(region_b, 11264, D)
        yg = [carve(region_b, at, 2, D) for at in (9216, 0, 5120, 7168)]
        more_raw.append(carve(region_b, 2048, QUARTER))
        xgT_hi, xgT_lo = (t[:, :, 0:P] for t in (hT_hi, hT_lo))
        actT_hi, actT_lo = (t[:, 0:KF, P:2 * P] for t in (hT_hi, hT_lo))
        tmp_a = sb("tmp_a", [P, UB])
        tmp_b = sb("tmp_b", [P, UB])
        sig = pooled[:, 2:4, :]
        rcount = sb("rcount", [P, 16])
        begun = carve(tmp_a, 0, CHOICES, LISTED + 1)
        in_tile = carve(tmp_a, 260, CHOICES * LISTED // 2).bitcast(BF16).rearrange("p (c m) -> p c m", m=LISTED)
        tile_parts = carve(tmp_b, 0, CHOICES * LISTED).bitcast(BF16).rearrange("p (c a m) -> p c a m", a=2, m=LISTED)
        tile_start = carve(tmp_b, 260, LISTED + 1)

        ld_c = sem("ld_c")
        ld_x = sem("ld_x")
        ld_rows = sem("ld_rows")
        ld_mod = sem("ld_mod")
        ld_router = sem("ld_router")
        ld_bcast = sem("ld_bcast")
        const_ready = sem("const_ready")
        sums_ready = sem("sums_ready")
        conv_step = sem("conv_step")
        pool_chain = sem("pool_chain")
        silu_c_ready = sem("silu_c_ready")
        turned = sem("turned")
        turned_out = sem("turned_out")
        raw_ready = [sem(f"raw_ready{s}") for s in range(RAW)]
        more_ready = [sem(f"more_ready{s}") for s in range(TURN - RAW)]
        hi_done = sem("hi_done")
        lo_done = sem("lo_done")
        quarter_used = sem("quarter_used")
        cT_split = sem("cT_split")
        mod_stored = sem("mod_stored")
        hT_raw = sem("hT_raw")
        hT_hi_done = sem("hT_hi_done")
        hT_lo_done = sem("hT_lo_done")
        ld_dec = sem("ld_dec")
        m_hi_done = sem("m_hi_done")
        m_lo_done = sem("m_lo_done")
        xgT_hi_done = sem("xgT_hi_done")
        xgT_lo_done = sem("xgT_lo_done")
        actT_hi_done = sem("actT_hi_done")
        actT_lo_done = sem("actT_lo_done")
        ada_done = sem("ada_done")
        mod_ready = sem("mod_ready")
        modT_done = sem("modT_done")
        scaleT_ready = sem("scaleT_ready")
        ssq_ready = sem("ssq_ready")
        root_ready = sem("root_ready")
        ms_ready = sem("ms_ready")
        xn_ready = sem("xn_ready")
        xT_done = sem("xT_done")
        z_done = sem("z_done")
        set_free = [sem(f"set_free{m}") for m in range(4)]
        z_dve = sem("z_dve")
        pads_ready = sem("pads_ready")
        conv_ready = sem("conv_ready")
        sq_ready = sem("sq_ready")
        centred = sem("centred")
        branch_b = sem("branch_b")
        branch_c = sem("branch_c")
        normed = sem("normed")
        branch_a = sem("branch_a")
        sbr_hi_done = sem("sbr_hi_done")
        sbr_lo_done = sem("sbr_lo_done")
        va_hi_done = sem("va_hi_done")
        va_lo_done = sem("va_lo_done")
        mix_done = sem("mix_done")
        tail_ready = sem("tail_ready")
        merged = sem("merged")
        wo_done = sem("wo_done")
        t_ready = sem("t_ready")
        x1_ready = sem("x1_ready")
        h2_ready = sem("h2_ready")
        h2_stored = [sem(f"h2_stored{i}") for i in range(3)]
        h2T_done = sem("h2T_done")
        h2T_ready = sem("h2T_ready")
        logit_done = sem("logit_done")
        logits_ready = sem("logits_ready")
        diff_ready = sem("diff_ready")
        exp_ready = sem("exp_ready")
        onehot_ready = sem("onehot_ready")
        count_done = sem("count_done")
        slots_ready = sem("slots_ready")
        tokens_marked = sem("tokens_marked")
        tokens_found = sem("tokens_found")
        slot_idx_ready = sem("slot_idx_ready")
        table_ready = sem("table_ready")
        xg_ready = sem("xg_ready")
        gather_free = sem("gather_free")
        xgT_done = sem("xgT_done")
        silu_ready = sem("silu_ready")
        act_ready = sem("act_ready")
        actT_done = sem("actT_done")
        y_out_done = sem("y_out_done")
        last_y_half = sem("last_y_half")
        y_stored = sem("y_stored")
        y_zeroed = sem("y_zeroed")
        yg_ready = [[sem(f"yg_ready{b}_{k}") for k in range(2)] for b in range(4)]
        yg_scaled = sem("yg_scaled")
        moe_ready = sem("moe_ready")
        share_ready = sem("share_ready")
        x2_ready = sem("x2_ready")
        last_x2_ready = sem("last_x2_ready")
        out_ready = sem("out_ready")
        out_stored = sem("out_stored")
        dve_step = sem("dve_step")
        act_step = sem("act_step")

        route_at = [12288]

        def routing(*dims):
            route_at[0] += int(np.prod(dims))
            return carve(region_b, route_at[0] - int(np.prod(dims)), *dims)

        logits = routing(NTILE, NR)
        rank4 = routing(4)
        valid = routing(NTILE)
        gdiff, eq4, tmp4, gone, sel, one_a, one_b, exp_g = (routing(NTILE, 4) for _ in range(8))
        col1 = routing(NTILE, 6)
        work16 = routing(NTILE, NE)
        slotbase = routing(NTILE, NE)
        share = routing(2, NTILE)
        slot_f = routing(2, NTILE)
        tiles16, scan_a, scan_b = (routing(8 + NE) for _ in range(3))
        tile_f = routing(MAX_TILES)
        ended = routing(MAX_TILES, NE)
        slot_tile = routing(CHOICES)
        slot_row = routing(CHOICES)
        tok_found = routing(2, LISTED)
        slot_no_f = carve(region_b, 3072, P)
        in_row = carve(region_b, 3072 + P, NTILE * P).bitcast(BF16).rearrange("p (c s) -> p c s", s=P)
        onehot = routing(2, NTILE, NE)
        exp_in = (gdiff, col1[:, :, 2])
        exp_out = (exp_g, col1[:, :, 5])

        def rows(i):
            return P if i < NP // P else ND

        def halves(m):
            return ps[:, 2 * m:2 * m + 2, 0:HT]

        def split(ap):
            return ap.rearrange("p (h t) -> p h t", h=2)

        def z_complete(g, m):
            return (z_done, 3 * g + m + 1) if m < 3 else (quarter_used, N_IN + 4 * g + 4)

        def unit_done(n):
            if n < 12:
                return mix_done, n + 1
            t = n - 12
            return (mix_done, 12 + t // 2 + 1) if t % 2 == 0 else (quarter_used, splits(N_MIX + 1 + t // 2))

        row_loads = [
            (params[R_TAPS:R_TAPS + CK, :], conf_dw[0]),
            (params[R_STAPS:R_STAPS + SK, :], sc_dw[0]),
            (params[R_CB:R_CB + 1, :], conf_dw_b),
            (params[R_LG:R_LG + 1, :], conf_ln_g),
            (params[R_LB:R_LB + 1, :], conf_ln_b),
            (params[R_N1:R_N1 + 2, :], norm1_g.rearrange("a (h c) -> (a h) c", h=2)),
            (params[R_PS:R_PS + 2, :], pool_scale.rearrange("a (h c) -> (a h) c", h=2)),
            (conf_raw[0:120, 0, :], state_conf[0, 0:4].rearrange("s r c -> (s r) c")),
            (conf_raw[0:120, 1, :], state_conf[0, 4:8].rearrange("s r c -> (s r) c")),
            (pool_raw[0:120, :], state_pool[0].rearrange("s r c -> (s r) c")),
            (sconv_raw[0:16, :], state_sconv[0].rearrange("s r c -> (s r) c")),
        ]

        block = ctx.enter_context(nc.Block())

        @block.sync
        def _(sp):
            ada_v = w_ada[0].rearrange("(k p) n -> p k n", p=P)
            in_v = w_in[0].rearrange("(k p) n -> p k n", p=P)
            wo_v = w_o[0].rearrange("(k p) n -> p k n", p=P)

            sp.dma_start(c_raw[0:ND, :], c_sample).then_inc(ld_c, 16)
            sp.dma_start(c_raw[ND:ND + 1, :], c_prompt).then_inc(ld_c, 16)

            def load(n, k, src):
                place, ready, _ = raw_place(n)
                sp.dma_start(place.rearrange("p (k n) -> p k n", k=k), src).then_inc(ready, 16)

            def column_group(view, first_n, i):
                for q in range(TURN):
                    sp.wait_ge(hi_done, TURN * i + (first_n + q - RAW + 1))
                    sp.wait_ge(lo_done, TURN * i + (first_n + q - RAW + 1))
                    g, k = q // 4, 2 * (q % 4)
                    load(first_n + q, 2, view[:, k:k + 2, bass.ds(i * (3 * COLS) + g * COLS, COLS)])

            for n in range(TURN):
                if n == RAW:
                    sp.dma_start(mod, b_ada[0].partition_broadcast(ND + 1)).then_inc(ld_mod, 16)
                    for dst, src in row_loads:
                        sp.dma_start(dst, src).then_inc(ld_rows, 16)
                    for i in range(NP // P):
                        sp.dma_start(x_in[:, i, :], x_prompt[0, i * P:(i + 1) * P, :]).then_inc(ld_x, 16)
                    sp.dma_start(x_in[0:ND, 4, :], x_sample.rearrange("b t d -> (b t) d")).then_inc(ld_x, 16)
                if n >= RAW:
                    sp.wait_ge(hi_done, n - RAW + 1)
                    sp.wait_ge(lo_done, n - RAW + 1)
                k = 2 * (n % 4)
                load(n, 2, ada_v[:, k:k + 2, n // 4 * COLS:(n // 4 + 1) * COLS])
            with sp.Fori(1, G_ADA // 3) as i:
                column_group(ada_v, 0, i)
            with sp.Fori(0, G_IN // 3) as i:
                column_group(in_v, N_IN, i)

            def free(n):
                if n - RAW == N_MIX:
                    sp.wait_ge(mix_done, 11)
                else:
                    sp.wait_ge(hi_done, splits(n - RAW))
                    sp.wait_ge(lo_done, splits(n - RAW))

            free(N_MIX)
            load(N_MIX, 4, pool_w[0].rearrange("g p n -> p g n"))
            for b, w in enumerate((sc_out, conf_pw)):
                for q in range(4):
                    n = N_MIX + 1 + 4 * b + q
                    free(n)
                    col = 256 * ((q + 2 * b) % 4)
                    load(n, KW, w[0].rearrange("(k p) n -> p k n", p=P)[:, :, col:col + 256])
            for h in range(2):
                for q in range(4):
                    n = N_WO + 4 * h + q
                    free(n)
                    k = MERGE_ORDER[2 * q]
                    load(n, 2, wo_v[:, k:k + 2, h * COLS:(h + 1) * COLS])

            def turn_free(c, j):
                if j is not None:
                    sp.wait_ge(hi_done, TURN * j + (splits(N_EXP + c) - TURN))
                    sp.wait_ge(lo_done, TURN * j + (splits(N_EXP + c) - TURN))
                elif c < RAW:
                    free(N_EXP + c)
                elif c == RAW:
                    sp.wait_ge(logits_ready, NTILE)
                    sp.wait_ge(h2T_ready, NTILE)

            def up_weights(c, wx, e, j):
                for q in range(4):
                    turn_free(c + q, j)
                    load(N_EXP + c + q, 2, wx[0, bass.ds(e, 1), 2 * q * P:(2 * q + 2) * P, :].rearrange("a (k p) n -> p (a k) n", p=P))

            def down_weights(c, _, e, j):
                for q in range(KF):
                    turn_free(c + q, j)
                    load(N_EXP + c + q, 1, exp_w2[0, bass.ds(e, 1), q * P:(q + 1) * P, :].rearrange("a p n -> p a n"))

            def where_fresh(loads, c, wx, at, j, flags):
                fresh = sp.value_load(fresh_flags[0:1, flags, at], min_val=0, max_val=1)
                e = expert_of(at)
                with sp.If(fresh != 0):
                    loads(c, wx, e, j)
                with sp.If(fresh == 0):
                    for q in range(4):
                        turn_free(c + q, j)
                        _, ready, _ = raw_place(N_EXP + c + q)
                        sp.dma_start(kept_mark[0:1, c + q:c + q + 1], table[0:1, 0:1]).then_inc(ready, 16)

            def expert_of(at):
                return sp.value_load(tile_expert[0:1, at], min_val=0, max_val=NE - 1)

            up_weights(0, exp_w1, 0, None)
            up_weights(4, exp_w3, 0, None)
            sp.wait_ge(table_ready, 6)
            last = sp.value_load(table[0:1, 1:2], min_val=NE - 1, max_val=MAX_TILES - 1)
            before_last = sp.value_load(table[0:1, 2:3], min_val=NE - 2, max_val=MAX_TILES - 2)
            sp.wait_ge(xg_ready, 16)
            up_weights(8, exp_w1, expert_of(slice(1, 2)), None)
            with sp.Fori(1, last) as j:
                where_fresh(up_weights, 0, exp_w3, bass.ds(j, 1), j, 1)
                where_fresh(down_weights, 4, None, bass.ds(j - 1, 1), j, 0)
                where_fresh(up_weights, 8, exp_w1, bass.ds(j + 1, 1), j, 0)
            where_fresh(up_weights, 0, exp_w3, bass.ds(last, 1), last, 1)
            where_fresh(down_weights, 4, None, bass.ds(before_last, 1), last, 0)
            down_weights(8, None, expert_of(bass.ds(last, 1)), last)
            for i in range(NTILE):
                sp.wait_ge(out_ready, i + 1)
                dst = y_prompt[0, i * P:(i + 1) * P, :] if i < NP // P else y_sample.rearrange("b t d -> (b t) d")
                sp.dma_start(dst, x1[0:rows(i), i, :]).then_inc(out_stored, 16)

        @block.tensor
        def _(pe):
            def three(out, pairs, moving, start, stop):
                pe.matmul(out, pairs[0], moving[0], start=start, stop=False)
                pe.matmul(out, pairs[0], moving[1], start=False, stop=False)
                return pe.matmul(out, pairs[1], moving[0], start=False, stop=stop)

            def split_weights(n, k):
                return slot(w_hi, split_slot(n), k), slot(w_lo, split_slot(n), k)

            for m in range(4):
                pe.sem_inc(set_free[m], 1)
            pe.sem_inc(y_out_done, 1)
            pe.sem_inc(y_stored, 1)
            pe.wait_ge(const_ready, 2)
            pe.wait_ge(silu_c_ready, 1)
            for k in range(KD):
                t = pe.transpose(ps[:, 0, 9 * k:9 * k + 9], c_raw[0:ND + 1, k * P:(k + 1) * P], ident[0:ND + 1, 0:ND + 1])
            t.then_inc(turned, 1)

            pe.wait_ge(cT_split, 2)
            for n in range(N_IN):
                g, q = n // 4, n % 4
                pe.wait_ge(lo_done, n + 1)
                if q == 0 and g >= 3:
                    pe.wait_ge(mod_ready, g - 2)
                hi, lo = split_weights(n, 2)
                for k in range(2):
                    x = (cT_hi[:, 2 * q + k, :], cT_lo[:, 2 * q + k, :])
                    m = three(ps[0:16, 5 + g % 3, :], x, (hi[:, k, :], lo[:, k, :]), q == 0 and k == 0, q == 3 and k == 1)
                m.then_inc(quarter_used, 1)
                if n == Q_PARAMS:
                    pe.wait_ge(ld_rows, 16 * len(row_loads))
                    for c in range(KW):
                        cs = slice(c * P, (c + 1) * P)
                        pe.transpose(ps[:, 1, c * N_PARAM:(c + 1) * N_PARAM], params[:, cs], ident[0:N_PARAM, 0:N_PARAM])
                        pe.transpose(ps[:, 1, 256 + 16 * c:272 + 16 * c], sconv_raw[0:16, cs], ident[0:16, 0:16])
                        for h in range(2):
                            o = 240 * (c % 2) + 120 * h
                            pe.transpose(ps[:, 2 + c // 2, o:o + 120], conf_raw[0:120, h, cs], ident[0:120, 0:120])
                        t = pe.transpose(ps[:, 4, 120 * c:120 * c + 120], pool_raw[0:120, cs], ident[0:120, 0:120])
                    t.then_inc(turned, 1)
                elif n == Q_SCALE:
                    pe.wait_ge(mod_ready, 4)
                    pe.wait_ge(turned_out, 4)
                    for k in range(2 * KD):
                        t = pe.transpose(ps[:, 0, 9 * k:9 * k + 9], mod[:, k * P:(k + 1) * P], ident[0:ND + 1, 0:ND + 1])
                    t.then_inc(modT_done, 1)
                elif n == Q_SCALE + 1:
                    pe.wait_ge(xn_ready, NTILE)
                    for k in range(KD):
                        t = pe.transpose(ps[:, 1, 8 * k:8 * k + 8], x_in[0:ND, 4, k * P:(k + 1) * P], ident[0:ND, 0:ND])
                    t.then_inc(xT_done, 1)
                elif Q_TURN <= n < Q_TURN + KD:
                    k = n - Q_TURN
                    if k >= 3:
                        pe.wait_ge(hT_raw, max(1, k - 3))
                    for i in range(NP // P):
                        t = pe.transpose(ps[:, (2 + k) % 5, i * P:(i + 1) * P], x_in[:, i, k * P:(k + 1) * P], ident[:, :])
                    t.then_inc(xT_done, 1)

            pe.wait_ge(hT_lo_done, KD + 1)
            with pe.Fori(0, G_IN // 3) as i:
                for n in range(TURN):
                    g, q = n // 4, n % 4
                    pe.wait_ge(lo_done, TURN * i + splits(N_IN + n))
                    hi, lo = split_weights(N_IN + n, 2)
                    for m in range(4):
                        ms = slice(m * P, (m + 1) * P)
                        if q == 0:
                            pe.wait_ge(set_free[m], 3 * i + g + 1)
                            if m >= 2 and g == 0:
                                pe.wait_ge(mod_ready, G_ADA + m - 3)
                        for k in range(2):
                            kk = 2 * q + k
                            first, final = kk == 0, kk == KD - 1
                            for w, x, start, stop in ((hi, hT_hi, first, False), (hi, hT_lo, False, False), (lo, hT_hi, False, final)):
                                for h in range(2):
                                    mm = pe.matmul(ps[:, 2 * m + h, 0:HT], w[:, k, ms], x[:, kk, h * HT:(h + 1) * HT], start=start, stop=stop)
                        if q == 3 and m < 3:
                            mm.then_inc(z_done, 1)
                    mm.then_inc(quarter_used, 1)

            unit = [0]

            def next_set():
                s = unit[0] % 4
                pe.wait_ge(set_free[s], 1 + G_IN + unit[0] // 4)
                unit[0] += 1
                return s

            def product(s, lhs, rhs, n):
                for k in range(n):
                    for h in range(2):
                        mm = pe.matmul(ps[:, 2 * s + h, 0:HT], lhs(k), rhs(k)[:, h * HT:(h + 1) * HT], start=(k == 0), stop=(k == n - 1))
                return mm.then_inc(mix_done, 1)

            def raw_weights(n, k):
                pe.wait_ge(raw_ready[n % RAW], 16 * (n // RAW + 1))
                return slot(raw, n % RAW, k)

            pe.wait_ge(conv_ready, 1)
            product(next_set(), lambda k: ones_w[:, :], lambda k: va[:, k, :], KW)
            s = next_set()
            for c in range(KW):
                pe.transpose(ps[0:38, 2 * s, c * P:(c + 1) * P], ua[:, c, UA - 38:UA], ident[:, :])
                t = pe.transpose(ps[0:23, 2 * s + 1, c * P:(c + 1) * P], ub[:, c, UB - 23:UB], ident[:, :])
            t.then_inc(mix_done, 1)
            s = next_set()
            pe.wait_ge(branch_c, KW)
            for c in range(KW):
                t = pe.transpose(ps[0:10, 2 * s, c * P:(c + 1) * P], uc[:, c, UC - 10:UC], ident[:, :])
            t.then_inc(mix_done, 1)
            pe.wait_ge(branch_b, len(WINDOWS))
            w = raw_weights(N_MIX, 4)
            for j in range(KD):
                g = j // 2
                product(next_set(), lambda k: w[:, g, (j % 2) * P:(j % 2 + 1) * P], lambda k: pooled[:, g, :], 1)
            pe.wait_ge(sq_ready, 1)
            product(next_set(), lambda k: ones_w[:, :], lambda k: squares[:, k, :], KW)
            for t in range(2 * KD):
                n = N_MIX + 1 + t // 2
                if t == 0:
                    pe.wait_ge(sbr_lo_done, KW)
                if t % 2 == 0:
                    pe.wait_ge(lo_done, splits(n))
                s = next_set()
                w_h, w_l = split_weights(n, KW)
                for k in range(KW):
                    kk = k + (KW if t < KD else 0)
                    if t == KD:
                        pe.wait_ge(va_lo_done, k + 1)
                    for w, x, start, stop in ((w_h, hT_hi, k == 0, False), (w_h, hT_lo, False, False), (w_l, hT_hi, False, k == KW - 1)):
                        for h in range(2):
                            mm = pe.matmul(ps[:, 2 * s + h, 0:HT], w[:, k, (t % 2) * P:(t % 2 + 1) * P], x[:, kk, h * HT:(h + 1) * HT], start=start, stop=stop)
                mm.then_inc(unit_done(12 + t)[0], 1)

            def w_o_part(out, i, q, k, w):
                n = rows(i)
                hi, lo = w
                kk = MERGE_ORDER[2 * q + k]
                x = (hT_hi[:, kk, i * P:i * P + n], hT_lo[:, kk, i * P:i * P + n])
                return three(out, x, (hi[:, k, :], lo[:, k, :]), q == 0 and k == 0, q == 3 and k == 1)

            for q in range(4):
                pe.wait_ge(lo_done, splits(N_WO + q))
                for k in range(2):
                    pe.wait_ge(m_lo_done, 2 * q + k + 1)
                    if q == k == 0:
                        for m in range(4):
                            pe.wait_ge(set_free[m], 1 + G_IN + 7)
                    for i in range(NTILE):
                        mm = w_o_part(ps[0:rows(i), i, :], i, q, k, split_weights(N_WO + q, 2))
                mm.then_inc(quarter_used, 1)

            def w_o_tile(i):
                if i >= 2:
                    pe.wait_ge(t_ready, i - 1)
                for q in range(4):
                    pe.wait_ge(lo_done, splits(N_WO + 4 + q))
                    for k in range(2):
                        mm = w_o_part(ps[0:rows(i), 5 + i % 2, :], i, q, k, split_weights(N_WO + 4 + q, 2))
                    if i == NTILE - 1:
                        mm.then_inc(quarter_used, 1)
                if i < NTILE - 1:
                    mm.then_inc(wo_done, 1)

            def router_turn(i):
                n = rows(i)
                pe.wait_ge(h2_ready, i + 1)
                if i >= 1:
                    pe.wait_ge(h2T_ready, i)
                for k in range(KD):
                    t = pe.transpose(ps[:, (i, 7)[k // 4], (k % 4) * P:(k % 4) * P + n], h2[i % 3][0:n, k * P:(k + 1) * P], ident[0:n, 0:n])
                t.then_inc(h2T_done, 1)

            def router_logits(i):
                n = rows(i)
                pe.wait_ge(h2T_ready, i + 1)
                for k in range(KD):
                    mm = pe.matmul(ps[0:n, i, 0:NR], h2T[:, k, 0:n], wrouter[:, k, :], start=(k == 0), stop=(k == KD - 1))
                mm.then_inc(logit_done, 1)

            pe.wait_ge(ld_router, 64)
            for i in range(NTILE + 2):
                if i < NTILE:
                    w_o_tile(i)
                if i >= 3:
                    router_logits(i - 3)
                if i >= 2:
                    router_turn(i - 2)
            router_logits(NTILE - 1)

            pe.wait_ge(onehot_ready, 1)
            oh = onehot_both
            for i in range(NTILE):
                for j in range(i + 1):
                    pe.matmul(ps[:, 7, i * NE:(i + 1) * NE], (before if j == i else ones16)[:, :], oh[:, j, :], start=(j == 0), stop=(j == i))
            for j in range(NTILE):
                mm = pe.matmul(ps[:, 7, NTILE * NE:(NTILE + 1) * NE], ones16[:, :], oh[:, j, :], start=(j == 0), stop=(j == NTILE - 1))
            mm.then_inc(count_done, 1)

            def turn_rows(j):
                pe.wait_ge(xg_ready, 16 * j + 16)
                for k in range(KD):
                    t = pe.transpose(ps[:, 2 + k // 4, (k % 4) * P:(k % 4 + 1) * P], xg[:, k * P:(k + 1) * P], ident[:, :])
                t.then_inc(xgT_done, 1)

            def up(c, j, bank):
                for q in range(4):
                    n = N_EXP + c + q
                    pe.wait_ge(lo_done, TURN * j + splits(n))
                    hi, lo = split_weights(n, 2)
                    for k in range(2):
                        kk = 2 * q + k
                        mm = three(ps[:, bank, :], (xgT_hi[:, kk, :], xgT_lo[:, kk, :]), (hi[:, k, :], lo[:, k, :]), kk == 0, kk == KD - 1)
                    mm.then_inc(quarter_used, 1)

            def down(c, j):
                for q in range(KF):
                    n = N_EXP + c + q
                    pe.wait_ge(lo_done, TURN * j + splits(n))
                    x = (actT_hi[:, q, :], actT_lo[:, q, :])
                    for h in range(2):
                        hs = slice(h * COLS, (h + 1) * COLS)
                        mm = three(ps[:, 4 + h, :], x, (w_hi[:, split_slot(n), hs], w_lo[:, split_slot(n), hs]), q == 0, q == KF - 1)
                    mm.then_inc(quarter_used, 1)

            def turn_product(j):
                pe.wait_ge(act_ready, j + 1)
                for k in range(KF):
                    t = pe.transpose(ps[:, 6, k * P:(k + 1) * P], act_t[:, k * P:(k + 1) * P], ident[:, :])
                t.then_inc(actT_done, 1)

            pe.wait_ge(tokens_marked, 3)
            for c in range(CHOICES):
                t = pe.matmul(ps[:, 7, 0:2 * LISTED], in_row[:, c, :], tile_parts[:, c, :, :].rearrange("p a m -> p (a m)"), start=(c == 0), stop=(c == CHOICES - 1))
            t.then_inc(tokens_found, 1)
            pe.wait_ge(table_ready, 6)
            last = pe.value_load(table[0:1, 1:2], min_val=NE - 1, max_val=MAX_TILES - 1)
            before_last = pe.value_load(table[0:1, 2:3], min_val=NE - 2, max_val=MAX_TILES - 2)
            turn_rows(0)
            pe.wait_ge(xgT_lo_done, 1)
            up(0, 0, 0)
            up(4, 0, 1)
            turn_rows(1)
            turn_product(0)
            pe.wait_ge(xgT_lo_done, 2)
            pe.wait_ge(silu_ready, 1)
            up(8, 0, 0)

            def w3_of(j):
                pe.wait_ge(act_ready, j)
                up(0, j, 1)

            def w2_of(c, turn, jn, y_before):
                pe.wait_ge(actT_lo_done, jn)
                pe.wait_ge(y_out_done, y_before + 1)
                down(c, turn)

            with pe.Fori(1, last) as j:
                w3_of(j)
                turn_rows(j + 1)
                w2_of(4, j, j, j - 1)
                turn_product(j)
                pe.wait_ge(xgT_lo_done, j + 2)
                pe.wait_ge(silu_ready, j + 1)
                up(8, j, 0)
            w3_of(last)
            w2_of(4, last, last, before_last)
            turn_product(last)
            w2_of(8, last, last + 1, last)

        @block.scalar
        def _(act):
            steps = [0]

            def link(ins):
                steps[0] += 1
                ins.then_inc(act_step, 1)
                act.wait_ge(act_step, steps[0])

            def hi(n, turn=None):
                place, ready, count = raw_place(n, turn)
                act.wait_ge(ready, count)
                if splits(n) > SPLIT or turn is not None:
                    act.wait_ge(quarter_used, splits(n) - SPLIT if turn is None else turn * TURN + (splits(n) - SPLIT))
                act.activation(w_hi[:, split_slot(n), :], place, ACT.Copy).then_inc(hi_done, 1)

            act.wait_ge(ld_c, 32)
            act.activation(c_raw[0:ND + 1, :], c_raw[0:ND + 1, :], ACT.Silu).then_inc(silu_c_ready, 1)
            act.wait_ge(turned_out, 1)
            act.activation(cT_hi[:, :, :], small[:, 0:16 * KD].rearrange("p (k s) -> p k s", k=KD), ACT.Copy).then_inc(cT_split, 1)
            for n in range(N_IN):
                hi(n)
                if n in range(Q_NORM, Q_ROOT, 2):
                    i = (n - Q_NORM) // 2
                    if i == 0:
                        act.wait_ge(ld_x, 16 * NTILE)
                        act.wait_ge(sums_ready, 1)
                    else:
                        act.wait_ge(ssq_ready, i)
                    act.activation(square_junk[0:rows(i), :], x_in[0:rows(i), i, :], ACT.Square, accum_out=sums[0:rows(i), 0, i:i + 1]).then_inc(ssq_ready, 1)
                elif n == Q_ROOT + 2:
                    act.wait_ge(ms_ready, 1)
                    act.activation(sums[:, 2, 0:NTILE], sums[:, 1, 0:NTILE], ACT.Sqrt).then_inc(root_ready, 1)
                elif Q_TURN + AHEAD + 2 <= n <= Q_TURN + AHEAD + KD + 2:
                    k = n - (Q_TURN + AHEAD + 2)
                    if k == 0:
                        act.wait_ge(hT_raw, 1)
                        act.activation(hT_hi[:, :, NP:NT], small[:, 0:64].rearrange("p (k s) -> p k s", k=KD), ACT.Copy).then_inc(hT_hi_done, 1)
                    else:
                        k -= 1
                        tmp = (tmp_a, tmp_b)[k % 2][:, 0:NP]
                        act.wait_ge(xT_done, k + 2)
                        if k >= 2:
                            act.wait_ge(hT_lo_done, k)
                        act.activation(tmp, ps[:, (2 + k) % 5, :], ACT.Identity, bias=shiftT[:, k, ND:ND + 1], scale=scaleT[:, k, ND:ND + 1]).then_inc(hT_raw, 1)
                        act.wait_ge(hT_raw, k + 2)
                        act.activation(hT_hi[:, k, 0:NP], tmp, ACT.Copy).then_inc(hT_hi_done, 1)
            for q in range(7):
                hi(N_IN + q)
                if q == 4:
                    act.wait_ge(mod_ready, G_ADA)
                    act.dma_start(mod_dram, mod[:, 2 * D:6 * D]).then_inc(mod_stored, 16)
            act.dma_start(wrouter[:, :, 0:NG], router_g[0].rearrange("(k p) n -> p k n", p=P)).then_inc(ld_router, 16)
            act.dma_start(wrouter[:, :, NG:NR], router_e[0].rearrange("(k p) n -> p k n", p=P)).then_inc(ld_router, 16)
            act.dma_start(rbias[:, 0:NG], router_g_b[0].partition_broadcast(P)).then_inc(ld_router, 16)
            act.dma_start(rbias[:, NG:NR], router_e_b[0].partition_broadcast(P)).then_inc(ld_router, 16)
            act.dma_start(conf_s[0, :, 0:CK - 2, :], state_conf[0, :, 1:CK - 1, :]).then_inc(out_stored, 16)
            act.dma_start(pool_s[0, :, 0:PB - 1, :], state_pool[0, :, 1:PB, :]).then_inc(out_stored, 16)
            act.dma_start(sconv_s[0, :, 0:SK - 2, :], state_sconv[0, :, 1:SK - 1, :]).then_inc(out_stored, 16)

            act.wait_ge(pads_ready, 1)
            for g in range(G_IN):
                if g == 9:
                    act.wait_ge(y_zeroed, 16 * (MAX_TILES - NE))
                for m in range(4):
                    if g == 5:
                        break
                    act.wait_ge(*z_complete(g, m))
                    if g == 0:
                        act.activation(split(ua[:, m, CK - 1:UA]), halves(m), ACT.Copy).then_inc(set_free[m], 1)
                    elif g == 1:
                        if m >= 2:
                            act.wait_ge(z_dve, m - 1)
                        act.activation(split(sig[:, m % 2, :]), halves(m), ACT.Sigmoid).then_inc(set_free[m], 1)
                    elif g == 2:
                        act.activation(split(ub[:, m, PB:UB]), halves(m), ACT.Copy).then_inc(set_free[m], 1)
                    elif g == 3:
                        act.activation(split(uc[:, m, SK - 1:UC]), halves(m), ACT.Copy).then_inc(set_free[m], 1)
                    elif g == 4:
                        act.activation(split(sbr[:, m, :]), halves(m), ACT.Copy).then_inc(set_free[m], 1)
                    else:
                        act.activation(split(gates[:, 4 * (g - 6) + m, :]), halves(m), ACT.Sigmoid).then_inc(set_free[m], 1)
                for q in range(4 * g + 7, min(4 * g + 11, 4 * G_IN)):
                    hi(N_IN + q)

            act.wait_ge(quarter_used, splits(N_MIX - 1))
            for c in range(KW):
                act.wait_ge(branch_c, c + 1)
                act.activation(hT_hi[:, KW + c, :], sbr[:, c, :], ACT.Copy).then_inc(sbr_hi_done, 1)
            hi(N_MIX + 1)
            act.wait_ge(mix_done, 3)
            act.activation(tail[0:38, 0, :], ps[0:38, 2, :], ACT.Copy).then_inc(tail_ready, 1)
            act.activation(tail[0:23, 1, :], ps[0:23, 3, :], ACT.Copy).then_inc(set_free[1], 1)
            act.activation(tail[0:10, 2, :], ps[0:10, 4, :], ACT.Copy).then_inc(set_free[2], 1)
            act.wait_ge(tail_ready, 1)
            act.wait_ge(set_free[1], 1 + G_IN + 1)
            act.wait_ge(set_free[2], 1 + G_IN + 1)
            for n, (own, last, new_p, new_s) in enumerate(((CK - 1, CK - 2, conf_p, conf_s), (PB, PB - 1, pool_p, pool_s), (SK - 1, SK - 2, sconv_p, sconv_s))):
                act.dma_start(new_p[0, 0], tail[0:own, n, :]).then_inc(out_stored, 16)
                act.dma_start(new_s[0, :, last, :], tail[own:own + ND, n, :]).then_inc(out_stored, 16)
            act.wait_ge(centred, KW - 1)
            act.wait_ge(set_free[0], 1 + G_IN + 1)
            for c in range(KW):
                s = act.activation(squares[:, c, :], va[:, c, :], ACT.Square)
            s.then_inc(sq_ready, 1)
            for q in range(2, 5):
                hi(N_MIX + q)
            act.wait_ge(ms_ready, 2)
            act.activation(tmp_b[:, 0:NT], tmp_a[:, 0:NT], ACT.Sqrt).then_inc(root_ready, 1)
            for c in range(KW + 1):
                if c < KW:
                    act.wait_ge(normed, c + 1)
                    act.activation(va[:, c, :], va[:, c, :], ACT.Silu, bias=pT[:, c, R_LB:R_LB + 1], scale=pT[:, c, R_LG:R_LG + 1]).then_inc(branch_a, 1)
                if c:
                    act.wait_ge(branch_a, c)
                    act.activation(hT_hi[:, c - 1, :], va[:, c - 1, :], ACT.Copy).then_inc(va_hi_done, 1)
            for q in range(5, 9):
                hi(N_MIX + q)
            for p, j in enumerate(MERGE_ORDER):
                act.wait_ge(merged, KD + p + 1)
                if p == 4:
                    act.wait_ge(*unit_done(27))
                act.activation(hT_hi[:, j, :], gates[:, KD + j, :], ACT.Copy).then_inc(m_hi_done, 1)
                if p in (0, 2, 3):
                    hi(N_WO + (p + 1) // 2)
            hi(N_WO + 3)
            act.wait_ge(m_lo_done, KD)
            act.wait_ge(mod_stored, 16)
            for n, dst in enumerate((G1, SH2, SC2, G2)):
                act.dma_start(bvec[:, dst, :], mod_dram[ND, n * D:(n + 1) * D].partition_broadcast(P)).then_inc(ld_bcast, 16)
            act.dma_start(n2b, norm2_g[0].partition_broadcast(P)).then_inc(ld_bcast, 16)
            act.dma_start(bvec[:, FG, :], final_g.partition_broadcast(P)).then_inc(ld_bcast, 16)
            act.wait_ge(out_stored, 16 * 9)
            for n, dst in enumerate((g1_dec, sh2_dec, sc2_dec, g2_dec)):
                act.dma_start(dst[0:ND, :], mod_dram[0:ND, n * D:(n + 1) * D]).then_inc(ld_dec, 16)
            for i in range(NP // P):
                act.dma_start(x1[:, i, :], x_prompt[0, i * P:(i + 1) * P, :]).then_inc(ld_x, 16)
            act.dma_start(x1[0:ND, 4, :], x_sample.rearrange("b t d -> (b t) d")).then_inc(ld_x, 16)
            for q in range(4, 8):
                hi(N_WO + q)

            def his(first, end, j=None):
                for c in range(first, end):
                    hi(N_EXP + c, j)

            def squares_of(i):
                n = rows(i)
                act.wait_ge(x1_ready, i + 1)
                act.activation(sq_row[0:n, :], x1[0:n, i, :], ACT.Square, accum_out=sums[0:n, 0, i:i + 1]).then_inc(ssq_ready, 1)

            def root_of(i):
                n = rows(i)
                act.wait_ge(ms_ready, 3 + i)
                act.activation(sums[0:n, 2, i:i + 1], sums[0:n, 1, i:i + 1], ACT.Sqrt).then_inc(root_ready, 1)

            def store_h2(i):
                n = rows(i)
                act.wait_ge(h2_ready, i + 1)
                act.dma_start(h2_dram[i * P:i * P + n, :], h2[i % 3][0:n, :]).then_inc(h2_stored[i % 3], 16)

            def turned_h2(i):
                n = rows(i)
                act.wait_ge(h2T_done, i + 1)
                if i >= 1:
                    act.wait_ge(logit_done, i)
                for half, bank in ((0, i), (1, 7)):
                    out = act.activation(h2T[:, 4 * half:4 * half + 4, 0:n],
                                         ps[:, bank, :].rearrange("p (k t) -> p k t", k=4)[:, :, 0:n], ACT.Copy)
                out.then_inc(h2T_ready, 1)

            for i in range(NTILE + 2):
                if i < NTILE:
                    squares_of(i)
                elif i == NTILE:
                    his(0, 2)
                if i >= 2:
                    turned_h2(i - 2)
                if 1 <= i <= NTILE:
                    store_h2(i - 1)
                if i < NTILE:
                    root_of(i)
            his(2, 4)
            for n in range(2):
                act.wait_ge(diff_ready, n + 1)
                act.activation(exp_out[n], exp_in[n], ACT.Exp).then_inc(exp_ready, 1)

            def silu_tile(j):
                act.wait_ge(quarter_used, TURN * j + splits(N_EXP - 1))
                act.wait_ge(act_ready, j)
                act.activation(silu_t, ps[:, 0, :], ACT.Silu).then_inc(silu_ready, 1)

            def turned_rows_out(j):
                act.wait_ge(xgT_done, j + 1)
                act.activation(xgT_hi, ps[:, 2:4, :].rearrange("p b (k t) -> p (b k) t", k=4), ACT.Copy).then_inc(xgT_hi_done, 1)

            def y_out(jm, used):
                act.wait_ge(quarter_used, used)
                act.wait_ge(y_stored, jm * 16 + 1)
                act.activation(split(y_t), ps[:, 4:6, :], ACT.Copy).then_inc(y_out_done, 1)

            def y_store(jn, jm):
                act.wait_ge(y_out_done, jn + 1)
                act.dma_start(y_dram[bass.ds(jm * P, P), :], y_t).then_inc(y_stored, 16)

            def turned_product_out(j):
                act.wait_ge(actT_done, j + 1)
                act.activation(actT_hi, ps[:, 6, :].rearrange("p (k t) -> p k t", k=KF), ACT.Copy).then_inc(actT_hi_done, 1)

            act.wait_ge(table_ready, 6)
            last = act.value_load(table[0:1, 1:2], min_val=NE - 1, max_val=MAX_TILES - 1)
            before_last = act.value_load(table[0:1, 2:3], min_val=NE - 2, max_val=MAX_TILES - 2)
            turned_rows_out(0)
            his(4, 8)
            act.wait_ge(quarter_used, splits(N_EXP + 3))
            act.activation(silu_t, ps[:, 0, :], ACT.Silu).then_inc(silu_ready, 1)
            his(8, 11)
            turned_rows_out(1)
            turned_product_out(0)
            his(11, 15)
            with act.Fori(1, last) as j:
                his(3, 4, j)
                silu_tile(j)
                his(4, 8, j)
                turned_rows_out(j + 1)
                his(8, 11, j)
                y_out(j - 1, TURN * j + splits(N_EXP + 7))
                turned_product_out(j)
                his(11, 12, j)
                y_store(j, j - 1)
                his(12, 15, j)
            his(3, 4, last)
            silu_tile(last)
            his(4, 11, last)
            y_out(before_last, TURN * last + splits(N_EXP + 7))
            y_store(last, before_last)
            turned_product_out(last)
            his(11, 12, last)
            act.wait_ge(quarter_used, TURN * last + splits(N_EXP + 11))
            act.wait_ge(y_stored, 16 * last + 1)
            act.activation(y_t[:, 0:COLS], ps[:, 4, :], ACT.Copy).then_inc(y_out_done, 1)
            act.wait_ge(last_y_half, 1)
            y_store(last + 1, last)
            act.wait_ge(share_ready, 1)
            act.activation(sums[:, 2, 0:1], sums[:, 1, 0:1], ACT.Sqrt)

            def scale_first(i):
                n = rows(i)
                act.wait_ge(yg_ready[i % 4][0], 16 * (i // 4 + 1))
                act.activation(yg[i % 4][0:n, 0, :], yg[i % 4][0:n, 0, :], ACT.Copy, scale=share[0:n, 0, i:i + 1]).then_inc(yg_scaled, 1)

            for i in range(NTILE + 2):
                if i < NTILE:
                    scale_first(i)
                if i >= 2:
                    t = i - 2
                    n = rows(t)
                    act.wait_ge(*((x2_ready, t + 1) if t < NTILE - 1 else (last_x2_ready, 1)))
                    act.activation(sq_row[0:n, :], x1[0:n, t, :], ACT.Square, accum_out=sums[0:n, 0, NTILE + t:NTILE + t + 1]).then_inc(ssq_ready, 1)
                    act.wait_ge(ms_ready, 3 + NTILE + t)
                    act.activation(sums[0:n, 2, NTILE + t:NTILE + t + 1], sums[0:n, 1, NTILE + t:NTILE + t + 1], ACT.Sqrt).then_inc(root_ready, 1)
            act.wait_ge(out_stored, 16 * (3 + 6 + NTILE))

        @block.gpsimd
        def _(pool):
            pool.memset(ident[:, :], 0.0).then_inc(pool_chain, 1)
            pool.memset(before[:, :], 1.0).then_inc(pool_chain, 1)
            pool.memset(ones_w[:, :], 1.0 / W).then_inc(pool_chain, 1)
            pool.memset(ones16[:, :], 1.0).then_inc(pool_chain, 1)
            pool.iota(tok_id[:, :], [[0, 1]], base=0, channel_multiplier=1).then_inc(pool_chain, 1)
            pool.iota(tile_no[:, :], [[1, LISTED + 1]], base=0, channel_multiplier=0).then_inc(pool_chain, 1)
            pool.iota(slot_no[:, :], [[1, P]], base=0, channel_multiplier=0).then_inc(pool_chain, 1)
            pool.wait_ge(pool_chain, 7)
            pool.affine_select(out=ident[:, :], in_=ident[:, :], compare_op=ALU.not_equal, fill=1.0, base=0,
                               pattern=[[-1, P]], channel_multiplier=1).then_inc(const_ready, 1)
            pool.affine_select(out=before[:, :], in_=before[:, :], compare_op=ALU.is_gt, fill=0.0, base=0,
                               pattern=[[1, P]], channel_multiplier=-1).then_inc(const_ready, 1)

            def branch_rest(first, branch, hi_ready, signal):
                for c in range(KW):
                    pool.wait_ge(hi_ready, c + 1)
                    pool.tensor_tensor(hT_lo[:, first + c, :], branch[:, c, :], hT_hi[:, first + c, :].bitcast(F32), ALU.subtract).then_inc(signal, 1)

            pool.wait_ge(set_free[0], 1 + 1)
            pool.memset(zeros, 0.0).then_inc(pool_chain, 1)
            pool.wait_ge(pool_chain, 8)
            for t in range(NE, MAX_TILES):
                pool.dma_start(y_dram[t * P:(t + 1) * P, :], zeros).then_inc(y_zeroed, 16)

            branch_rest(KW, sbr, sbr_hi_done, sbr_lo_done)
            branch_rest(0, va, va_hi_done, va_lo_done)
            for p in range(3):
                pool.wait_ge(h2_stored[p], 16 * ((NTILE + 2 - p) // 3))

            def gather(j):
                pool.wait_ge(slot_idx_ready, j + 1)
                pool.sem_inc(gather_free, 1)
                pool.indirect_dma_start(xg, None, h2_dram, bass.IndirectOffsetOnAxis(ap=slot_idx[:, :], axis=0)).then_inc(xg_ready, 16)

            gather(0)
            pool.wait_ge(table_ready, 6)
            n_tiles = pool.value_load(table[0:1, 0:1], min_val=NE, max_val=MAX_TILES)
            with pool.Fori(1, n_tiles) as j:
                pool.wait_ge(xgT_done, j)
                gather(j)
            pool.wait_ge(slots_ready, 1)
            pool.wait_ge(y_stored, 16 * n_tiles + 1)
            pool.sem_inc(gather_free, 1)
            for i in range(NTILE):
                n = rows(i)
                if i >= 4:
                    pool.wait_ge(x2_ready, 1)
                for k in range(2):
                    pool.indirect_dma_start(yg[i % 4][0:n, k, :], None, y_dram, bass.IndirectOffsetOnAxis(ap=slot_i[0:n, k, i:i + 1], axis=0)).then_inc(yg_ready[i % 4][k], 16)
                if i >= 3:
                    for t in ((0,) if i == 3 else range(1, NTILE - 1)):
                        pool.wait_ge(moe_ready, t + 1)
                        pool.tensor_tensor(x1[0:rows(t), t, :], x1[0:rows(t), t, :], yg[t % 4][0:rows(t), 1, :], ALU.add).then_inc(x2_ready, 1)

        @block.vector
        def _(dve):
            steps = [0]

            def link(ins, signal=None, value=0):
                if signal is None:
                    steps[0] += 1
                ins.then_inc(dve_step if signal is None else signal, 1)
                dve.wait_ge(dve_step if signal is None else signal, steps[0] if signal is None else value)

            def rsqrt(ms, root, out, tmp, n_root):
                dve.wait_ge(root_ready, n_root)
                link(dve.reciprocal(out, root))
                link(dve.tensor_tensor(tmp, out, out, ALU.mult))
                link(dve.tensor_tensor(tmp, tmp, ms, ALU.mult))
                link(dve.tensor_scalar(tmp, tmp, -0.5, 1.5, ALU.mult, ALU.add))
                link(dve.tensor_tensor(out, out, tmp, ALU.mult))

            dve.memset(sums[:, :, :], 1.0).then_inc(sums_ready, 1)
            for t in range(16):
                dve.memset(rcount[:, t:t + 1], 1.0 / (t + 1))
            link(dve.memset(tok_parts[:, :, :], 0.0))
            for t in range(NTILE):
                dve.memset(tok_parts[0:rows(t), t, 0:1], float(t))
            dve.wait_ge(const_ready, 2)
            for t in range(NTILE):
                dve.tensor_copy(tok_parts[0:rows(t), t, 1:2], tok_id[0:rows(t), 0:1])

            def rest(out, whole, first):
                return dve.tensor_tensor(out, whole, first.bitcast(F32), ALU.subtract)

            def lo(n, turn=None):
                count = splits(n) if turn is None else turn * TURN + splits(n)
                dve.wait_ge(hi_done, count)
                rest(w_lo[:, split_slot(n), :], raw_place(n)[0], w_hi[:, split_slot(n), :]).then_inc(lo_done, 1)

            c_pad = small[:, 0:16 * KD].rearrange("p (k s) -> p k s", k=KD)
            link(dve.memset(small[:, :], 0.0))
            dve.wait_ge(turned, 1)
            link(dve.tensor_copy(c_pad[:, :, 0:ND + 1], ps[:, 0, 0:9 * KD].rearrange("p (k s) -> p k s", s=9)), turned_out, 1)
            dve.wait_ge(cT_split, 1)
            rest(cT_lo[:, :, :], c_pad, cT_hi[:, :, :]).then_inc(cT_split, 1)

            def mod_group(g):
                dve.wait_ge(quarter_used, 4 * g + 4)
                cols = mod[:, g * COLS:(g + 1) * COLS]
                dve.tensor_tensor(cols, ps[0:ND + 1, 5 + g % 3, :], cols, ALU.add).then_inc(mod_ready, 1)

            def params_out():
                dve.wait_ge(turned, 2)
                dve.tensor_copy(pT[:, :, :], ps[:, 1, 0:KW * N_PARAM].rearrange("p (c r) -> p c r", c=KW))
                dve.tensor_copy(sconvT[:, :, :, :], ps[:, 1, 256:320].rearrange("p (c s r) -> p c s r", c=KW, s=ND)).then_inc(turned_out, 1)
                for c in range(2):
                    dve.tensor_copy(confT[:, 2 * c:2 * c + 2, :, :].rearrange("p c s r -> p (c s r)"), ps[:, 2 + c, 0:480])
                dve.tensor_copy(poolT[:, :, :, :], ps[:, 4, 0:480].rearrange("p (c s r) -> p c s r", c=KW, s=ND)).then_inc(turned_out, 2)

            def mean_squares():
                dve.wait_ge(ssq_ready, NTILE)
                dve.tensor_scalar(sums[:, 1, 0:NTILE], sums[:, 0, 0:NTILE], 1.0 / D, EPS, ALU.mult, ALU.add).then_inc(ms_ready, 1)

            def norm_root():
                rsqrt(sums[:, 1, 0:NTILE], sums[:, 2, 0:NTILE], sums[:, 3, 0:NTILE], sums[:, 2, 0:NTILE], 1)

            def scale_out():
                dve.wait_ge(modT_done, 1)
                dve.tensor_copy(shiftT[:, :, :], ps[:, 0, 0:72].rearrange("p (k s) -> p k s", s=9))
                link(dve.tensor_scalar(scaleT[:, :, :], ps[:, 0, 72:144].rearrange("p (k s) -> p k s", s=9), 1.0, None, ALU.add))
                for h in range(2):
                    s = dve.tensor_tensor(scaleT[:, 4 * h:4 * h + 4, :], scaleT[:, 4 * h:4 * h + 4, :],
                                          pT[:, :, R_N1 + h:R_N1 + h + 1].broadcast_to([P, KW, ND + 1]), ALU.mult)
                    s.then_inc(scaleT_ready, 1)

            dec = small[:, 0:64].rearrange("p (k s) -> p k s", k=KD)

            def sampled_input():
                dve.wait_ge(xT_done, 1)
                dve.wait_ge(scaleT_ready, 2)
                link(dve.tensor_tensor(dec, ps[:, 1, 0:64].rearrange("p (k s) -> p k s", k=KD), scaleT[:, :, 0:ND], ALU.mult))
                dve.tensor_tensor(dec, dec, shiftT[:, :, 0:ND], ALU.add).then_inc(hT_raw, 1)

            def sampled_rest():
                dve.wait_ge(hT_hi_done, 1)
                rest(hT_lo[:, :, NP:NT], dec, hT_hi[:, :, NP:NT]).then_inc(hT_lo_done, 1)

            def prompt_rest(k):
                dve.wait_ge(hT_hi_done, k + 2)
                rest(hT_lo[:, k, 0:NP], (tmp_a, tmp_b)[k % 2][:, 0:NP], hT_hi[:, k, 0:NP]).then_inc(hT_lo_done, 1)

            for n in range(N_IN + 4):
                lo(n)
                if n == 7:
                    dve.wait_ge(ld_mod, 16)
                if n % 4 == 3 and n > 4:
                    mod_group(n // 4 - 1)
                i = n - Q_ROOT
                k = n - (Q_TURN + AHEAD + 1)
                if n == Q_PARAMS + AHEAD:
                    params_out()
                elif i == 0:
                    mean_squares()
                elif i == 2:
                    norm_root()
                elif 3 <= i < 6:
                    for t in range(2 * i - 6, min(2 * i - 4, NTILE)):
                        dve.tensor_scalar(x_in[0:rows(t), t, :], x_in[0:rows(t), t, :], sums[0:rows(t), 3, t:t + 1], None, ALU.mult).then_inc(xn_ready, 1)
                elif n == Q_SCALE + AHEAD:
                    scale_out()
                elif k == -1:
                    sampled_input()
                elif 0 <= k <= KD + 1:
                    if k == 1:
                        sampled_rest()
                    elif k > 1:
                        prompt_rest(k - 2)

            dve.wait_ge(mod_stored, 16)
            dve.memset(ua[:, :, 0:CK - 1], 0.0)
            dve.memset(ub[:, :, 0:PB], 0.0)
            dve.memset(uc[:, :, 0:SK - 1], 0.0).then_inc(pads_ready, 1)
            for q in range(4, 7):
                lo(N_IN + q)

            def glu():
                for m in range(4):
                    dve.wait_ge(set_free[m], 1 + 2)
                    dve.tensor_tensor(ua[:, m, CK - 1:UA], ua[:, m, CK - 1:UA], sig[:, m % 2, :], ALU.mult).then_inc(z_dve, 1)

            def taps(t):
                for c in range(KW):
                    w = pT[:, c, R_TAPS + t:R_TAPS + t + 1]
                    if t:
                        dve.wait_ge(conv_step, KW * (t - 1) + c + 1)
                        dve.scalar_tensor_tensor(va[:, c, 0:NP], ua[:, c, t:t + NP], w, va[:, c, 0:NP], ALU.mult, ALU.add).then_inc(conv_step, 1)
                    else:
                        dve.wait_ge(z_dve, c + 1)
                        dve.tensor_scalar(va[:, c, 0:NP], ua[:, c, 0:NP], w, pT[:, c, R_CB:R_CB + 1], ALU.mult, ALU.add).then_inc(conv_step, 1)

            def conv_sampled():
                prod = confT[:, :, :, :]
                for c in range(KW):
                    s = dve.tensor_tensor(prod[:, c, :, :], confT[:, c, :, :], pT[:, c:c + 1, 0:CK - 1].broadcast_to([P, ND, CK - 1]), ALU.mult)
                link(s)
                va_d, ua_d = va[:, :, NP:NT], ua[:, :, CK - 1 + NP:UA]
                dec = small[:, 64:96].rearrange("p (c s) -> p c s", c=KW)
                link(dve.tensor_reduce(va_d, prod, AX.X, ALU.add))
                link(dve.tensor_tensor(dec, ua_d, pT[:, :, CK - 1:CK].broadcast_to([P, KW, ND]), ALU.mult))
                link(dve.tensor_tensor(va_d, va_d, dec, ALU.add))
                dve.tensor_tensor(va_d, va_d, pT[:, :, R_CB:R_CB + 1].broadcast_to([P, KW, ND]), ALU.add).then_inc(conv_ready, 1)

            def pooling(g):
                w = WINDOWS[g]
                dve.wait_ge(set_free[g], 1 + 3)
                src, n = ub[:, g, 0:PB + NP], 1
                for dst in (tmp_a, tmp_b, tmp_a, tmp_b)[:g + 1]:
                    at = 2 * n - 1
                    link(dve.tensor_tensor(dst[:, at:PB + NP], src[:, at:PB + NP], src[:, at - n:PB + NP - n], ALU.add))
                    src, n = dst, 2 * n
                tok, tot, out = ub[:, g, PB:PB + NP], src[:, PB:PB + NP], pooled[:, g, 0:NP]
                link(dve.scalar_tensor_tensor(out, tot, 1.0 / w, tok, ALU.mult, ALU.subtract))
                link(dve.tensor_tensor(small[:, 0:w - 1], tot[:, 0:w - 1], rcount[:, 0:w - 1], ALU.mult))
                link(dve.tensor_tensor(out[:, 0:w - 1], small[:, 0:w - 1], tok[:, 0:w - 1], ALU.subtract))
                tok, out, tot = ub[:, g, PB + NP:UB], pooled[:, g, NP:NT], small[:, 32:40]
                link(dve.tensor_reduce(tot, poolT[:, g, :, PB - (w - 1):PB], AX.X, ALU.add))
                link(dve.tensor_tensor(tot, tot, tok, ALU.add))
                link(dve.scalar_tensor_tensor(out, tot, 1.0 / w, tok, ALU.mult, ALU.subtract), branch_b, g + 1)

            def times_s_c():
                for m in range(4):
                    dve.wait_ge(*z_complete(5, m))
                    dve.wait_ge(set_free[m], 1 + 5)
                    dve.tensor_tensor(split(uc[:, m, SK - 1:UC]), halves(m), split(uc[:, m, SK - 1:UC]), ALU.mult).then_inc(set_free[m], 1)

            def short_conv(m):
                dve.wait_ge(set_free[m], 1 + 6)
                tap = [pT[:, m, R_STAPS + t:R_STAPS + t + 1] for t in range(SK)]
                acc = tmp_a[:, 0:NP]
                link(dve.tensor_scalar(acc, uc[:, m, 0:NP], tap[0], None, ALU.mult))
                link(dve.scalar_tensor_tensor(acc, uc[:, m, 1:1 + NP], tap[1], acc, ALU.mult, ALU.add))
                link(dve.scalar_tensor_tensor(acc, uc[:, m, 2:2 + NP], tap[2], acc, ALU.mult, ALU.add))
                link(dve.tensor_tensor(sbr[:, m, 0:NP], sbr[:, m, 0:NP], acc, ALU.mult))
                acc = tmp_a[:, 0:ND]
                link(dve.tensor_scalar(acc, sconvT[:, m, :, 0:1].rearrange("p s r -> p (s r)"), tap[0], None, ALU.mult))
                link(dve.scalar_tensor_tensor(acc, sconvT[:, m, :, 1:2].rearrange("p s r -> p (s r)"), tap[1], acc, ALU.mult, ALU.add))
                link(dve.scalar_tensor_tensor(acc, uc[:, m, SK - 1 + NP:UC], tap[2], acc, ALU.mult, ALU.add))
                link(dve.tensor_tensor(sbr[:, m, NP:NT], sbr[:, m, NP:NT], acc, ALU.mult), branch_c, m + 1)

            for q in range(7, 4 * G_IN):
                if q == 11:
                    glu()
                if q == 27:
                    times_s_c()
                lo(N_IN + q)
                if 11 <= q < 11 + CK:
                    taps(q - 11)
                elif q == 11 + CK:
                    conv_sampled()
                elif 11 + CK < q <= 11 + CK + len(WINDOWS):
                    pooling(q - 12 - CK)
                if q >= 44:
                    short_conv(q - 44)
            dve.wait_ge(mix_done, 1)
            dve.wait_ge(conv_ready, 1)
            for c in range(KW):
                s = dve.tensor_tensor(split(va[:, c, :]), split(va[:, c, :]), halves(0), ALU.subtract)
                s.then_inc(centred if c < KW - 1 else set_free[0], 1)

            def unit(n):
                dve.wait_ge(*unit_done(n))
                return n % 4

            def free_at(n):
                return 1 + G_IN + n // 4 + 1

            for j in range(KD):
                s = unit(3 + j)
                dve.scalar_tensor_tensor(split(gates[:, KD + j, :]), halves(s), pT[:, j % 4, R_PS + j // 4:R_PS + j // 4 + 1], split(gates[:, KD + j, :]), ALU.mult, ALU.mult).then_inc(set_free[s], 1)
            lo(N_MIX + 1)
            s = unit(11)
            link(dve.tensor_scalar(split(tmp_b[:, 0:NT]), halves(s), EPS, None, ALU.add), set_free[s], free_at(11))
            dve.tensor_copy(tmp_a[:, 0:NT], tmp_b[:, 0:NT]).then_inc(ms_ready, 1)
            dve.wait_ge(ms_ready, 2)
            lo(N_MIX + 2)
            lo(N_MIX + 3)
            rsqrt(tmp_a[:, 0:NT], tmp_b[:, 0:NT], rstdT, tmp_b[:, 0:NT], 2)

            def merged_rest(p):
                dve.wait_ge(m_hi_done, p + 1)
                j = MERGE_ORDER[p]
                rest(hT_lo[:, j, :], gates[:, KD + j, :], hT_hi[:, j, :]).then_inc(m_lo_done, 1)

            def merge(t):
                first, j = (2 * KD, t) if t < KD else (0, MERGE_ORDER[t - KD])
                s = unit(12 + t)
                tmp = (tmp_a, tmp_b)[t % 2][:, 0:NT]
                link(dve.tensor_tensor(split(tmp), halves(s), split(gates[:, first + j, :]), ALU.mult), set_free[s], free_at(12 + t))
                dve.tensor_tensor(gates[:, KD + j, :], gates[:, KD + j, :], tmp, ALU.add).then_inc(merged, 1)

            for c in range(KW):
                if c in (0, 3):
                    merge(c // 3)
                dve.tensor_tensor(va[:, c, :], va[:, c, :], rstdT, ALU.mult).then_inc(normed, 1)
            lo(N_MIX + 4)
            for t in range(2, 2 * KD):
                merge(t)
                if KD < t <= KD + 4:
                    merged_rest(t - KD - 1)
                if t >= 3 and t % 2:
                    lo(N_MIX + 4 + t // 2)
            for p in range(4, KD):
                merged_rest(p)
            lo(N_WO + 3)

            dve.wait_ge(merged, 2 * KD)
            for r in range(4):
                dve.memset(rank4[:, r:r + 1], 4.0 - r)
            dve.memset(valid[:, 0:NTILE - 1], 1.0)
            link(dve.memset(valid[:, NTILE - 1:NTILE], 0.0))
            dve.memset(valid[0:ND, NTILE - 1:NTILE], 1.0)
            for pad in (tiles16, scan_a, scan_b):
                dve.memset(pad[:, 0:8], 0.0)
            link(dve.memset(logits[:, :, :], 0.0))
            for q in range(4, 8):
                lo(N_WO + q)
            dve.wait_ge(ld_bcast, 16 * 6)
            dve.wait_ge(ld_dec, 16 * 4)
            link(dve.scalar_tensor_tensor(bvec[:, SC2, :], bvec[:, SC2, :], 1.0, n2b, ALU.add, ALU.mult))
            link(dve.scalar_tensor_tensor(sc2_dec[0:ND, :], sc2_dec[0:ND, :], 1.0, n2b[0:ND, :], ALU.add, ALU.mult))
            dve.wait_ge(ld_x, 2 * 16 * NTILE)
            dve.wait_ge(ld_router, 64)

            def los(first, end, j=None):
                for c in range(first, end):
                    lo(N_EXP + c, j)

            def row_means(i, col, n_ssq, n_root):
                n = rows(i)
                dve.wait_ge(ssq_ready, n_ssq)
                link(dve.tensor_scalar(sums[0:n, 1, col:col + 1], sums[0:n, 0, col:col + 1], 1.0 / D, EPS, ALU.mult, ALU.add), ms_ready, n_root)

            def row_rsqrt(i, col, n_root):
                n = rows(i)
                ms, root, out = (sums[0:n, r, col:col + 1] for r in (1, 2, 3))
                dve.wait_ge(root_ready, n_root)
                link(dve.reciprocal(out, root))
                link(dve.scalar_tensor_tensor(root, out, ms, out, ALU.mult, ALU.mult))
                link(dve.tensor_scalar(root, root, -0.5, 1.5, ALU.mult, ALU.add))
                link(dve.tensor_tensor(out, out, root, ALU.mult))
                return out

            def logit_tile(i):
                n = rows(i)
                dve.wait_ge(logit_done, i + 1)
                dve.tensor_tensor(logits[0:n, i, :], ps[0:n, i, 0:NR], rbias[0:n, :], ALU.add).then_inc(logits_ready, 1)

            def residual(i):
                n = rows(i)
                dve.wait_ge(*((wo_done, i + 1) if i < NTILE - 1 else (quarter_used, splits(N_WO + 7))))
                g1 = bvec[0:n, G1, :] if i < NP // P else g1_dec[0:ND, :]
                dve.tensor_tensor(t_row[0:n, 0:COLS], ps[0:n, i, :], g1[:, 0:COLS], ALU.mult)
                link(dve.tensor_tensor(t_row[0:n, COLS:D], ps[0:n, 5 + i % 2, :], g1[:, COLS:D], ALU.mult), t_ready, i + 1)
                link(dve.tensor_tensor(x1[0:n, i, :], x1[0:n, i, :], t_row[0:n, :], ALU.add), x1_ready, i + 1)

            def second_norm(i):
                n = rows(i)
                r = row_rsqrt(i, i, 3 + i)
                if i >= 3:
                    dve.wait_ge(h2T_done, i - 2)
                    dve.wait_ge(h2_stored[i % 3], 16 * (i // 3))
                sc2 = bvec[0:n, SC2, :] if i < NP // P else sc2_dec[0:ND, :]
                link(dve.scalar_tensor_tensor(h2[i % 3][0:n, :], x1[0:n, i, :], r, sc2, ALU.mult, ALU.mult))
                shift = bvec[0:n, SH2, :] if i < NP // P else sh2_dec[0:ND, :]
                dve.tensor_tensor(h2[i % 3][0:n, :], h2[i % 3][0:n, :], shift, ALU.add).then_inc(h2_ready, 1)

            for i in range(NTILE + 1):
                if i < NTILE:
                    residual(i)
                if i:
                    second_norm(i - 1)
                if i < NTILE:
                    row_means(i, i, NTILE + i + 1, 3 + i)
                if i >= 3:
                    logit_tile(i - 3)
            dve.memset(fresh_flags[:, 0, 0:1], 1)
            dve.memset(fresh_flags[:, 1, 0:2], 1)
            dve.tensor_copy(tile_f, tile_no[:, 0:MAX_TILES])
            dve.tensor_scalar(tile_start[:, :], tile_no[:, :], float(P), None, ALU.mult)
            dve.tensor_copy(slot_no_f, slot_no[:, :])
            los(0, 2)
            logit_tile(NTILE - 2)
            logit_tile(NTILE - 1)
            dve.wait_ge(logits_ready, NTILE)

            def list_out(j):
                dve.tensor_copy(slot_idx[:, :], slot_tokens[:, j]).then_inc(slot_idx_ready, 1)

            T5 = [P, NTILE, 4]

            def first_of(eq, rank_tmp, out):
                link(dve.tensor_tensor(rank_tmp, eq, rank4[:, None, :].broadcast_to(T5), ALU.mult))
                link(dve.tensor_reduce(col1[:, :, 0], rank_tmp, AX.X, ALU.max))
                link(dve.tensor_tensor(out, rank_tmp, col1[:, :, 0:1].broadcast_to(T5), ALU.is_equal))

            glog, elog = logits[:, :, 0:NG], logits[:, :, NG:NR]
            link(dve.tensor_reduce(col1[:, :, 0], glog, AX.X, ALU.max))
            link(dve.tensor_tensor(gdiff, glog, col1[:, :, 0:1].broadcast_to(T5), ALU.subtract), diff_ready, 1)
            link(dve.tensor_scalar(eq4, gdiff, 0.0, None, ALU.is_equal))
            first_of(eq4, tmp4, gone)
            link(dve.tensor_tensor(gone, gone, valid[:, :, None].broadcast_to(T5), ALU.mult))
            e44 = elog.rearrange("p t (g j) -> p t g j", g=NG)
            w44 = work16.rearrange("p t (g j) -> p t g j", g=NG)
            link(dve.tensor_tensor(w44, e44, gone[:, :, :, None].broadcast_to([P, NTILE, NG, EG]), ALU.mult))
            link(dve.tensor_reduce(sel, work16.rearrange("p t (g j) -> p t j g", g=NG), AX.X, ALU.add))
            link(dve.tensor_reduce(col1[:, :, 1], sel, AX.X, ALU.max))
            link(dve.tensor_tensor(sel, sel, col1[:, :, 1:2].broadcast_to(T5), ALU.subtract))
            link(dve.tensor_scalar(eq4, sel, 0.0, None, ALU.is_equal))
            first_of(eq4, tmp4, one_a)
            link(dve.scalar_tensor_tensor(sel, one_a, -1.0e30, sel, ALU.mult, ALU.add))
            link(dve.tensor_reduce(col1[:, :, 2], sel, AX.X, ALU.max), diff_ready, 2)
            link(dve.tensor_tensor(eq4, sel, col1[:, :, 2:3].broadcast_to(T5), ALU.is_equal))
            first_of(eq4, tmp4, one_b)
            for one, oh in ((one_a, onehot[:, 0]), (one_b, onehot[:, 1])):
                link(dve.tensor_tensor(oh.rearrange("p t (g j) -> p t g j", g=NG), gone[:, :, :, None].broadcast_to([P, NTILE, NG, EG]),
                                       one[:, :, None, :].broadcast_to([P, NTILE, NG, EG]), ALU.mult))
            dve.tensor_tensor(onehot_both[:, :, :], onehot[:, 0], onehot[:, 1], ALU.add).then_inc(onehot_ready, 1)
            dve.wait_ge(count_done, 1)
            count, tiles = ps[:, 7, NTILE * NE:(NTILE + 1) * NE], tiles16[:, 8:]
            link(dve.tensor_scalar(tiles, count, float(P), 1.0, ALU.is_gt, ALU.add))
            for full in range(2, (NT + P - 1) // P):
                link(dve.scalar_tensor_tensor(tiles, count, float(full * P), tiles, ALU.is_gt, ALU.add))
            src = tiles16
            for s, dst in ((1, scan_a), (2, scan_b), (4, scan_a), (8, scan_b)):
                link(dve.tensor_tensor(dst[:, 8:], src[:, 8:], src[:, 8 - s:8 - s + NE], ALU.add))
                src = dst
            ends = src[:, 8:]
            link(dve.tensor_tensor(ended, ends[:, None, :].broadcast_to([P, MAX_TILES, NE]), tile_f[:, :, None].broadcast_to([P, MAX_TILES, NE]), ALU.is_le))
            link(dve.tensor_reduce(tile_f, ended, AX.X, ALU.add))
            dve.tensor_copy(tile_expert[:, :], tile_f).then_inc(table_ready, 1)
            for flags, first in ((0, 1), (1, 2)):
                dve.tensor_tensor(fresh_flags[:, flags, first:], tile_f[:, first:], tile_f[:, first - 1:MAX_TILES - 1], ALU.not_equal).then_inc(table_ready, 1)
            dve.tensor_scalar(table[:, 1:2], ends[:, NE - 1:NE], -1.0, None, ALU.add).then_inc(table_ready, 1)
            dve.tensor_scalar(table[:, 2:3], ends[:, NE - 1:NE], -2.0, None, ALU.add).then_inc(table_ready, 1)
            dve.tensor_copy(table[:, 0:1], ends[:, NE - 1:NE]).then_inc(table_ready, 1)
            start = scan_a[:, 8:]
            link(dve.tensor_tensor(start, ends, tiles, ALU.subtract))
            link(dve.scalar_tensor_tensor(slotbase, start[:, None, :].broadcast_to([P, NTILE, NE]), float(P),
                                          ps[:, 7, 0:NTILE * NE].rearrange("p (t e) -> p t e", e=NE), ALU.mult, ALU.add))
            link(dve.tensor_tensor(onehot, onehot, slotbase[:, None, :, :].broadcast_to([P, 2, NTILE, NE]), ALU.mult))
            link(dve.tensor_reduce(slot_f, onehot, AX.X, ALU.add))
            slots = slot_f.rearrange("p k t -> p (k t)")
            link(dve.tensor_tensor(begun[:, :, :], slots[:, :, None].broadcast_to([P, CHOICES, LISTED + 1]),
                                   tile_start[:, None, :].broadcast_to([P, CHOICES, LISTED + 1]), ALU.is_ge))
            link(dve.tensor_reduce(slot_tile, begun[:, :, 1:], AX.X, ALU.add))
            link(dve.scalar_tensor_tensor(slot_row, slot_tile, -float(P), slots, ALU.mult, ALU.add))
            dve.tensor_tensor(in_row, slot_row[:, :, None].broadcast_to([P, CHOICES, P]),
                              slot_no_f[:, None, :].broadcast_to([P, CHOICES, P]), ALU.is_equal).then_inc(tokens_marked, 1)
            link(dve.tensor_tensor(in_tile[:, :, :], begun[:, :, 0:LISTED], begun[:, :, 1:], ALU.subtract))
            for k in range(2):
                cs = slice(k * NTILE, (k + 1) * NTILE)
                dve.tensor_tensor(tile_parts[:, cs, :, :], in_tile[:, cs, None, :].broadcast_to([P, NTILE, 2, LISTED]),
                                  tok_parts[:, :, :, None].broadcast_to([P, NTILE, 2, LISTED]), ALU.mult).then_inc(tokens_marked, 1)
            dve.tensor_copy(slot_i[:, :, :], slot_f).then_inc(slots_ready, 1)
            dve.wait_ge(tokens_found, 1)
            link(dve.tensor_copy(tok_found, ps[:, 7, 0:2 * LISTED].rearrange("p (a m) -> p a m", a=2)))
            link(dve.scalar_tensor_tensor(slot_tokens[:, :], tok_found[:, 0, :], float(P), tok_found[:, 1, :], ALU.mult, ALU.add))
            list_out(slice(0, 1))
            los(2, 4)
            dve.wait_ge(exp_ready, 2)
            link(dve.tensor_reduce(col1[:, :, 3], exp_out[0], AX.X, ALU.add))
            link(dve.tensor_scalar(col1[:, :, 4], col1[:, :, 5], 1.0, None, ALU.add))
            link(dve.tensor_tensor(col1[:, :, 4], col1[:, :, 4], col1[:, :, 3], ALU.mult))
            link(dve.reciprocal(share[:, 0, :], col1[:, :, 4]))
            link(dve.tensor_tensor(share[:, 1, :], share[:, 0, :], col1[:, :, 5], ALU.mult), share_ready, 1)

            def product_tile(j, used):
                dve.wait_ge(quarter_used, used)
                dve.wait_ge(silu_ready, j + 1)
                dve.wait_ge(actT_done, j)
                dve.tensor_tensor(act_t, ps[:, 1, :], silu_t, ALU.mult).then_inc(act_ready, 1)

            def turned_rows_rest(j):
                dve.wait_ge(xgT_hi_done, j + 1)
                rest(xgT_lo, ps[:, 2:4, :].rearrange("p b (k t) -> p (b k) t", k=4), xgT_hi).then_inc(xgT_lo_done, 1)

            def turned_product_rest(j):
                dve.wait_ge(actT_hi_done, j + 1)
                rest(actT_lo, ps[:, 6, :].rearrange("p (k t) -> p k t", k=KF), actT_hi).then_inc(actT_lo_done, 1)

            dve.wait_ge(table_ready, 6)
            last = dve.value_load(table[0:1, 1:2], min_val=NE - 1, max_val=MAX_TILES - 1)
            turned_rows_rest(0)
            list_out(slice(1, 2))
            los(4, 6)
            los(6, 11)
            dve.wait_ge(quarter_used, splits(N_EXP + 7))
            dve.wait_ge(silu_ready, 1)
            dve.tensor_tensor(act_t, ps[:, 1, :], silu_t, ALU.mult).then_inc(act_ready, 1)
            turned_rows_rest(1)
            list_out(slice(2, 3))
            turned_product_rest(0)
            los(11, 15)
            with dve.Fori(1, last) as j:
                los(3, 7, j)
                product_tile(j, TURN * j + splits(N_EXP + 3))
                los(7, 8, j)
                turned_rows_rest(j + 1)
                list_out(bass.ds(j + 2, 1))
                los(8, 11, j)
                turned_product_rest(j)
                los(11, 15, j)
            los(3, 7, last)
            product_tile(last, TURN * last + splits(N_EXP + 3))
            los(7, 11, last)
            turned_product_rest(last)
            los(11, 12, last)
            dve.wait_ge(quarter_used, TURN * last + splits(N_EXP + 11))
            dve.wait_ge(y_stored, 16 * last + 1)
            dve.tensor_copy(y_t[:, COLS:D], ps[:, 5, :]).then_inc(last_y_half, 1)

            for i in range(NTILE + 2):
                if i < NTILE:
                    n = rows(i)
                    y = yg[i % 4]
                    dve.wait_ge(yg_scaled, i + 1)
                    dve.wait_ge(yg_ready[i % 4][1], 16 * (i // 4 + 1))
                    link(dve.scalar_tensor_tensor(y[0:n, 1, :], y[0:n, 1, :], share[0:n, 1, i:i + 1], y[0:n, 0, :], ALU.mult, ALU.add))
                    g2 = bvec[0:n, G2, :] if i < NP // P else g2_dec[0:ND, :]
                    dve.tensor_tensor(y[0:n, 1, :], y[0:n, 1, :], g2, ALU.mult).then_inc(moe_ready, 1)
                    if i == NTILE - 1:
                        dve.wait_ge(moe_ready, NTILE)
                        dve.tensor_tensor(x1[0:n, i, :], x1[0:n, i, :], y[0:n, 1, :], ALU.add).then_inc(last_x2_ready, 1)
                if 1 <= i <= NTILE:
                    row_means(i - 1, NTILE + i - 1, 2 * NTILE + i, 2 + NTILE + i)
                if i >= 2:
                    t = i - 2
                    r = row_rsqrt(t, NTILE + t, 3 + NTILE + t)
                    dve.scalar_tensor_tensor(x1[0:rows(t), t, :], x1[0:rows(t), t, :], r, bvec[0:rows(t), FG, :], ALU.mult, ALU.mult).then_inc(out_ready, 1)


_INS = ['x_prompt', 'x_sample', 'state_conf', 'state_pool', 'state_sconv', 'c_prompt', 'c_sample', 'w_ada', 'b_ada',
        'norm1_g', 'norm2_g', 'final_g', 'w_in', 'conf_dw', 'conf_dw_b', 'conf_ln_g', 'conf_ln_b', 'conf_pw',
        'pool_w', 'pool_scale', 'sc_dw', 'sc_out', 'w_o', 'router_g', 'router_g_b', 'router_e', 'router_e_b',
        'exp_w1', 'exp_w3', 'exp_w2']
_OUTS = [(1, NP, D), (ND, 1, D), (1, 1, CK - 1, W), (1, ND, CK - 1, W), (1, 1, PB, W), (1, ND, PB, W),
         (1, 1, SK - 1, W), (1, ND, SK - 1, W)]


def kernel(**inputs):
    import concourse.bacc as bacc
    from concourse.bass_utils import run_bass_kernel_spmd

    nc = bacc.Bacc("TRN2", target_bir_lowering=False, num_devices=1)
    arrays, args = {}, []
    for name in _INS:
        a = np.ascontiguousarray(inputs[name])
        arrays[f"in_{name}_dram"] = a
        args.append(nc.dram_tensor(f"in_{name}_dram", a.shape, mybir.dt.from_np(a.dtype), kind="ExternalInput").ap())
    for i, shape in enumerate(_OUTS):
        args.append(nc.dram_tensor(f"out_{i}_dram", shape, F32, kind="ExternalOutput").ap())
    trunk_step(nc, *args)
    r = run_bass_kernel_spmd(nc, [arrays], core_ids=[0])
    return tuple(r.results[0][f"out_{i}_dram"] for i in range(len(_OUTS)))
```
